# Optimizing a Trainium2 kernel written in Bass

```python
import math
import jax, jax.numpy as jnp
from jax import lax
import numpy as np

D_MODEL = 1024
BATCH = 1
SEQ = 256
DEPTH = 2

CTX_LEN = 256
GRID_W = 64
HEAD_DIM = 64
ROPE_THETA = 10000.0
EPS = 1e-6
BLOCK = 128
A_HEADS = 8
A_KV_HEADS = 2
A_GROUPS = A_HEADS // A_KV_HEADS
WINDOW = 128
B_HEADS = 4
B_VDIM = 2 * HEAD_DIM
C_WIDTH = 512
C_BLOCKS = 8
C_BW = C_WIDTH // C_BLOCKS
CONV_W = 4
LRU_C = 8.0
N_BRANCH = 3
BRANCH_W = 512
FFN_HIDDEN = -(-8 * D_MODEL // (3 * 256)) * 256
IN_SIZES = (A_HEADS * HEAD_DIM, A_KV_HEADS * HEAD_DIM, A_KV_HEADS * HEAD_DIM,
            B_HEADS * 2 * HEAD_DIM, B_HEADS * 2 * HEAD_DIM, B_HEADS * B_VDIM,
            C_WIDTH, C_WIDTH, N_BRANCH * D_MODEL)
IN_WIDTH = sum(IN_SIZES)
IN_SPLITS = tuple(int(s) for s in np.cumsum(IN_SIZES)[:-1])

kernel_name = "hybrid_gated_swa_diffattn_rglru_ctxprefix"

def rms_norm(x, g):
    xf = x.astype(jnp.float32)
    y = xf * lax.rsqrt(jnp.mean(xf * xf, axis=-1, keepdims=True) + EPS)
    return (y * g.astype(jnp.float32)).astype(x.dtype)

def modulate(h, shift, scale):
    return h * (1 + scale) + shift

def axial_rope_tables(n_tokens, dtype):
    rows = n_tokens // GRID_W
    row, col = jnp.meshgrid(jnp.arange(rows), jnp.arange(GRID_W), indexing="ij")
    pos = jnp.stack([row.reshape(-1), col.reshape(-1)], axis=-1).astype(jnp.float32)
    rd = HEAD_DIM // 4
    inv = 1.0 / (ROPE_THETA ** (jnp.arange(rd, dtype=jnp.float32) * 2.0 / (HEAD_DIM // 2)))
    ang = pos[:, :, None] * inv
    return jnp.cos(ang).astype(dtype), jnp.sin(ang).astype(dtype)

def apply_rope(x, cos, sin):
    shp = x.shape
    rd = HEAD_DIM // 4
    xs = x.reshape(shp[:-1] + (2, 2, rd))
    bshape = (1, shp[1]) + (1,) * (len(shp) - 3) + (2, rd)
    cb = cos.reshape(bshape)
    sb = sin.reshape(bshape)
    x1 = xs[..., 0, :]
    x2 = xs[..., 1, :]
    out = jnp.stack([x1 * cb - x2 * sb, x2 * cb + x1 * sb], axis=-2)
    return out.reshape(shp)

def window_attention(q, k, v, kc, vc, sink):
    bsz, n_tok = q.shape[:2]
    n_ctx = kc.shape[1]
    nb = n_tok // BLOCK
    span = BLOCK + 2 * WINDOW
    scale = HEAD_DIM ** -0.5
    qb = q.reshape(bsz, nb, BLOCK, A_KV_HEADS, A_GROUPS, HEAD_DIM).transpose(1, 0, 2, 3, 4, 5)
    pad = ((0, 0), (WINDOW, WINDOW), (0, 0), (0, 0))
    kp = jnp.pad(k, pad)
    vp = jnp.pad(v, pad)
    qi = jnp.arange(BLOCK)[:, None]
    kj = jnp.arange(span)[None, :]
    rel = kj - WINDOW - qi
    sink_l = sink.astype(jnp.float32).reshape(A_KV_HEADS, A_GROUPS)[None, :, :, None, None]

    def one_block(args):
        n, qblk = args
        start = n * BLOCK
        kw = lax.dynamic_slice_in_dim(kp, start, span, axis=1)
        vw = lax.dynamic_slice_in_dim(vp, start, span, axis=1)
        kpos = start - WINDOW + kj
        valid = (jnp.abs(rel) <= WINDOW) & (kpos >= 0) & (kpos < n_tok)
        s_loc = jnp.einsum("bqhgd,bkhd->bhgqk", qblk, kw).astype(jnp.float32) * scale
        s_loc = jnp.where(valid, s_loc, -jnp.inf)
        s_ctx = jnp.einsum("bqhgd,bchd->bhgqc", qblk, kc).astype(jnp.float32) * scale
        s_sink = jnp.broadcast_to(sink_l, s_ctx.shape[:-1] + (1,))
        p = jax.nn.softmax(jnp.concatenate([s_loc, s_ctx, s_sink], axis=-1), axis=-1).astype(q.dtype)
        return (jnp.einsum("bhgqk,bkhd->bqhgd", p[..., :span], vw)
                + jnp.einsum("bhgqc,bchd->bqhgd", p[..., span:span + n_ctx], vc))

    out = lax.map(one_block, (jnp.arange(nb), qb))
    return out.transpose(1, 0, 2, 3, 4, 5).reshape(bsz, n_tok, A_HEADS * HEAD_DIM)

def sink_attention_dense(q, k, v, sink):
    bsz, n = q.shape[:2]
    qg = q.reshape(bsz, n, A_KV_HEADS, A_GROUPS, HEAD_DIM)
    s = jnp.einsum("bqhgd,bkhd->bhgqk", qg, k).astype(jnp.float32) * HEAD_DIM ** -0.5
    sink_l = sink.astype(jnp.float32).reshape(A_KV_HEADS, A_GROUPS)[None, :, :, None, None]
    s_sink = jnp.broadcast_to(sink_l, s.shape[:-1] + (1,))
    p = jax.nn.softmax(jnp.concatenate([s, s_sink], axis=-1), axis=-1)[..., :-1].astype(q.dtype)
    return jnp.einsum("bhgqk,bkhd->bqhgd", p, v).reshape(bsz, n, A_HEADS * HEAD_DIM)

def diff_attend(q, k, v, lam):
    s = jnp.einsum("bqhmd,bkhmd->bhmqk", q, k).astype(jnp.float32) * HEAD_DIM ** -0.5
    p = jax.nn.softmax(s, axis=-1)
    w = (p[:, :, 0] - lam * p[:, :, 1]).astype(v.dtype)
    return jnp.einsum("bhqk,bkhe->bqhe", w, v)

def diff_attention_latent(q, k, v, kc, vc, lam):
    bsz, n_tok = q.shape[:2]
    nb = n_tok // BLOCK
    k_all = jnp.concatenate([k, kc], axis=1)
    v_all = jnp.concatenate([v, vc], axis=1)
    qb = q.reshape(bsz, nb, BLOCK, B_HEADS, 2, HEAD_DIM).swapaxes(0, 1)
    out = lax.map(lambda qblk: diff_attend(qblk, k_all, v_all, lam), qb)
    return out.swapaxes(0, 1).reshape(bsz, n_tok, B_HEADS, B_VDIM)

def short_conv(u, w, b):
    left = CONV_W // 2
    y = lax.conv_general_dilated(u, w[:, None, :].astype(u.dtype), window_strides=(1,),
                                 padding=[(left, CONV_W - 1 - left)],
                                 dimension_numbers=("NWC", "WIO", "NWC"),
                                 feature_group_count=C_WIDTH)
    return y + b

def lru_coeffs(u, w_gate, b_gate, lam):
    bsz, n = u.shape[:2]
    ub = u.reshape(bsz, n, C_BLOCKS, C_BW)
    g = jnp.einsum("blnc,dgncf->dgblnf", ub, w_gate).reshape(2, 2, bsz, n, C_WIDTH)
    g = jax.nn.sigmoid((g + b_gate[:, :, None, None, :]).astype(jnp.float32))
    r, i = g[:, 0], g[:, 1]
    log_a = -LRU_C * jax.nn.softplus(-lam.astype(jnp.float32))[:, None, None, :] * r
    a = jnp.exp(log_a)
    bx = jnp.sqrt(-jnp.expm1(2.0 * log_a)) * i * u.astype(jnp.float32)
    return a, bx

def linear_scan(a, b, h0):
    b = b.at[:, 0].add(a[:, 0] * h0)

    def combine(e1, e2):
        a1, b1 = e1
        a2, b2 = e2
        return a1 * a2, a2 * b1 + b2

    _, h = lax.associative_scan(combine, (a, b), axis=1)
    return h

def bidir_lru(a, bx, h0_fwd, h0_bwd):
    h_f = linear_scan(a[0], bx[0], h0_fwd)
    h_b = jnp.flip(linear_scan(jnp.flip(a[1], 1), jnp.flip(bx[1], 1), h0_bwd), 1)
    return h_f, h_b

def gated_merge(ys, gates, w_branch, w_out):
    g = jax.nn.sigmoid(gates.reshape(gates.shape[:-1] + (N_BRANCH, D_MODEL)))
    return jnp.sum(g * jnp.einsum("blnw,nwd->blnd", ys, w_branch), axis=2) @ w_out

def swiglu(h, w_in, w_out):
    gate, up = jnp.split(h @ w_in, 2, axis=-1)
    return (jax.nn.silu(gate) * up) @ w_out

def trunk_layer(l, x, ctx, c, c_ctx, cos, sin, w_mod, b_mod, norm_g, w_in, attn_sink,
                diff_lambda, diff_subln, conv_w, conv_b, lru_w, lru_b, lru_lambda,
                w_branch, w_out, w_ffn_in, w_ffn_out, need_ctx):
    bsz, n_tok = x.shape[:2]
    n_ctx = ctx.shape[1]
    mx = (jax.nn.silu(c) @ w_mod + b_mod)[:, None, :]
    mc = (jax.nn.silu(c_ctx) @ w_mod + b_mod)[None, None, :]
    shx1, scx1, gx1, shx2, scx2, gx2 = jnp.split(mx, 6, axis=-1)
    shc1, scc1, gc1, shc2, scc2, gc2 = jnp.split(mc, 6, axis=-1)

    px = modulate(rms_norm(x, norm_g[0]), shx1, scx1) @ w_in
    pc = modulate(rms_norm(ctx, norm_g[0]), shc1, scc1) @ w_in
    aq, ak, av, bq, bk, bv, cu, cg, gt = jnp.split(px, IN_SPLITS, axis=-1)
    aq_c, ak_c, av_c, bq_c, bk_c, bv_c, cu_c, cg_c, gt_c = jnp.split(pc, IN_SPLITS, axis=-1)

    qA = apply_rope(aq.reshape(bsz, n_tok, A_HEADS, HEAD_DIM), cos, sin)
    kA = apply_rope(ak.reshape(bsz, n_tok, A_KV_HEADS, HEAD_DIM), cos, sin)
    vA = av.reshape(bsz, n_tok, A_KV_HEADS, HEAD_DIM)
    kA_c = ak_c.reshape(bsz, n_ctx, A_KV_HEADS, HEAD_DIM)
    vA_c = av_c.reshape(bsz, n_ctx, A_KV_HEADS, HEAD_DIM)
    yA = window_attention(qA, kA, vA, kA_c, vA_c, attn_sink)

    lam_init = 0.8 - 0.6 * math.exp(-0.3 * l)
    dl = diff_lambda.astype(jnp.float32)
    lam = jnp.exp(jnp.sum(dl[0] * dl[1])) - jnp.exp(jnp.sum(dl[2] * dl[3])) + lam_init
    qB = apply_rope(bq.reshape(bsz, n_tok, B_HEADS, 2, HEAD_DIM), cos, sin)
    kB = apply_rope(bk.reshape(bsz, n_tok, B_HEADS, 2, HEAD_DIM), cos, sin)
    vB = bv.reshape(bsz, n_tok, B_HEADS, B_VDIM)
    kB_c = bk_c.reshape(bsz, n_ctx, B_HEADS, 2, HEAD_DIM)
    vB_c = bv_c.reshape(bsz, n_ctx, B_HEADS, B_VDIM)
    yB = diff_attention_latent(qB, kB, vB, kB_c, vB_c, lam)
    yB = (rms_norm(yB, diff_subln) * (1.0 - lam_init)).reshape(bsz, n_tok, BRANCH_W)

    u_c = short_conv(cu_c, conv_w, conv_b)
    a_c, b_c = lru_coeffs(u_c, lru_w, lru_b, lru_lambda)
    h0 = jnp.zeros((bsz, C_WIDTH), jnp.float32)
    hf_c, hb_c = bidir_lru(a_c, b_c, h0, h0)
    u_l = short_conv(cu, conv_w, conv_b)
    a_l, b_l = lru_coeffs(u_l, lru_w, lru_b, lru_lambda)
    hf_l, hb_l = bidir_lru(a_l, b_l, hf_c[:, -1], hb_c[:, 0])
    yC = ((hf_l + hb_l) * jax.nn.gelu(cg.astype(jnp.float32))).astype(x.dtype)

    mix = gated_merge(jnp.stack([yA, yB, yC], axis=2), gt, w_branch, w_out)
    x = x + gx1 * rms_norm(mix, norm_g[1])
    f = swiglu(modulate(rms_norm(x, norm_g[2]), shx2, scx2), w_ffn_in, w_ffn_out)
    x = x + gx2 * rms_norm(f, norm_g[3])
    if not need_ctx:
        return x, None

    yA_c = sink_attention_dense(aq_c.reshape(bsz, n_ctx, A_HEADS, HEAD_DIM), kA_c, vA_c, attn_sink)
    yB_c = diff_attend(bq_c.reshape(bsz, n_ctx, B_HEADS, 2, HEAD_DIM), kB_c, vB_c, lam)
    yB_c = (rms_norm(yB_c, diff_subln) * (1.0 - lam_init)).reshape(bsz, n_ctx, BRANCH_W)
    yC_c = ((hf_c + hb_c) * jax.nn.gelu(cg_c.astype(jnp.float32))).astype(ctx.dtype)
    mix_c = gated_merge(jnp.stack([yA_c, yB_c, yC_c], axis=2), gt_c, w_branch, w_out)
    ctx = ctx + gc1 * rms_norm(mix_c, norm_g[1])
    f_c = swiglu(modulate(rms_norm(ctx, norm_g[2]), shc2, scc2), w_ffn_in, w_ffn_out)
    ctx = ctx + gc2 * rms_norm(f_c, norm_g[3])
    return x, ctx

def setup_inputs(seed: int = 0) -> dict:
    key = jax.random.key(seed)
    ks = jax.random.split(key, 24)
    f32 = jnp.float32

    def nrm(k, shape, scale):
        return jax.random.normal(k, shape, f32) * scale

    u = jax.random.uniform(ks[20], (DEPTH, 2, C_WIDTH), f32, minval=0.9, maxval=0.999)
    a0 = u ** (1.0 / LRU_C)
    lru_lambda = jnp.log(a0) - jnp.log1p(-a0)
    return {
        "x": nrm(ks[0], (BATCH, SEQ, D_MODEL), 1.0),
        "c": nrm(ks[1], (BATCH, D_MODEL), 1.0),
        "ctx": nrm(ks[2], (BATCH, CTX_LEN, D_MODEL), 1.0),
        "c_ctx": nrm(ks[3], (D_MODEL,), 1.0),
        "w_mod": nrm(ks[4], (DEPTH, D_MODEL, 6 * D_MODEL), 0.5 * D_MODEL ** -0.5),
        "b_mod": nrm(ks[5], (DEPTH, 6 * D_MODEL), 0.02),
        "norm_g": 1.0 + nrm(ks[6], (DEPTH, 4, D_MODEL), 0.02),
        "w_in": nrm(ks[7], (DEPTH, D_MODEL, IN_WIDTH), D_MODEL ** -0.5),
        "attn_sink": nrm(ks[8], (DEPTH, A_HEADS), 0.5),
        "diff_lambda": nrm(ks[9], (DEPTH, 4, HEAD_DIM), 0.1),
        "diff_subln": 1.0 + nrm(ks[10], (DEPTH, B_VDIM), 0.02),
        "conv_w": nrm(ks[11], (DEPTH, CONV_W, C_WIDTH), CONV_W ** -0.5),
        "conv_b": nrm(ks[12], (DEPTH, C_WIDTH), 0.02),
        "lru_w": nrm(ks[13], (DEPTH, 2, 2, C_BLOCKS, C_BW, C_BW), C_BW ** -0.5),
        "lru_b": nrm(ks[14], (DEPTH, 2, 2, C_WIDTH), 0.02),
        "lru_lambda": lru_lambda,
        "w_branch": nrm(ks[15], (DEPTH, N_BRANCH, BRANCH_W, D_MODEL), BRANCH_W ** -0.5),
        "w_out": nrm(ks[16], (DEPTH, D_MODEL, D_MODEL), D_MODEL ** -0.5),
        "w_ffn_in": nrm(ks[17], (DEPTH, D_MODEL, 2 * FFN_HIDDEN), D_MODEL ** -0.5),
        "w_ffn_out": nrm(ks[18], (DEPTH, FFN_HIDDEN, D_MODEL), FFN_HIDDEN ** -0.5),
    }

def reference(x, c, ctx, c_ctx, w_mod, b_mod, norm_g, w_in, attn_sink, diff_lambda, diff_subln,
              conv_w, conv_b, lru_w, lru_b, lru_lambda, w_branch, w_out, w_ffn_in, w_ffn_out):
    cos, sin = axial_rope_tables(x.shape[1], x.dtype)
    for l in range(DEPTH):
        x, ctx = trunk_layer(l, x, ctx, c, c_ctx, cos, sin, w_mod[l], b_mod[l], norm_g[l], w_in[l],
                             attn_sink[l], diff_lambda[l], diff_subln[l], conv_w[l], conv_b[l],
                             lru_w[l], lru_b[l], lru_lambda[l], w_branch[l], w_out[l],
                             w_ffn_in[l], w_ffn_out[l], need_ctx=(l < DEPTH - 1))
    return x


_drawn_inputs = setup_inputs


def setup_inputs(seed=0):
    import zlib

    import numpy as np

    out = dict(_drawn_inputs(seed))
    spreads = {}
    factors = {'norm_g': 2.934, 'attn_sink': 64.0, 'diff_lambda': 8.0, 'diff_subln': 28.192, 'lru_b': 8.0}
    for name, (base, spread) in spreads.items():
        noise = np.random.default_rng([zlib.crc32(name.encode()), seed]).standard_normal(out[name].shape)
        drawn = base * np.exp(spread * noise) if base else spread * noise
        out[name] = __import__('jax').numpy.asarray(drawn.astype(out[name].dtype))
    for name, factor in factors.items():
        out[name] = (out[name] * factor).astype(out[name].dtype)
    return out
```

```python
import math
from contextlib import ExitStack

import numpy as np
import concourse.bass as bass
from concourse import mybir

P = 128
F32, F32R, BF16 = mybir.dt.float32, mybir.dt.float32r, mybir.dt.bfloat16
ACT = mybir.ActivationFunctionType
ALU = mybir.AluOpType
AX = mybir.AxisListType.X

DEPTH, D, SEQ, CTX = 2, 1024, 256, 256
T = CTX + SEQ
KD = D // P
HEAD = 64
A_HEADS, A_KV, B_HEADS, B_VDIM = 8, 2, 4, 128
C_W, CONV_W, C_BLOCKS = 512, 4, 8
KC = C_W // P
N_BRANCH = 3
FFN = 2816
KF = FFN // P
EPS = 1e-6
SCALE = HEAD ** -0.5
GRID_W, WINDOW = 64, 128
MASKED = -1e30

IN_TILE = {"aq": 0, "ak": 4, "av": 5, "bq": 6, "bk": 10, "bv": 14, "cu": 18, "cg": 22, "gt": 26}
PROJ = ([("cu", t) for t in range(4)] + [("ak", 0), ("av", 0), ("aq", 0), ("lru", 0), ("aq", 1), ("bk", 0),
        ("lru", 1), ("aq", 2), ("bk", 1), ("lru", 2), ("aq", 3), ("bk", 2), ("lru", 3), ("bk", 3)]
        + [("bv", h) for h in range(4)] + [("bq", h) for h in range(4)] + [("cg", t) for t in range(4)])
N_MOD = 6 * KD
ACC = 4
RAW = 4
SPLIT = 3

V_BMOD, V_G, V_CW, V_CB, V_LB, V_LAM, V_SINK, V_DL, V_SUB = 0, 96, 160, 176, 180, 196, 204, 212, 468
V_N = 469


def block_order():
    order = [("w_in", k, IN_TILE[kind] + t) for kind, t in PROJ if kind != "lru" for k in range(KD)]
    for m in range(KD):
        for n in range(N_BRANCH):
            order += [("w_in", k, IN_TILE["gt"] + n * KD + m) for k in range(KD)]
            order += [("w_branch", n * KC + k, m) for k in range(KC)]
    order += [("w_out", k, m) for m in range(KD) for k in range(KD)]
    order += [("w_ffn_in", k, j + half * KF) for j in range(KF) for half in range(2) for k in range(KD)]
    order += [("w_ffn_out", k, m) for m in range(KD) for k in range(KF)]
    return order


N_GRAN = len(block_order()) // 8


class Done:

    def __init__(self, sem, known):
        self.sem, self.known, self.marks, self.count = sem, known, {}, 0

    def mark(self, *keys):
        self.count += 1
        for key in keys:
            self.marks[key] = self.count
        return 1

    def after(self, *key):
        return self.known[key] if self.known else 1


def program(nc, io, known):
    with ExitStack() as ctx:
        def sem(name):
            return ctx.enter_context(nc.semaphore(name))

        def sb(name, shape, dt=F32):
            return ctx.enter_context(nc.sbuf_tensor(name, shape, dt))

        xT = sb("xT", [P, KD, T])
        h_base = -(-nc.sbuf_base // 32) * 32
        h_hi = sb("h_hi", [P, KD, T], F32R)
        h_lo = sb("h_lo", [P, KD, T], F32R)
        raw = sb("raw", [P, RAW, 8 * P])
        w_hi = sb("w_hi", [P, SPLIT, 8, P], F32R)
        w_lo = sb("w_lo", [P, SPLIT, 8, P], F32R)
        lruw = sb("lruw", [P, 16, P])
        vec = sb("vec", [P, DEPTH, V_N])
        cos, sin = sb("cos", [P, SEQ]), sb("sin", [P, SEQ])
        ident, identb = sb("ident", [P, P]), sb("identb", [P, P], BF16)
        ones = sb("ones", [P, P])
        mask = sb("mask", [P, 2, SEQ], BF16)
        cT, cs = sb("cT", [P, KD, 2]), sb("cs", [P, KD, 2])
        modv = sb("modv", [P, N_MOD, 2])
        gain = sb("gain", [P, 4, KD, 2])
        small = sb("small", [P, 64])
        kdec = sb("kdec", [P, 3, 8])
        hb = sb("hb", [P, 16])
        nlam, gsub = sb("nlam", [P, 4]), sb("gsub", [P, 1])
        nsink = sb("nsink", [P, 8])
        sm = sb("sm", [P, 8, 8])
        bss, bst = sb("bss", [P, 4, 4]), sb("bst", [P, 2, 16])
        rt = sb("rt", [P, 2, 4])

        base = -(-nc.sbuf_base // 32) * 32
        sb("arena", [P, 95 * 256])

        def at(name, kib, shape, dt=F32):
            return nc.alloc_sbuf_tensor_at(name, shape, dt, offset=base + int(kib * 1024))

        q_a, q_b = at("q_a", 0, [P, 4, T]), at("q_b", 8, [P, 4, T])
        k_a, k_b = at("k_a", 16, [P, 1, T]), at("k_b", 20, [P, 4, T])
        k_sw = at("k_sw", 18, [P, 1, T])
        vv = at("vv", 28, [P, 4, 5 * P])
        y_c = at("y_c", 38, [P, 4, T])
        cu = at("cu", 46, [P, 4, 2, CTX + 4])
        uu = at("uu", 54.25, [P, 4, T])
        l_r, l_i = at("l_r", 62.25, [P, 2, T]), at("l_i", 66.25, [P, 2, T])
        l_a, l_q = at("l_a", 70.25, [P, 2, T]), at("l_q", 74.25, [P, 2, T])
        yrow = at("yrow", 62.25, [P, 4, C_W])
        yrow_a = at("yrow_a", 70.25, [P, 2, C_W])
        pt = at("pt", 74.25, [P, 2, 4, P])
        pp = at("pp", 78.25, [P, 4, T])
        ww = at("ww", 86.25, [P, 2, T])
        rope = at("rope", 90.25, [P, 2, SEQ])
        gel = at("gel", 92.25, [P, T])
        yh, yl = at("yh", 46, [P, 12, T], F32R), at("yl", 70, [P, 12, T], F32R)
        mx_hi, mx_lo = at("mx_hi", 0, [P, KD, T], F32R), at("mx_lo", 16, [P, KD, T], F32R)
        tg, mixt, mixu = at("tg", 38, [P, 2, T]), at("mixt", 42, [P, T]), at("mixu", 44, [P, T])
        f_hi, f_lo = at("f_hi", 0, [P, KF, T], F32R), at("f_lo", 44, [P, KF, T], F32R)
        sg, hid = at("sg", 88, [P, 2, T]), at("hid", 92, [P, T])
        sq = at("sq", 88, [P, 2, T])
        ht = at("ht", 76, [P, 2, T])
        rstd, diag = at("rstd", 80, [P, T]), at("diag", 82, [P, 4, P])
        maskf = at("maskf", 0, [P, 2, SEQ])
        fout = nc.alloc_sbuf_tensor_at("fout", [P, KD, T], F32, offset=h_base)

        acc = ctx.enter_context(nc.psum_tensor("acc", [P, ACC, 512], F32))
        sc = ctx.enter_context(nc.psum_tensor("sc", [P, 3, 512], F32))
        oo = ctx.enter_context(nc.psum_tensor("oo", [P, 512], F32))

        pe_done, act_done, dve_done, pool_done = (
            Done(sem(n), known[n]) for n in ("pe_done", "act_done", "dve_done", "pool_done"))
        raw_loaded = [sem(f"raw_loaded{i}") for i in range(RAW)]
        consts_loaded, x_loaded, lru_loaded, stored = (
            sem("consts_loaded"), sem("x_loaded"), sem("lru_loaded"), sem("stored"))

        def c0(l):
            return 0 if l == 0 else CTX

        def streams(l):
            return [(0, 0), (1, CTX)] if l == 0 else [(1, CTX)]

        def qtiles(l):
            return [0, 1, 2, 3] if l == 0 else [2, 3]

        plan = []
        for l in range(DEPTH):
            plan += [("mod", l)]
            plan += [("square", l, 0, k) for k in range(KD)] + [("norm", l, 0), ("modulate", l, 0)]
            for kind, t in PROJ:
                plan += [("lru", l, t)] if kind == "lru" else [("proj", l, kind, t)]
            plan += [("attend_b", l), ("attend_a", l), ("ysplit", l)]
            plan += [("merge", l, m) for m in range(KD)]
            for m in range(KD):
                plan += [("wout", l, m)] + ([("square", l, 1, m - 1)] if m else [])
            plan += [("square", l, 1, KD - 1), ("norm", l, 1), ("residual", l, 1)]
            plan += [("square", l, 2, k) for k in range(KD)] + [("norm", l, 2), ("modulate", l, 2)]
            plan += [("ffn_in", l, j) for j in range(KF)]
            for m in range(KD):
                plan += [("ffn_out", l, m)] + ([("square", l, 3, m - 1)] if m else [])
            plan += [("square", l, 3, KD - 1), ("norm", l, 3), ("residual", l, 3)]

        items = []
        for step in plan:
            s, l, a = step[0], step[1], step[2:]
            if s == "proj":
                items.append((("proj", l) + a, 8, "A"))
            elif s == "lru":
                items += [(("gate", l, a[0], d, g), 0, "A") for d in range(2) for g in range(2)]
            elif s == "norm":
                items.append((("spread", l, a[0]), 0, "A"))
            elif s == "attend_b":
                units = [(t, h) for t in qtiles(l) for h in range(B_HEADS)]
                for i, (t, h) in enumerate(units):
                    items.append((("pt_b", l, t, h), 0, "A"))
                    if i:
                        items.append((("pv_b", l, i - 1), 0, "A"))
                items.append((("pv_b", l, len(units) - 1), 0, "A"))
            elif s == "attend_a":
                items += [(("yt_b", l, t), 0, "A") for t in qtiles(l)]
                for j, t in enumerate(qtiles(l)):
                    for h in range(A_HEADS):
                        items.append((("pt_a", l, t, h), 0, "A"))
                        if h:
                            items.append((("pv_a", l, j * A_HEADS + h - 1), 0, "D"))
                    items += [(("pv_a", l, j * A_HEADS + A_HEADS - 1), 0, "D"), (("yt_a", l, t), 0, "A")]
            elif s == "merge":
                for n in range(N_BRANCH):
                    items += [(("mgate", l, a[0], n), 8, "A"), (("mbranch", l, a[0], n), KC, "D")]
            elif s in ("wout", "ffn_out"):
                items.append(((s, l, a[0]), KD if s == "wout" else KF, "A"))
            elif s == "ffn_in":
                items += [(("fgate", l, a[0]), 8, "A"), (("fup", l, a[0]), 8, "D")]
        order = [key for key, n, by in items]
        info = {key: (n, by) for key, n, by in items}
        slot_of = {key: i for i, key in enumerate(order)}
        blocks_end, total = {}, 0
        for key in order:
            total += info[key][0]
            blocks_end[key] = total
        assert total == DEPTH * N_GRAN * 8

        def bank(key):
            return acc[:, slot_of[key] % ACC, :]

        def is_mod(g):
            return g % (N_MOD + N_GRAN) < N_MOD

        def gran_of(q):
            return q // N_GRAN * (N_MOD + N_GRAN) + N_MOD + q % N_GRAN

        def wait_raw(eng, g):
            eng.wait_ge(raw_loaded[g % RAW], 16 * (g // RAW + 1))

        block = ctx.enter_context(nc.Block())

        @block.sync
        def _(sp):
            for name, t in (("cT", cT), ("vec", vec), ("ident", ident), ("cos", cos), ("sin", sin), ("maskf", maskf)):
                sp.dma_start(t[:], io[name]).then_inc(consts_loaded, 16)
            sp.dma_start(xT[:], io["xT"]).then_inc(x_loaded, 16)
            q = 0
            for g in range(DEPTH * (N_MOD + N_GRAN)):
                l = g // (N_MOD + N_GRAN)
                if g % (N_MOD + N_GRAN) == 0:
                    if l:
                        sp.wait_ge(pe_done.sem, pe_done.after("gate", l - 1, KC - 1, 1, 1))
                    sp.dma_start(lruw[:], io["lruw"][l]).then_inc(lru_loaded, 16)
                if g >= RAW:
                    old = g - RAW
                    if is_mod(old):
                        sp.wait_ge(pe_done.sem, pe_done.after("mod", old // (N_MOD + N_GRAN), old % (N_MOD + N_GRAN)))
                    else:
                        sp.wait_ge(dve_done.sem, dve_done.after("w_lo", q))
                        q += 1
                sp.dma_start(raw[:, g % RAW, :], io["stream"][g]).then_inc(raw_loaded[g % RAW], 16)
            for k in range(KD):
                sp.wait_ge(dve_done.sem, dve_done.after("x", DEPTH - 1, 3, k))
                sp.dma_start(io["out"][:, k, :], xT[:, k, CTX:T]).then_inc(stored, 16)
            sp.wait_ge(stored, 16 * KD)

        @block.gpsimd
        def _(pool):
            pool.memset(ones[:], 1.0).then_inc(pool_done.sem, pool_done.mark(("ones",)))
            for q in range(DEPTH * N_GRAN):
                g = gran_of(q)
                wait_raw(pool, g)
                if q >= SPLIT:
                    pool.wait_ge(pe_done.sem, pe_done.after("used", q - SPLIT))
                pool.tensor_scalar(w_hi[:, q % SPLIT].rearrange("p k n -> p (k n)"), raw[:, g % RAW, :], 1.0, 0.0,
                                   ALU.mult, ALU.add).then_inc(pool_done.sem, pool_done.mark(("w_hi", q)))

        @block.tensor
        def _(pe):
            blocks = [0]

            def take(key):
                n = slot_of[key]
                if n >= ACC:
                    last = order[n - ACC]
                    if info[last][1] == "A":
                        pe.wait_ge(act_done.sem, act_done.after("read", last))
                    else:
                        pe.wait_ge(dve_done.sem, dve_done.after("read", last))
                return bank(key)

            def next_block():
                q, k = divmod(blocks[0], 8)
                blocks[0] += 1
                if k == 0:
                    pe.wait_ge(dve_done.sem, dve_done.after("w_lo", q))
                return q, k

            def gemm(key, src_hi, src_lo, cols):
                out = take(key)
                n = info[key][0]
                for i in range(n):
                    q, k = next_block()
                    wh, wl = w_hi[:, q % SPLIT, k, :], w_lo[:, q % SPLIT, k, :]
                    o = out[:, cols]
                    pe.matmul(o, wh, src_hi[:, i, cols], start=i == 0, stop=False)
                    pe.matmul(o, wh, src_lo[:, i, cols], start=False, stop=False)
                    last = pe.matmul(o, wl, src_hi[:, i, cols], start=False, stop=i == n - 1)
                    names = ([("used", q)] if k == 7 else []) + ([key] if i == n - 1 else [])
                    if names:
                        last.then_inc(pe_done.sem, pe_done.mark(*names))

            def gemm_tokens(key):
                out = take(key).rearrange("p (t n) -> p t n", n=P)
                q, _ = next_block()
                blocks[0] += 7
                for t in range(T // P):
                    tok = slice(t * P, (t + 1) * P)
                    for k in range(KD):
                        wh, wl = w_hi[:, q % SPLIT, k, :], w_lo[:, q % SPLIT, k, :]
                        pe.matmul(out[:, t], h_hi[:, k, tok], wh, start=k == 0, stop=False)
                        pe.matmul(out[:, t], h_lo[:, k, tok], wh, start=False, stop=False)
                        last = pe.matmul(out[:, t], h_hi[:, k, tok], wl, start=False, stop=k == KD - 1)
                last.then_inc(pe_done.sem, pe_done.mark(("used", q), key))

            def mod(l):
                pe.wait_ge(act_done.sem, act_done.after("silu_c",))
                if l:
                    pe.wait_ge(act_done.sem, act_done.after("read", ("stat", l - 1, 3)))
                for j in range(N_MOD):
                    g = l * (N_MOD + N_GRAN) + j
                    wait_raw(pe, g)
                    for k in range(KD):
                        last = pe.matmul(oo[:, 2 * j:2 * j + 2], raw[:, g % RAW, k * P:(k + 1) * P], cs[:, k, :],
                                         start=k == 0, stop=k == KD - 1)
                    last.then_inc(pe_done.sem, pe_done.mark(("mod", l, j)))

            def square(l, which, k):
                if k == 0:
                    pe.wait_ge(dve_done.sem, dve_done.after("modv", l))
                pe.wait_ge(pool_done.sem, pool_done.after("ones",))
                pe.wait_ge(act_done.sem, act_done.after("square", l, which, k))
                tiles = range(4) if which == 0 else qtiles(l)
                for t in tiles:
                    last = pe.matmul(oo[:, t:t + 1], sq[:, k % 2, t * P:(t + 1) * P], ones[:, 0:1],
                                     start=k == 0 and t == tiles[0], stop=k == KD - 1, skip_group_check=True)
                last.then_inc(pe_done.sem, pe_done.mark(("squared", l, which, k)))

            def norm(l, which):
                key = ("spread", l, which)
                out = take(key)
                for t in range(4) if which == 0 else qtiles(l):
                    pe.wait_ge(dve_done.sem, dve_done.after("diag", l, which, t))
                    last = pe.matmul(out[:, t * P:(t + 1) * P], ones[:], diag[:, t, :], start=True, stop=True)
                last.then_inc(pe_done.sem, pe_done.mark(key))

            def modulate(l, which):
                for k in range(KD):
                    pe.wait_ge(dve_done.sem, dve_done.after("h_lo", l, which, k))

            def proj(l, kind, t):
                if kind in ("av", "bv"):
                    gemm_tokens(("proj", l, kind, t))
                else:
                    whole = kind in ("cu", "ak", "bk")
                    gemm(("proj", l, kind, t), h_hi, h_lo, slice(0 if whole else c0(l), T))

            def lru(l, t):
                pe.wait_ge(lru_loaded, 16 * (l + 1))
                pe.wait_ge(dve_done.sem, dve_done.after("conv", l, t))
                for d in range(2):
                    for g in range(2):
                        key = ("gate", l, t, d, g)
                        pe.matmul(take(key), lruw[:, (d * 2 + g) * KC + t, :], uu[:, t, :], start=True, stop=True)\
                            .then_inc(pe_done.sem, pe_done.mark(key))

            def keys_of(t):
                return T if t >= 2 else CTX

            def scores(key, n, q, kk, t, local):
                if n >= 3:
                    pe.wait_ge(act_done.sem, act_done.after("exp", key[1], n - 3))
                qt = q[:, t * P:(t + 1) * P]
                if local and t >= 2:
                    pe.matmul(sc[:, n % 3, 0:CTX], qt, kk[:, 0:CTX], start=True, stop=True)
                    pe.matmul(sc[:, n % 3, CTX:T], qt, kk[:, CTX:T], start=True, stop=False)
                    last = pe.matmul(sc[:, n % 3, CTX:T], identb[:], mask[:, t - 2, :], start=False, stop=True)
                else:
                    last = pe.matmul(sc[:, n % 3, 0:keys_of(t)], qt, kk[:, 0:keys_of(t)], start=True, stop=True)
                last.then_inc(pe_done.sem, pe_done.mark(key))

            def turn_keys(key, src, t):
                out = take(key)
                nk = keys_of(t) // P
                for j in range(nk):
                    last = pe.transpose(out[:, j * P:(j + 1) * P], src[:, j * P:(j + 1) * P], ident[:])
                last.then_inc(pe_done.sem, pe_done.mark(key))

            def weigh(key, slot, v, t):
                o = take(key)[:, 0:v.stop - v.start]
                nk = keys_of(t) // P
                for j in range(nk):
                    last = pe.matmul(o, pt[:, slot, j, :], vv[:, j, v], start=j == 0, stop=j == nk - 1)
                last.then_inc(pe_done.sem, pe_done.mark(key))

            def attend_b(l):
                units = [(t, h) for t in qtiles(l) for h in range(B_HEADS)]
                for h in range(B_HEADS):
                    for kind in ("bq", "bk"):
                        pe.wait_ge(dve_done.sem, dve_done.after("qk", l, kind, h))
                    pe.wait_ge(act_done.sem, act_done.after("v", l, "bv", h))

                def score(i):
                    t, h = units[i]
                    for m in range(2):
                        half = slice(HEAD * m, HEAD * (m + 1))
                        scores(("s_b", l, 2 * i + m), 2 * i + m, q_b[half, h, :], k_b[half, h, :], t, False)

                def turn(i):
                    t, h = units[i]
                    pe.wait_ge(dve_done.sem, dve_done.after("w_b", l, i))
                    turn_keys(("pt_b", l, t, h), ww[:, i % 2, :], t)

                def value(i):
                    t, h = units[i]
                    pe.wait_ge(act_done.sem, act_done.after("read", ("pt_b", l, t, h)))
                    weigh(("pv_b", l, i), i % 2, slice(P * (h + 1), P * (h + 2)), t)

                score(0)
                for i in range(len(units)):
                    if i + 1 < len(units):
                        score(i + 1)
                    turn(i)
                    if i:
                        value(i - 1)
                value(len(units) - 1)

            def attend_a(l):
                units = [(t, h) for t in qtiles(l) for h in range(A_HEADS)]
                nb = 2 * len(qtiles(l)) * B_HEADS
                for t in range(4):
                    pe.wait_ge(dve_done.sem, dve_done.after("qk", l, "aq", t))
                pe.wait_ge(act_done.sem, act_done.after("k_sw", l))
                pe.wait_ge(act_done.sem, act_done.after("v", l, "av", 0))

                def score(i):
                    t, h = units[i]
                    half = slice(HEAD * (h % 2), HEAD * (h % 2 + 1))
                    kk = k_a if h // 4 == h % 2 else k_sw
                    scores(("s_a", l, i), nb + i, q_a[half, h // 2, :], kk[half, 0, :], t, True)

                def turn(i):
                    t, h = units[i]
                    pe.wait_ge(act_done.sem, act_done.after("exp", l, nb + i))
                    turn_keys(("pt_a", l, t, h), pp[:, i % 4, :], t)

                def value(i):
                    t, h = units[i]
                    pe.wait_ge(act_done.sem, act_done.after("read", ("pt_a", l, t, h)))
                    weigh(("pv_a", l, i), i % 2, slice(HEAD * (h // 4), HEAD * (h // 4 + 1)), t)

                def turn_rows(key, src):
                    out = take(key)
                    for j in range(4):
                        last = pe.transpose(out[:, j * P:(j + 1) * P], src[:, j * P:(j + 1) * P], ident[:])
                    last.then_inc(pe_done.sem, pe_done.mark(key))

                score(0)
                for j, t in enumerate(qtiles(l)):
                    pe.wait_ge(dve_done.sem, dve_done.after("yrow_b", l, t))
                    turn_rows(("yt_b", l, t), yrow[:, j, :])
                for i, (t, h) in enumerate(units):
                    if i + 1 < len(units):
                        score(i + 1)
                    turn(i)
                    if h:
                        value(i - 1)
                    if h == A_HEADS - 1:
                        value(i)
                        pe.wait_ge(dve_done.sem, dve_done.after("o_a", l, t, h))
                        turn_rows(("yt_a", l, t), yrow_a[:, t % 2, :])

            def ysplit(l):
                pass

            def merge(l, m):
                cols = slice(c0(l), T)
                for n in range(N_BRANCH):
                    gemm(("mgate", l, m, n), h_hi, h_lo, cols)
                    if m == 0:
                        for k in range(KC):
                            pe.wait_ge(dve_done.sem, dve_done.after("y_lo", l, n * KC + k))
                    gemm(("mbranch", l, m, n), yh[:, n * KC:(n + 1) * KC], yl[:, n * KC:(n + 1) * KC], cols)

            def wout(l, m):
                if m == 0:
                    pe.wait_ge(dve_done.sem, dve_done.after("mx_lo", l, KD - 1))
                gemm(("wout", l, m), mx_hi, mx_lo, slice(c0(l), T))

            def ffn_in(l, j):
                gemm(("fgate", l, j), h_hi, h_lo, slice(c0(l), T))
                gemm(("fup", l, j), h_hi, h_lo, slice(c0(l), T))

            def ffn_out(l, m):
                if m == 0:
                    pe.wait_ge(dve_done.sem, dve_done.after("f_lo", l, KF - 1))
                gemm(("ffn_out", l, m), f_hi, f_lo, slice(c0(l), T))

            def residual(l, which):
                pass

            pe.wait_ge(consts_loaded, 16 * 6)
            pe.wait_ge(dve_done.sem, dve_done.after("mask",))
            steps = dict(mod=mod, square=square, norm=norm, modulate=modulate, proj=proj, lru=lru, attend_b=attend_b,
                         attend_a=attend_a, ysplit=ysplit, merge=merge, wout=wout, ffn_in=ffn_in, ffn_out=ffn_out,
                         residual=residual)
            for step, *args in plan:
                steps[step](*args)

        @block.scalar
        def _(act):
            def finish(ins, *names):
                ins.then_inc(act_done.sem, act_done.mark(*names))

            def own():
                act.wait_ge(act_done.sem, act_done.count)

            def mod(l):
                act.wait_ge(dve_done.sem, dve_done.after("dots", l))
                finish(act.activation(nlam[:, 0:2], small[:, 16:18], ACT.Exp), ("exp_dots", l))
                finish(act.activation(small[:, 0:8], vec[:, l, V_LAM:V_LAM + 8], ACT.Abs))
                own()
                finish(act.activation(small[:, 8:16], small[:, 0:8], ACT.Exp, scale=-1.0), ("exp_lam", l))

            def square(l, which, k):
                cols = slice(0 if which == 0 else c0(l), T)
                n = k if k >= 2 else None
                if n is not None:
                    act.wait_ge(pe_done.sem, pe_done.after("squared", l, which, k - 2))
                if which in (0, 2):
                    if which == 0 and l == 0:
                        act.wait_ge(x_loaded, 16)
                    else:
                        act.wait_ge(dve_done.sem, dve_done.after("x", l if which else l - 1, 1 if which else 3, k))
                    src = xT[:, k, cols]
                else:
                    act.wait_ge(act_done.sem, act_done.after("read", ({1: "wout", 3: "ffn_out"}[which], l, k)))
                    src = fout[:, k, cols]
                finish(act.activation(sq[:, k % 2, cols], src, ACT.Square), ("square", l, which, k))

            def norm(l, which):
                tiles = slice(0, 4) if which == 0 or l == 0 else slice(2, 4)
                cols = slice(0 if which == 0 else c0(l), T)
                act.wait_ge(pe_done.sem, pe_done.after("squared", l, which, KD - 1))
                finish(act.activation(rt[:, 0, tiles], oo[:, tiles], ACT.Sqrt, bias=EPS,
                                      scale=1.0 / D), ("read", ("stat", l, which)))
                act.wait_ge(pe_done.sem, pe_done.after("spread", l, which))
                finish(act.activation(rstd[:, cols], bank(("spread", l, which))[:, cols], ACT.Copy),
                       ("read", ("spread", l, which)))

            def modulate(l, which):
                for k in range(KD):
                    for s, a in ([(0, 0), (1, CTX)] if which == 0 else streams(l)):
                        act.wait_ge(dve_done.sem, dve_done.after("ht", l, which, k, s))
                        finish(act.activation(h_hi[:, k, a:a + CTX], ht[:, k % 2, a:a + CTX], ACT.Identity,
                                              bias=modv[:, (0 if which == 0 else 3 * KD) + k, s:s + 1]),
                               ("h_hi", l, which, k, s))

            def proj(l, kind, t):
                key = ("proj", l, kind, t)
                b = bank(key)
                act.wait_ge(pe_done.sem, pe_done.after(*key))
                if kind == "cu":
                    act.wait_ge(dve_done.sem, dve_done.after("pad", l))
                    finish(act.activation(cu[:, t, :, 2:2 + CTX], b.rearrange("p (s n) -> p s n", s=2), ACT.Copy),
                           ("read", key))
                elif kind in ("av", "bv"):
                    col = 0 if kind == "av" else P * (t + 1)
                    finish(act.activation(vv[:, :, col:col + P], b.rearrange("p (t n) -> p t n", n=P), ACT.Copy),
                           ("read", key), ("v", l, kind, t))
                elif kind == "cg":
                    if t:
                        act.wait_ge(dve_done.sem, dve_done.after("y_c", l, t - 1))
                    finish(act.activation(gel[:, c0(l):T], b[:, c0(l):T], ACT.Gelu_apprx_tanh), ("read", key))
                else:
                    dst = {"aq": q_a, "ak": k_a, "bq": q_b, "bk": k_b}[kind]
                    cols = slice(0 if kind in ("ak", "bk") else c0(l), T)
                    finish(act.activation(dst[:, t, cols], b[:, cols], ACT.Copy), ("read", key))
                    if kind == "ak":
                        act.wait_ge(dve_done.sem, dve_done.after("qk", l, kind, t))
                        own()
                        finish(act.activation(k_sw[0:HEAD, 0, :], k_a[HEAD:P, 0, :], ACT.Copy))
                        finish(act.activation(k_sw[HEAD:P, 0, :], k_a[0:HEAD, 0, :], ACT.Copy), ("k_sw", l))

            def lru(l, t):
                for d in range(2):
                    kd = kdec[:, 0, d * 4 + t:d * 4 + t + 1]
                    kn = kdec[:, 1, d * 4 + t:d * 4 + t + 1]
                    if d == 0:
                        act.wait_ge(dve_done.sem, dve_done.after("kdec", l))
                        if t:
                            act.wait_ge(dve_done.sem, dve_done.after("hsum", l, t - 1))
                    for g, dst in ((0, l_r), (1, l_i)):
                        key = ("gate", l, t, d, g)
                        act.wait_ge(pe_done.sem, pe_done.after(*key))
                        j = (d * 2 + g) * KC + t
                        finish(act.activation(dst[:, d], bank(key), ACT.Tanh, bias=hb[:, j:j + 1], scale=0.5),
                               ("read", key), ("l_gate", l, t, d, g))
                    act.wait_ge(act_done.sem, act_done.after("l_gate", l, t, d, 0))
                    finish(act.activation(l_a[:, d], l_r[:, d], ACT.Exp, bias=kd, scale=kd), ("l_a", l, t, d))
                    own()
                    finish(act.activation(l_r[:, d], l_r[:, d], ACT.Tanh, bias=kn, scale=kn), ("l_th", l, t, d))
                for d in range(2):
                    act.wait_ge(dve_done.sem, dve_done.after("l_q", l, t, d))
                    finish(act.activation(l_q[:, d], l_q[:, d], ACT.Sqrt, scale=0.25), ("l_sqrt", l, t, d))

            def nk(t):
                return T if t >= 2 else CTX

            def exp(l, n, ring, t, key):
                act.wait_ge(pe_done.sem, pe_done.after(*key))
                act.wait_ge(dve_done.sem, dve_done.after("nmax", l, n))
                finish(act.activation(pp[:, ring, 0:nk(t)], sc[:, n % 3, 0:nk(t)], ACT.Exp, bias=sm[:, n % 8, 1:2],
                                      scale=SCALE, accum_out=sm[:, n % 8, 2:3]), ("exp", l, n))

            def copy_pt(key, slot, t):
                act.wait_ge(pe_done.sem, pe_done.after(*key))
                finish(act.activation(pt[:, slot, 0:nk(t) // P, :].rearrange("p j n -> p (j n)"), bank(key)[:, 0:nk(t)], ACT.Copy),
                       ("read", key))

            def attend_b(l):
                units = [(t, h) for t in qtiles(l) for h in range(B_HEADS)]

                def turned(i):
                    t, h = units[i]
                    if i >= 2:
                        act.wait_ge(pe_done.sem, pe_done.after("pv_b", l, i - 2))
                    copy_pt(("pt_b", l, t, h), i % 2, t)

                def out(i):
                    t, h = units[i]
                    j = i // B_HEADS
                    act.wait_ge(pe_done.sem, pe_done.after("pv_b", l, i))
                    o = bank(("pv_b", l, i))[:, 0:P]
                    finish(act.activation(yrow[:, j, h * P:(h + 1) * P], o, ACT.Copy), ("yraw", l, i))
                    own()
                    finish(act.activation(ww_sq(i), o, ACT.Square, accum_out=bss[:, j, h:h + 1]),
                           ("read", ("pv_b", l, i)))

                def ww_sq(i):
                    return gel[:, i % 2 * P:(i % 2 + 1) * P]

                act.wait_ge(dve_done.sem, dve_done.after("y_c", l, KC - 1))
                for i, (t, h) in enumerate(units):
                    for m in range(2):
                        n = 2 * i + m
                        if i >= 2:
                            act.wait_ge(dve_done.sem, dve_done.after("w_b", l, i - 2))
                        exp(l, n, n % 4, t, ("s_b", l, n))
                    if i >= 1:
                        turned(i - 1)
                    if i >= 2:
                        out(i - 2)
                last = len(units) - 1
                turned(last)
                out(last - 1)
                out(last)
                own()
                finish(act.activation(bst[:, 0, :], bss[:].rearrange("p a b -> p (a b)")[:, 0:16], ACT.Sqrt, bias=EPS,
                                      scale=1.0 / B_VDIM), ("bst", l))

            def attend_a(l):
                units = [(t, h) for t in qtiles(l) for h in range(A_HEADS)]
                nb = 2 * len(qtiles(l)) * B_HEADS

                def turned(i):
                    t, h = units[i]
                    if i >= 2:
                        act.wait_ge(pe_done.sem, pe_done.after("pv_a", l, i - 2))
                    else:
                        act.wait_ge(pe_done.sem, pe_done.after("pv_b", l, nb // 2 - 2 + i))
                    copy_pt(("pt_a", l, t, h), i % 2, t)

                def rows(name, dst, t, scale):
                    key = (name, l, t)
                    act.wait_ge(pe_done.sem, pe_done.after(*key))
                    finish(act.activation(dst[:, :, t * P:(t + 1) * P], bank(key).rearrange("p (j n) -> p j n", n=P),
                                          ACT.Copy, scale=scale), ("read", key), ("yT", l, name, t))

                for i, (t, h) in enumerate(units):
                    n = nb + i
                    if i >= 4:
                        act.wait_ge(pe_done.sem, pe_done.after("pt_a", l, *units[i - 4]))
                    else:
                        act.wait_ge(dve_done.sem, dve_done.after("w_b", l, nb // 2 - 1))
                    exp(l, n, i % 4, t, ("s_a", l, i))
                    finish(act.activation(sm[:, n % 8, 3:4], vec[:, l, V_SINK + h:V_SINK + h + 1], ACT.Exp,
                                          bias=sm[:, n % 8, 1:2]), ("exp_sink", l, n))
                    if i == 0:
                        for u in qtiles(l):
                            rows("yt_b", q_b, u, gsub[:, 0:1])
                    if i and h:
                        turned(i - 1)
                    if h == A_HEADS - 1:
                        turned(i)
                        rows("yt_a", q_a, t, 1.0)

            def ysplit(l):
                cols = slice(c0(l), T)
                act.wait_ge(pe_done.sem, pe_done.after("yt_a", l, qtiles(l)[-1]))
                own()
                for c in range(12):
                    src = (q_a, q_b, y_c)[c // KC]
                    if c // KC == 2:
                        act.wait_ge(dve_done.sem, dve_done.after("y_c", l, c % KC))
                    finish(act.activation(yh[:, c, cols], src[:, c % KC, cols], ACT.Copy), ("y_hi", l, c))

            def merge(l, m):
                cols = slice(c0(l), T)
                for n in range(N_BRANCH):
                    key = ("mgate", l, m, n)
                    u = m * N_BRANCH + n
                    act.wait_ge(pe_done.sem, pe_done.after(*key))
                    if u >= 2:
                        act.wait_ge(dve_done.sem, dve_done.after("read", ("mbranch", l, *divmod(u - 2, N_BRANCH))))
                    else:
                        act.wait_ge(dve_done.sem, dve_done.after("y_lo", l, 11))
                    finish(act.activation(tg[:, u % 2, cols], bank(key)[:, cols], ACT.Tanh, scale=0.5),
                           ("read", key), ("tg", l, m, n))
                act.wait_ge(dve_done.sem, dve_done.after("mixt", l, m))
                finish(act.activation(mx_hi[:, m, cols], mixt[:, cols], ACT.Copy, scale=0.5), ("mx_hi", l, m))

            def wout(l, m):
                key = ("wout", l, m)
                act.wait_ge(pe_done.sem, pe_done.after(*key))
                finish(act.activation(fout[:, m, c0(l):T], bank(key)[:, c0(l):T], ACT.Copy), ("read", key))

            def ffn_in(l, j):
                key, cols = ("fgate", l, j), slice(c0(l), T)
                act.wait_ge(pe_done.sem, pe_done.after(*key))
                if j >= 2:
                    act.wait_ge(dve_done.sem, dve_done.after("read", ("fup", l, j - 2)))
                finish(act.activation(sg[:, j % 2, cols], bank(key)[:, cols], ACT.Silu), ("read", key))
                act.wait_ge(dve_done.sem, dve_done.after("read", ("fup", l, j)))
                finish(act.activation(f_hi[:, j, cols], hid[:, cols], ACT.Copy), ("f_hi", l, j))

            def ffn_out(l, m):
                key = ("ffn_out", l, m)
                act.wait_ge(pe_done.sem, pe_done.after(*key))
                finish(act.activation(fout[:, m, c0(l):T], bank(key)[:, c0(l):T], ACT.Copy), ("read", key))

            def residual(l, which):
                pass

            act.wait_ge(consts_loaded, 16 * 6)
            finish(act.activation(cs[:], cT[:], ACT.Silu), ("silu_c",))
            steps = dict(mod=mod, square=square, norm=norm, modulate=modulate, proj=proj, lru=lru, attend_b=attend_b,
                         attend_a=attend_a, ysplit=ysplit, merge=merge, wout=wout, ffn_in=ffn_in, ffn_out=ffn_out,
                         residual=residual)
            for step, *args in plan:
                steps[step](*args)

        @block.vector
        def _(dve):
            split = [0]

            def finish(ins, *names):
                ins.then_inc(dve_done.sem, dve_done.mark(*names))

            def own():
                dve.wait_ge(dve_done.sem, dve_done.count)

            def splits(key):
                n = blocks_end[key]
                before = n - info[key][0]
                limit = min(max(before // 8 + SPLIT, -(-n // 8)), DEPTH * N_GRAN)
                while split[0] < limit:
                    q = split[0]
                    dve.wait_ge(pool_done.sem, pool_done.after("w_hi", q))
                    finish(dve.tensor_tensor(w_lo[:, q % SPLIT].rearrange("p k n -> p (k n)"), raw[:, gran_of(q) % RAW, :],
                                             w_hi[:, q % SPLIT].bitcast(F32).rearrange("p k n -> p (k n)"),
                                             ALU.subtract), ("w_lo", q))
                    split[0] += 1

            def mod(l):
                v = vec[:, l]
                dl = v[:, V_DL:V_DL + 256].rearrange("p (a b n) -> p a b n", a=2, b=2)
                finish(dve.tensor_tensor(rstd[:, 0:128].rearrange("p (a n) -> p a n", a=2), dl[:, :, 0, :], dl[:, :, 1, :], ALU.mult))
                own()
                finish(dve.tensor_reduce(small[:, 16:18], rstd[:, 0:128].rearrange("p (a n) -> p a n", a=2), AX, ALU.add),
                       ("dots", l))
                init = 0.8 - 0.6 * math.exp(-0.3 * l)
                dve.wait_ge(act_done.sem, act_done.after("exp_dots", l))
                finish(dve.tensor_tensor(nlam[:, 2:3], nlam[:, 1:2], nlam[:, 0:1], ALU.subtract))
                own()
                finish(dve.tensor_scalar(nlam[:, 3:4], nlam[:, 2:3], -init, None, ALU.add))
                finish(dve.tensor_scalar(gsub[:], v[:, V_SUB:V_SUB + 1], 1.0 - init, None, ALU.mult), ("gsub", l))
                finish(dve.tensor_scalar(nsink[:], v[:, V_SINK:V_SINK + 8], -1.0, None, ALU.mult))
                finish(dve.tensor_scalar(hb[:], v[:, V_LB:V_LB + 16], 0.5, None, ALU.mult))
                dve.wait_ge(act_done.sem, act_done.after("exp_lam", l))
                y, z, z2, p = small[:, 8:16], small[:, 24:32], small[:, 32:40], small[:, 40:48]
                w = small[:, 48:56]
                finish(dve.tensor_scalar(w, y, 2.0, None, ALU.add))
                own()
                finish(dve.reciprocal(p, w))
                own()
                finish(dve.tensor_tensor(z, y, p, ALU.mult))
                own()
                finish(dve.tensor_tensor(z2, z, z, ALU.mult))
                own()
                finish(dve.tensor_scalar(p, z2, 1.0 / 17, None, ALU.mult))
                for c in (15, 13, 11, 9, 7, 5, 3):
                    own()
                    finish(dve.scalar_tensor_tensor(p, p, 1.0 / c, z2, ALU.add, ALU.mult))
                own()
                finish(dve.scalar_tensor_tensor(p, p, 1.0, z, ALU.add, ALU.mult))
                finish(dve.tensor_scalar(w, v[:, V_LAM:V_LAM + 8], -1.0, 0.0, ALU.mult, ALU.max))
                own()
                finish(dve.scalar_tensor_tensor(z, p, 2.0, w, ALU.mult, ALU.add))
                own()
                finish(dve.tensor_scalar(kdec[:, 0, :], z, -4.0, None, ALU.mult))
                finish(dve.tensor_scalar(kdec[:, 1, :], z, 4.0, None, ALU.mult), ("kdec", l))
                dve.wait_ge(pe_done.sem, pe_done.after("mod", l, N_MOD - 1))
                finish(dve.tensor_tensor(modv[:], oo[:, 0:2 * N_MOD].rearrange("p (j s) -> p j s", s=2),
                                         v[:, V_BMOD:V_BMOD + 96].rearrange("p (j s) -> p j s", s=2), ALU.add),
                       ("modv", l))
                own()
                for i, (chunk, add) in enumerate(((1, 1.0), (2, 0.0), (4, 1.0), (5, 0.0))):
                    finish(dve.scalar_tensor_tensor(gain[:, i].rearrange("p k s -> p (k s)"),
                                                    modv[:, chunk * KD:(chunk + 1) * KD, :].rearrange("p k s -> p (k s)"), add,
                                                    v[:, V_G + 16 * i:V_G + 16 * (i + 1)], ALU.add, ALU.mult),
                           ("gain", l, i))

            def square(l, which, k):
                pass

            def norm(l, which):
                tiles = range(4) if which == 0 else qtiles(l)
                dve.wait_ge(act_done.sem, act_done.after("read", ("stat", l, which)))
                finish(dve.reciprocal(rt[:, 1, tiles[0]:4], rt[:, 0, tiles[0]:4]))
                own()
                for t in tiles:
                    finish(dve.tensor_scalar(diag[:, t, :], ident[:], rt[:, 1, t:t + 1], None, ALU.mult),
                           ("diag", l, which, t))

            def modulate(l, which):
                def low(k):
                    for s, a in sts:
                        dve.wait_ge(act_done.sem, act_done.after("h_hi", l, which, k, s))
                        finish(dve.scalar_tensor_tensor(h_lo[:, k, a:a + CTX], ht[:, k % 2, a:a + CTX],
                                                        modv[:, (0 if which == 0 else 3 * KD) + k, s:s + 1],
                                                        h_hi[:, k, a:a + CTX].bitcast(F32), ALU.add, ALU.subtract),
                               ("h_lo", l, which, k))

                sts = [(0, 0), (1, CTX)] if which == 0 else streams(l)
                dve.wait_ge(act_done.sem, act_done.after("read", ("spread", l, which)))
                for k in range(KD):
                    if k >= 2:
                        dve.wait_ge(dve_done.sem, dve_done.after("h_lo", l, which, k - 2))
                    for s, a in sts:
                        finish(dve.scalar_tensor_tensor(ht[:, k % 2, a:a + CTX], xT[:, k, a:a + CTX],
                                                        gain[:, which, k, s:s + 1], rstd[:, a:a + CTX], ALU.mult, ALU.mult),
                               ("ht", l, which, k, s))
                    if k:
                        low(k - 1)
                low(KD - 1)

            def proj(l, kind, t):
                key = ("proj", l, kind, t)
                if (kind, t) == ("cu", 0):
                    finish(dve.memset(cu[:, :, :, 0:2], 0.0))
                    finish(dve.memset(cu[:, :, :, 2 + CTX:4 + CTX], 0.0), ("pad", l))
                splits(key)
                b = bank(key)
                if kind == "cu":
                    dve.wait_ge(act_done.sem, act_done.after("read", key))
                    u = uu[:, t].rearrange("p (s n) -> p s n", s=2)
                    tap = lambda i: vec[:, l, V_CW + i * KC + t:V_CW + i * KC + t + 1]
                    own()
                    finish(dve.tensor_scalar(u, cu[:, t, :, 0:CTX], tap(0), vec[:, l, V_CB + t:V_CB + t + 1], ALU.mult, ALU.add))
                    for i in range(1, CONV_W):
                        own()
                        finish(dve.scalar_tensor_tensor(u, cu[:, t, :, i:i + CTX], tap(i), u, ALU.mult, ALU.add),
                               ("conv", l, t))
                elif kind == "cg":
                    dve.wait_ge(act_done.sem, act_done.after("read", key))
                    dve.wait_ge(dve_done.sem, dve_done.after("hsum", l, t))
                    cols = slice(c0(l), T)
                    finish(dve.tensor_tensor(y_c[:, t, cols], gel[:, cols], uu[:, t, cols], ALU.mult), ("y_c", l, t))
                elif kind in ("aq", "ak", "bq", "bk"):
                    dst = {"aq": q_a, "ak": k_a, "bq": q_b, "bk": k_b}[kind][:, t, CTX:T]
                    dve.wait_ge(act_done.sem, act_done.after("read", key))
                    own()
                    finish(dve.stream_shuffle(rope[:, 0, :], dst, [i ^ 16 for i in range(32)]))
                    own()
                    finish(dve.tensor_tensor(dst, dst, cos[:], ALU.mult))
                    finish(dve.tensor_tensor(rope[:, 1, :], rope[:, 0, :], sin[:], ALU.mult))
                    own()
                    finish(dve.tensor_tensor(dst, dst, rope[:, 1, :], ALU.add), ("qk", l, kind, t))

            def lru(l, t):
                for d in range(2):
                    dve.wait_ge(act_done.sem, act_done.after("l_a", l, t, d))
                    finish(dve.tensor_tensor(l_q[:, d], l_a[:, d], l_a[:, d], ALU.mult))
                    dve.wait_ge(act_done.sem, act_done.after("l_gate", l, t, d, 1))
                    finish(dve.scalar_tensor_tensor(l_i[:, d], l_i[:, d], 1.0, uu[:, t], ALU.add, ALU.mult))
                    dve.wait_ge(act_done.sem, act_done.after("l_th", l, t, d))
                    own()
                    finish(dve.scalar_tensor_tensor(l_q[:, d], l_q[:, d], 1.0, l_r[:, d], ALU.add, ALU.mult),
                           ("l_q", l, t, d))
                for d in range(2):
                    dve.wait_ge(act_done.sem, act_done.after("l_sqrt", l, t, d))
                    finish(dve.tensor_tensor(l_i[:, d], l_i[:, d], l_q[:, d], ALU.mult))
                    own()
                    if d == 0:
                        finish(dve.tensor_tensor_scan(l_r[:, 0], l_a[:, 0], l_i[:, 0], 0.0, ALU.mult, ALU.add))
                    else:
                        finish(dve.tensor_tensor_scan(l_r[:, 1, CTX - 1::-1], l_a[:, 1, CTX - 1::-1],
                                                      l_i[:, 1, CTX - 1::-1], 0.0, ALU.mult, ALU.add))
                        own()
                        finish(dve.tensor_tensor_scan(l_r[:, 1, T - 1:CTX - 1:-1], l_a[:, 1, T - 1:CTX - 1:-1],
                                                      l_i[:, 1, T - 1:CTX - 1:-1], l_r[:, 1, 0:1], ALU.mult, ALU.add))
                own()
                cols = slice(c0(l), T)
                finish(dve.tensor_tensor(uu[:, t, cols], l_r[:, 0, cols], l_r[:, 1, cols], ALU.add), ("hsum", l, t))

            def nk(t):
                return T if t >= 2 else CTX

            def row_max(l, n, key, t, sink):
                dve.wait_ge(pe_done.sem, pe_done.after(*key))
                finish(dve.tensor_reduce(sm[:, n % 8, 0:1], sc[:, n % 3, 0:nk(t)], AX, ALU.max, negate=True))
                own()
                if sink is None:
                    ins = dve.tensor_scalar(sm[:, n % 8, 1:2], sm[:, n % 8, 0:1], SCALE, None, ALU.mult)
                else:
                    ins = dve.tensor_scalar(sm[:, n % 8, 1:2], sm[:, n % 8, 0:1], SCALE, sink, ALU.mult, ALU.min)
                finish(ins, ("nmax", l, n))

            def attend_b(l):
                units = [(t, h) for t in qtiles(l) for h in range(B_HEADS)]

                def combine(i):
                    t, h = units[i]
                    a, b = 2 * i, 2 * i + 1
                    cols = slice(0, nk(t))
                    dve.wait_ge(act_done.sem, act_done.after("exp", l, b))
                    finish(dve.reciprocal(sm[:, a % 8, 4:5], sm[:, a % 8, 2:3]))
                    finish(dve.reciprocal(sm[:, b % 8, 4:5], sm[:, b % 8, 2:3]))
                    own()
                    finish(dve.tensor_scalar(sm[:, b % 8, 5:6], sm[:, b % 8, 4:5], nlam[:, 3:4], None, ALU.mult))
                    if i >= 2:
                        dve.wait_ge(pe_done.sem, pe_done.after("pt_b", l, *units[i - 2]))
                    finish(dve.tensor_scalar(ww[:, i % 2, cols], pp[:, a % 4, cols], sm[:, a % 8, 4:5], None, ALU.mult))
                    own()
                    finish(dve.scalar_tensor_tensor(ww[:, i % 2, cols], pp[:, b % 4, cols], sm[:, b % 8, 5:6],
                                                    ww[:, i % 2, cols], ALU.mult, ALU.add), ("w_b", l, i))

                for i, (t, h) in enumerate(units):
                    for m in range(2):
                        n = 2 * i + m
                        row_max(l, n, ("s_b", l, n), t, None)
                    if i:
                        combine(i - 1)
                combine(len(units) - 1)

            def attend_a(l):
                units = [(t, h) for t in qtiles(l) for h in range(A_HEADS)]
                nb = 2 * len(qtiles(l)) * B_HEADS

                def out(i):
                    t, h = units[i]
                    r = (nb + i) % 8
                    dve.wait_ge(act_done.sem, act_done.after("exp_sink", l, nb + i))
                    finish(dve.tensor_tensor(sm[:, r, 4:5], sm[:, r, 2:3], sm[:, r, 3:4], ALU.add))
                    own()
                    finish(dve.reciprocal(sm[:, r, 5:6], sm[:, r, 4:5]))
                    own()
                    dve.wait_ge(pe_done.sem, pe_done.after("pv_a", l, i))
                    if i >= 2 * A_HEADS:
                        dve.wait_ge(pe_done.sem, pe_done.after("yt_a", l, t - 2))
                    finish(dve.tensor_scalar(yrow_a[:, t % 2, h * HEAD:(h + 1) * HEAD], bank(("pv_a", l, i))[:, 0:HEAD],
                                             sm[:, r, 5:6], None, ALU.mult), ("o_a", l, t, h), ("read", ("pv_a", l, i)))

                def norm_b():
                    dve.wait_ge(act_done.sem, act_done.after("bst", l))
                    finish(dve.reciprocal(bst[:, 1, :], bst[:, 0, :]))
                    own()
                    for j, t in enumerate(qtiles(l)):
                        for h in range(B_HEADS):
                            c = slice(h * P, (h + 1) * P)
                            finish(dve.tensor_scalar(yrow[:, j, c], yrow[:, j, c], bst[:, 1, j * 4 + h:j * 4 + h + 1],
                                                     None, ALU.mult), ("yrow_b", l, t))

                row_max(l, nb, ("s_a", l, 0), units[0][0], nsink[:, units[0][1]:units[0][1] + 1])
                norm_b()
                for i, (t, h) in enumerate(units):
                    if i:
                        row_max(l, nb + i, ("s_a", l, i), t, nsink[:, h:h + 1])
                    if h >= 2:
                        out(i - 2)
                    if h == A_HEADS - 1:
                        out(i - 1)
                        out(i)

            def ysplit(l):
                cols = slice(c0(l), T)
                for c in range(12):
                    src = (q_a, q_b, y_c)[c // KC]
                    dve.wait_ge(act_done.sem, act_done.after("y_hi", l, c))
                    finish(dve.tensor_tensor(yl[:, c, cols], src[:, c % KC, cols], yh[:, c, cols].bitcast(F32),
                                             ALU.subtract), ("y_lo", l, c))

            def merge(l, m):
                cols = slice(c0(l), T)
                for n in range(N_BRANCH):
                    splits(("mgate", l, m, n))
                    key = ("mbranch", l, m, n)
                    splits(key)
                    u = m * N_BRANCH + n
                    dve.wait_ge(act_done.sem, act_done.after("tg", l, m, n))
                    dve.wait_ge(pe_done.sem, pe_done.after(*key))
                    if n == 0:
                        if m:
                            dve.wait_ge(dve_done.sem, dve_done.after("mx_lo", l, m - 1))
                            dve.wait_ge(act_done.sem, act_done.after("mx_hi", l, m - 1))
                        finish(dve.scalar_tensor_tensor(mixt[:, cols], tg[:, u % 2, cols], 1.0, bank(key)[:, cols], ALU.add,
                                                        ALU.mult), ("read", key))
                    else:
                        own()
                        finish(dve.scalar_tensor_tensor(mixu[:, cols], tg[:, u % 2, cols], 1.0, bank(key)[:, cols], ALU.add,
                                                        ALU.mult), ("read", key))
                        own()
                        finish(dve.tensor_tensor(mixt[:, cols], mixt[:, cols], mixu[:, cols], ALU.add), ("mixt", l, m))
                dve.wait_ge(act_done.sem, act_done.after("mx_hi", l, m))
                finish(dve.scalar_tensor_tensor(mx_lo[:, m, cols], mixt[:, cols], 0.5, mx_hi[:, m, cols].bitcast(F32),
                                                ALU.mult, ALU.subtract), ("mx_lo", l, m))

            def wout(l, m):
                splits(("wout", l, m))

            def residual(l, which):
                cols = slice(c0(l), T)
                dve.wait_ge(act_done.sem, act_done.after("read", ("spread", l, which)))
                for k in range(KD):
                    for s, a in streams(l):
                        finish(dve.scalar_tensor_tensor(ht[:, k % 2, a:a + CTX], fout[:, k, a:a + CTX],
                                                        gain[:, which, k, s:s + 1], rstd[:, a:a + CTX], ALU.mult, ALU.mult))
                    own()
                    finish(dve.tensor_tensor(xT[:, k, cols], xT[:, k, cols], ht[:, k % 2, cols], ALU.add),
                           ("x", l, which, k))

            def ffn_in(l, j):
                cols = slice(c0(l), T)
                splits(("fgate", l, j))
                key = ("fup", l, j)
                splits(key)
                dve.wait_ge(act_done.sem, act_done.after("read", ("fgate", l, j)))
                dve.wait_ge(pe_done.sem, pe_done.after(*key))
                if j:
                    own()
                finish(dve.tensor_tensor(hid[:, cols], sg[:, j % 2, cols], bank(key)[:, cols], ALU.mult), ("read", key))
                dve.wait_ge(act_done.sem, act_done.after("f_hi", l, j))
                own()
                finish(dve.tensor_tensor(f_lo[:, j, cols], hid[:, cols], f_hi[:, j, cols].bitcast(F32), ALU.subtract),
                       ("f_lo", l, j))

            def ffn_out(l, m):
                splits(("ffn_out", l, m))

            dve.wait_ge(consts_loaded, 16 * 6)
            finish(dve.tensor_copy(identb[:], ident[:]))
            finish(dve.tensor_copy(mask[:], maskf[:]), ("mask",))
            own()
            steps = dict(mod=mod, square=square, norm=norm, modulate=modulate, proj=proj, lru=lru, attend_b=attend_b,
                         attend_a=attend_a, ysplit=ysplit, merge=merge, wout=wout, ffn_in=ffn_in, ffn_out=ffn_out,
                         residual=residual)
            for step, *args in plan:
                steps[step](*args)

    return {"pe_done": pe_done.marks, "act_done": act_done.marks, "dve_done": dve_done.marks, "pool_done": pool_done.marks}


def build(make, shapes, launch_args):
    known = {n: {} for n in ("pe_done", "act_done", "dve_done", "pool_done")}
    nc = None
    for _ in range(2):
        nc = make()
        io = {n: nc.dram_tensor(f"{n}_dram", s, F32, kind=k).ap() for n, (s, k) in shapes.items()}
        known = program(nc, io, known)
    return nc


def rotary_tables():
    rd = HEAD // 4
    t = np.arange(SEQ)
    pos = np.stack([t // GRID_W, t % GRID_W]).astype(np.float32)
    inv = (1.0 / (10000.0 ** (np.arange(rd, dtype=np.float32) * 2.0 / (HEAD // 2)))).astype(np.float32)
    cos, sin = np.zeros((HEAD, SEQ), np.float32), np.zeros((HEAD, SEQ), np.float32)
    for axis in range(2):
        ang = (pos[axis][None, :] * inv[:, None]).astype(np.float32)
        for half in range(2):
            rows = slice((axis * 2 + half) * rd, (axis * 2 + half + 1) * rd)
            cos[rows] = np.cos(ang)
            sin[rows] = np.sin(ang) * (1 if half else -1)
    return np.tile(cos, (2, 1)), np.tile(sin, (2, 1))


def window_mask():
    q = np.arange(SEQ)[:, None]
    k = np.arange(SEQ)[None, :]
    m = np.where(np.abs(k - q) <= WINDOW, 0.0, MASKED).astype(np.float32)
    return np.ascontiguousarray(m.reshape(2, P, SEQ).transpose(1, 0, 2))


def columns(a):
    a = np.asarray(a)
    return a.reshape(-1, P).T


def kernel(x, c, ctx, c_ctx, w_mod, b_mod, norm_g, w_in, attn_sink, diff_lambda, diff_subln, conv_w, conv_b, lru_w,
           lru_b, lru_lambda, w_branch, w_out, w_ffn_in, w_ffn_out):
    import concourse.bacc as bacc
    from concourse.bass_utils import run_bass_kernel_spmd

    def blocks(w):
        w = np.asarray(w)
        k, n = w.shape
        return w.reshape(k // P, P, n // P, P).transpose(0, 2, 1, 3)

    order = block_order()
    stream = np.empty((DEPTH * (N_MOD + N_GRAN), P, 8, P), np.float32)
    for l in range(DEPTH):
        base = l * (N_MOD + N_GRAN)
        stream[base:base + N_MOD] = blocks(w_mod[l]).transpose(1, 2, 0, 3)
        cut = {"w_in": blocks(w_in[l]), "w_branch": blocks(np.asarray(w_branch[l]).reshape(N_BRANCH * C_W, D)),
               "w_out": blocks(w_out[l]), "w_ffn_in": blocks(w_ffn_in[l]), "w_ffn_out": blocks(w_ffn_out[l])}
        for i, (name, k, n) in enumerate(order):
            stream[base + N_MOD + i // 8, :, i % 8, :] = cut[name][k, n]

    vec = np.empty((P, DEPTH, V_N), np.float32)
    lruw = np.zeros((DEPTH, P, 16, P), np.float32)
    for l in range(DEPTH):
        v = vec[:, l]
        v[:, V_BMOD:V_BMOD + 96] = np.repeat(columns(b_mod[l]), 2, axis=1)
        v[:, V_G:V_G + 64] = np.repeat(columns(norm_g[l]), 2, axis=1)
        v[:, V_CW:V_CW + 16] = columns(conv_w[l])
        v[:, V_CB:V_CB + 4] = columns(conv_b[l])
        v[:, V_LB:V_LB + 16] = columns(lru_b[l])
        v[:, V_LAM:V_LAM + 8] = columns(lru_lambda[l])
        v[:, V_SINK:V_SINK + 8] = np.asarray(attn_sink[l])[None, :]
        v[:, V_DL:V_DL + 256] = np.asarray(diff_lambda[l]).reshape(1, 256)
        v[:, V_SUB] = np.asarray(diff_subln[l])
        w = np.asarray(lru_w[l]).reshape(4, C_BLOCKS, HEAD, HEAD)
        for dg in range(4):
            for n in range(C_BLOCKS):
                half = slice(HEAD * (n % 2), HEAD * (n % 2 + 1))
                lruw[l, half, dg * KC + n // 2, half] = w[dg, n]

    cos, sin = rotary_tables()
    both = np.concatenate([np.asarray(ctx)[0], np.asarray(x)[0]], axis=0)
    arrays = {
        "xT": both.T.reshape(KD, P, T).transpose(1, 0, 2),
        "cT": np.stack([columns(c_ctx), columns(np.asarray(c)[0])], axis=2),
        "vec": vec, "lruw": lruw, "stream": stream.reshape(-1, P, 8 * P),
        "ident": np.eye(P, dtype=np.float32), "cos": cos, "sin": sin, "maskf": window_mask(),
    }
    arrays = {n: np.ascontiguousarray(a) for n, a in arrays.items()}
    shapes = {n: (a.shape, "ExternalInput") for n, a in arrays.items()}
    shapes["out"] = ((P, KD, SEQ), "ExternalOutput")
    nc = build(lambda: bacc.Bacc("TRN2", target_bir_lowering=False, num_devices=1), shapes, None)
    result = run_bass_kernel_spmd(nc, [{f"{n}_dram": a for n, a in arrays.items()}], core_ids=[0])
    out = result.results[0]["out_dram"]
    return np.ascontiguousarray(out.transpose(1, 0, 2).reshape(D, SEQ).T)[None]
```

```python
import math
from contextlib import ExitStack

import numpy as np
import concourse.bass as bass
from concourse import mybir

P = 128
F32, F32R, BF16 = mybir.dt.float32, mybir.dt.float32r, mybir.dt.bfloat16
ACT = mybir.ActivationFunctionType
ALU = mybir.AluOpType
AX = mybir.AxisListType.X

DEPTH, D, SEQ, CTX = 2, 1024, 256, 256
T = CTX + SEQ
KD = D // P
HEAD = 64
A_HEADS, A_KV, B_HEADS, B_VDIM = 8, 2, 4, 128
C_W, CONV_W, C_BLOCKS = 512, 4, 8
KC = C_W // P
N_BRANCH = 3
FFN = 2816
KF = FFN // P
EPS = 1e-6
SCALE = HEAD ** -0.5
GRID_W, WINDOW = 64, 128
MASKED = -1e30

IN_TILE = {"aq": 0, "ak": 4, "av": 5, "bq": 6, "bk": 10, "bv": 14, "cu": 18, "cg": 22, "gt": 26}
N_STORED = (9, 18)
MOD_ROUNDS, MOD_COLS = 3, 2048
ACC = 4
RAW = 3
SPLIT = 3

V_BMOD, V_G, V_CW, V_CB, V_LB, V_LAM, V_SINK, V_SUB = 0, 96, 160, 176, 180, 196, 204, 212
V_N = 213


def plan_layer(l):
    tiles = [0, 1, 2, 3] if l == 0 else [2, 3]
    gates = [("gate_store", l, *divmod(i, N_BRANCH)) for i in range(N_STORED[l])]
    if l == 0:
        steps = [("square", 0, 0, k) for k in range(KD)] + [("norm", 0, 0)]
        steps += [("modk", 0, 0, k) for k in range(KD)] + [("modend", 0, 0), ("modulate", 0, 0)]
    else:
        steps = [("square", l, 0, k) for k in range(KD)] + [("norm", l, 0), ("modulate", l, 0)]

    first = [("proj", l, "cg", t) for t in range(KC)]
    first += [("proj", l, "cu", 0), ("proj", l, "cu", 1), ("lru", l, 0), ("proj", l, "cu", 2), ("lru", l, 1),
              ("proj", l, "cu", 3), ("lru", l, 2), ("proj", l, "bk", 0), ("proj", l, "bq", 0), ("lru", l, 3)]
    first += [("proj", l, kind, h) for kind, h in (("bv", 0), ("bk", 1), ("bq", 1), ("bv", 1))]
    k = 0
    for step in first:
        steps.append(step)
        if l == 0 and step[0] == "proj" and k < KD:
            steps.append(("modk", 0, 1, k))
            k += 1
    if l == 0:
        steps.append(("modend", 0, 1))

    fill = [("proj", l, kind, t) for kind, t in (
        ("bk", 2), ("bq", 2), ("bv", 2), ("ak", 0), ("bk", 3), ("bq", 3), ("bv", 3), ("av", 0), ("aq", 0), ("aq", 1),
        ("aq", 2), ("aq", 3))] + gates[:4]
    n = len(tiles) * B_HEADS
    each = len(fill) // n
    steps.append(("b_start", l))
    for i in range(n):
        steps += [("b", l, i)] + fill[i * each:(i + 1) * each]
    steps += [("b_end", l)]

    fill = gates[4:]
    n = len(tiles) * A_HEADS
    steps += [("a_start", l), fill[0], ("b_rows", l)]
    fill = fill[1:]
    done = k = 0
    for i in range(n):
        steps.append(("a", l, i))
        if i % A_HEADS == 1 and i > A_HEADS:
            steps.append(("a_rows", l, tiles[i // A_HEADS - 1]))
        if l == 0 and i % 4 == 2:
            steps.append(("modk", 0, 2, k))
            k += 1
        while done < (i + 1) * len(fill) // n:
            steps.append(fill[done])
            done += 1
    steps += [("a_end", l)] + ([("modend", 0, 2)] if l == 0 else []) + [("a_rows", l, tiles[-1]), ("ysplit", l)]

    steps += [("merge", l, m) for m in range(KD)]
    for m in range(KD):
        steps += [("wout", l, m)] + ([("square", l, 1, m - 1)] if m else [])
    steps += [("square", l, 1, KD - 1), ("norm", l, 1), ("residual", l, 1)]
    steps += [("square", l, 2, k) for k in range(KD)] + [("norm", l, 2), ("modulate", l, 2)]

    mods = []
    if l + 1 < DEPTH:
        for r in range(MOD_ROUNDS):
            mods += [[("modk", l + 1, r, k)] for k in range(KD)]
            mods[-1].append(("modend", l + 1, r))
    for j in range(KF):
        steps += [("ffn_in", l, j)] + (mods.pop(0) if mods else [])
    for m in range(KD):
        steps += [("ffn_out", l, m)] + ([("square", l, 3, m - 1)] if m else []) + (mods.pop(0) if mods else [])
    return steps + [("square", l, 3, KD - 1), ("norm", l, 3), ("residual", l, 3)]


def blocks_of(step):
    s, l, a = step[0], step[1], step[2:]

    def gate(m, n):
        return [("w_in", k, IN_TILE["gt"] + n * KD + m) for k in range(KD)]

    if s == "proj":
        return [("w_in", k, IN_TILE[a[0]] + a[1]) for k in range(KD)]
    if s == "gate_store":
        return gate(*a)
    if s == "merge":
        out = []
        for n in range(N_BRANCH):
            if a[0] * N_BRANCH + n >= N_STORED[l]:
                out += gate(a[0], n)
            out += [("w_branch", n * KC + k, a[0]) for k in range(KC)]
        return out
    if s == "wout":
        return [("w_out", k, a[0]) for k in range(KD)]
    if s == "ffn_in":
        return [("w_ffn_in", k, a[0] + half * KF) for half in range(2) for k in range(KD)]
    if s == "ffn_out":
        return [("w_ffn_out", k, a[0]) for k in range(KF)]
    return []


def block_order(l):
    return [b for step in plan_layer(l) for b in blocks_of(step)]


N_GRAN = len(block_order(0)) // 8


class Done:

    def __init__(self, sem, known):
        self.sem, self.known, self.marks, self.count = sem, known, {}, 0

    def mark(self, *keys):
        self.count += 1
        for key in keys:
            self.marks[key] = self.count
        return 1

    def after(self, *key):
        return self.known[key] if self.known else 1


def lam_init(l):
    return 0.8 - 0.6 * math.exp(-0.3 * l)


def program(nc, io, known):
    with ExitStack() as ctx:
        def sem(name):
            return ctx.enter_context(nc.semaphore(name))

        def sb(name, shape, dt=F32):
            return ctx.enter_context(nc.sbuf_tensor(name, shape, dt))

        xT = sb("xT", [P, KD, T])
        h_base = -(-nc.sbuf_base // 32) * 32
        h_hi = sb("h_hi", [P, KD, T], F32R)
        h_lo = sb("h_lo", [P, KD, T], F32R)
        raw = sb("raw", [P, RAW, 8 * P])
        w_hi = sb("w_hi", [P, SPLIT, 8, P], F32R)
        w_lo = sb("w_lo", [P, SPLIT, 8, P], F32R)
        modraw = sb("modraw", [P, MOD_COLS])
        mrow = sb("mrow", [P, T])
        vec = sb("vec", [P, DEPTH, V_N])
        cos, sin = sb("cos", [P, SEQ]), sb("sin", [P, SEQ])
        ident, identb = sb("ident", [P, P]), sb("identb", [P, P], BF16)
        ones = sb("ones", [P, P])
        mask = sb("mask", [P, 2, SEQ], BF16)
        cT, cs = sb("cT", [P, KD, 2]), sb("cs", [P, KD, 32])
        modv = sb("modv", [P, DEPTH, 6 * KD, 2])
        gain = sb("gain", [P, DEPTH, 4, KD, 2])
        small = sb("small", [P, 64])
        kdec = sb("kdec", [P, 3, 8])
        hb = sb("hb", [P, 16])
        nlam, gsub = sb("nlam", [P, DEPTH, 2]), sb("gsub", [P, 1])
        nsink = sb("nsink", [P, 8])
        sm = sb("sm", [P, 8, 8])
        bss, bst = sb("bss", [P, 4, 4]), sb("bst", [P, 2, 16])
        rt = sb("rt", [P, 2, 4])

        base = -(-nc.sbuf_base // 32) * 32
        sb("arena", [P, 104 * 256])

        def at(name, kib, shape, dt=F32):
            return nc.alloc_sbuf_tensor_at(name, shape, dt, offset=base + int(kib * 1024))

        q_a, q_b = at("q_a", 0, [P, 4, T]), at("q_b", 8, [P, 4, T])
        k_a, k_b = at("k_a", 16, [P, 1, T]), at("k_b", 20, [P, 4, T])
        k_sw = at("k_sw", 18, [P, 1, T])
        vv = at("vv", 28, [P, 4, 5 * P])
        y_c = at("y_c", 38, [P, 4, T])
        cu = at("cu", 46, [P, 4, 2, CTX + 4])
        uu = at("uu", 54.25, [P, 4, T])
        l_r, l_i = at("l_r", 62.25, [P, 2, T]), at("l_i", 66.25, [P, 2, T])
        l_a, l_q = at("l_a", 70.25, [P, 2, T]), at("l_q", 74.25, [P, 2, T])
        gst = at("gst", 46, [P, 18, CTX])
        yrow, yrow_a = at("yrow", 64, [P, 4, C_W]), at("yrow_a", 72, [P, 2, C_W])
        pt = at("pt", 76, [P, 2, 4, P])
        pp, ww = at("pp", 80, [P, 4, T]), at("ww", 88, [P, 2, T])
        rope, osq = at("rope", 92, [P, 2, SEQ]), at("osq", 94, [P, P])
        lruw = at("lruw", 96, [P, 16, P])
        yh = [at(f"yh{n}", a, [P, KC, T], F32R) for n, a in enumerate((16, 64, 80))]
        yl = [at(f"yl{n}", a, [P, KC, T], F32R) for n, a in enumerate((24, 72, 88))]
        tg, mixt = at("tg", 32, [P, 2, T]), at("mixt", 36, [P, T])
        mixu = mrow
        mx_hi = [at(f"mx_hi{m}", 2 * m, [P, T], F32R) for m in range(KD)]
        mx_lo = [at(f"mx_lo{m}", a, [P, T], F32R) for m, a in enumerate((38, 40, 42, 44, 96, 98, 100, 102))]
        f_hi = [at(f"f_hi{j}", 2 * j, [P, T], F32R) for j in range(KF)]
        f_lo = [at(f"f_lo{j}", 44 + 2 * j, [P, T], F32R) for j in range(KF)]
        sg, hid = at("sg", 88, [P, 2, T]), at("hid", 92, [P, T])
        sq = at("sq", 88, [P, 2, T])
        ht = at("ht", 76, [P, 2, T])
        rstd, diag = at("rstd", 80, [P, T]), at("diag", 82, [P, 4, P])
        mod0 = at("mod0", 0, [P, KD, MOD_COLS])
        maskf, dl, dots = at("maskf", 64, [P, 2, SEQ]), at("dl", 68, [P, DEPTH, 4, HEAD]), at("dots", 70, [P, 4, HEAD])
        fout = nc.alloc_sbuf_tensor_at("fout", [P, KD, T], F32, offset=h_base)
        hh, hl = [h_hi[:, k] for k in range(KD)], [h_lo[:, k] for k in range(KD)]

        acc = ctx.enter_context(nc.psum_tensor("acc", [P, ACC, 512], F32))
        sc = ctx.enter_context(nc.psum_tensor("sc", [P, 3, 512], F32))
        oo = ctx.enter_context(nc.psum_tensor("oo", [P, 512], F32))
        stat = sc[:, 0, :]

        pe_done, act_done, dve_done, pool_done = (
            Done(sem(n), known[n]) for n in ("pe_done", "act_done", "dve_done", "pool_done"))
        raw_loaded = [sem(f"raw_loaded{i}") for i in range(RAW)]
        mod0_loaded = [sem(f"mod0_loaded{k}") for k in range(KD)]
        consts_loaded, x_loaded, lru_loaded, mod_loaded, stored = (
            sem("consts_loaded"), sem("x_loaded"), sem("lru_loaded"), sem("mod_loaded"), sem("stored"))

        def c0(l):
            return 0 if l == 0 else CTX

        def streams(l):
            return [(0, 0), (1, CTX)] if l == 0 else [(1, CTX)]

        def qtiles(l):
            return [0, 1, 2, 3] if l == 0 else [2, 3]

        plan = [step for l in range(DEPTH) for step in plan_layer(l)]
        mods = [step[1:] for step in plan if step[0] == "modk"][KD:]
        rounds = [step[1:] for step in plan if step[0] == "modend"]

        items = []
        for step in plan:
            s, l, a = step[0], step[1], step[2:]
            if s == "proj":
                items.append((("proj", l) + a, KD, "A"))
            elif s == "gate_store":
                items.append((("mgate", l) + a, KD, "A"))
            elif s == "lru":
                items += [(("gate", l, a[0], d, g), 0, "A") for d in range(2) for g in range(2)]
            elif s == "norm":
                items.append((("spread", l, a[0]), 0, "A"))
            elif s == "modend":
                items.append((("modT", l, a[0]), 0, "D"))
            elif s == "b":
                items += ([(("pv_b", l, a[0] - 1), 0, "A")] if a[0] else []) + [(("pt_b", l, a[0]), 0, "A")]
            elif s == "b_end":
                items.append((("pv_b", l, len(qtiles(l)) * B_HEADS - 1), 0, "A"))
            elif s == "b_rows":
                items += [(("yt_b", l, t), 0, "A") for t in qtiles(l)]
            elif s == "a":
                items += [(("pt_a", l, a[0]), 0, "A")] + ([(("pv_a", l, a[0] - 1), 0, "D")] if a[0] else [])
            elif s == "a_end":
                items.append((("pv_a", l, len(qtiles(l)) * A_HEADS - 1), 0, "D"))
            elif s == "a_rows":
                items.append((("yt_a", l, a[0]), 0, "A"))
            elif s == "merge":
                for n in range(N_BRANCH):
                    if a[0] * N_BRANCH + n >= N_STORED[l]:
                        items.append((("mgate", l, a[0], n), KD, "A"))
                    items.append((("mbranch", l, a[0], n), KC, "D"))
            elif s in ("wout", "ffn_out"):
                items.append(((s, l, a[0]), KD if s == "wout" else KF, "A"))
            elif s == "ffn_in":
                items += [(("fgate", l, a[0]), KD, "A"), (("fup", l, a[0]), KD, "D")]
        order = [key for key, n, by in items]
        info = {key: (n, by) for key, n, by in items}
        slot_of = {key: i for i, key in enumerate(order)}
        blocks_end, total = {}, 0
        for key in order:
            total += info[key][0]
            blocks_end[key] = total
        assert total == DEPTH * N_GRAN * 8

        def bank(key):
            return acc[:, slot_of[key] % ACC, :]

        def wait_raw(eng, g):
            eng.wait_ge(raw_loaded[g % RAW], 16 * (g // RAW + 1))

        def unit_b(l, i):
            h, t = divmod(i, len(qtiles(l)))
            return qtiles(l)[t], h

        def unit_a(l, i):
            return qtiles(l)[i // A_HEADS], i % A_HEADS

        def n_b(l):
            return len(qtiles(l)) * B_HEADS

        def n_a(l):
            return len(qtiles(l)) * A_HEADS

        block = ctx.enter_context(nc.Block())

        consts = (("cT", cT), ("vec", vec), ("ident", ident), ("cos", cos), ("sin", sin), ("maskf", maskf), ("dl", dl))

        @block.sync
        def _(sp):
            sp.dma_start(xT[:], io["xT"]).then_inc(x_loaded, 16)
            for name, t in consts:
                sp.dma_start(t[:], io[name]).then_inc(consts_loaded, 16)
            for k in range(KD):
                sp.dma_start(mod0[:, k, :], io["w_mod"][0, k, :, 0:MOD_COLS]).then_inc(mod0_loaded[k], 16)
            sp.dma_start(lruw[:], io["lruw"][0]).then_inc(lru_loaded, 16)
            for g in range(DEPTH * N_GRAN):
                if g >= RAW:
                    sp.wait_ge(dve_done.sem, dve_done.after("w_lo", g - RAW))
                sp.dma_start(raw[:, g % RAW, :], io["stream"][g]).then_inc(raw_loaded[g % RAW], 16)
                if g == 0:
                    l, r, k = mods[0]
                    sp.dma_start(modraw[:], io["w_mod"][l, k, :, r * MOD_COLS:(r + 1) * MOD_COLS]).then_inc(mod_loaded, 16)
                if g == N_GRAN - 10:
                    sp.wait_ge(pe_done.sem, pe_done.after("wout", 0, KD - 1))
                    sp.dma_start(lruw[:], io["lruw"][1]).then_inc(lru_loaded, 16)
            for k in range(KD):
                sp.wait_ge(dve_done.sem, dve_done.after("x", DEPTH - 1, 3, k))
                sp.dma_start(io["out"][:, k, :], xT[:, k, CTX:T]).then_inc(stored, 16)
            sp.wait_ge(stored, 16 * KD)

        @block.gpsimd
        def _(pool):
            pool.memset(ones[:], 1.0).then_inc(pool_done.sem, pool_done.mark(("ones",)))
            for q in range(DEPTH * N_GRAN):
                wait_raw(pool, q)
                if q >= SPLIT:
                    pool.wait_ge(pe_done.sem, pe_done.after("used", q - SPLIT))
                pool.tensor_scalar(w_hi[:, q % SPLIT].rearrange("p k n -> p (k n)"), raw[:, q % RAW, :], 1.0, 0.0,
                                   ALU.mult, ALU.add).then_inc(pool_done.sem, pool_done.mark(("w_hi", q)))

        @block.tensor
        def _(pe):
            blocks = [0]

            def take(key):
                n = slot_of[key]
                if n >= ACC:
                    last = order[n - ACC]
                    if info[last][1] == "A":
                        pe.wait_ge(act_done.sem, act_done.after("read", last))
                    else:
                        pe.wait_ge(dve_done.sem, dve_done.after("read", last))
                return bank(key)

            def next_block():
                q, k = divmod(blocks[0], 8)
                blocks[0] += 1
                if k == 0:
                    pe.wait_ge(dve_done.sem, dve_done.after("w_lo", q))
                return q, k

            def gemm(key, src_hi, src_lo, cols, ready=None):
                out = take(key)
                n = info[key][0]
                for i in range(n):
                    q, k = next_block()
                    wh, wl = w_hi[:, q % SPLIT, k, :], w_lo[:, q % SPLIT, k, :]
                    if ready:
                        pe.wait_ge(dve_done.sem, dve_done.after(*ready(i)))
                    o = out[:, cols]
                    pe.matmul(o, wh, src_hi[i][:, cols], start=i == 0, stop=False)
                    pe.matmul(o, wh, src_lo[i][:, cols], start=False, stop=False)
                    last = pe.matmul(o, wl, src_hi[i][:, cols], start=False, stop=i == n - 1)
                    names = ([("used", q)] if k == 7 else []) + ([key] if i == n - 1 else [])
                    if names:
                        last.then_inc(pe_done.sem, pe_done.mark(*names))

            def gemm_tokens(key):
                out = take(key).rearrange("p (t n) -> p t n", n=P)
                q, _ = next_block()
                blocks[0] += 7
                for t in range(T // P):
                    tok = slice(t * P, (t + 1) * P)
                    for k in range(KD):
                        wh, wl = w_hi[:, q % SPLIT, k, :], w_lo[:, q % SPLIT, k, :]
                        pe.matmul(out[:, t], h_hi[:, k, tok], wh, start=k == 0, stop=False)
                        pe.matmul(out[:, t], h_lo[:, k, tok], wh, start=False, stop=False)
                        last = pe.matmul(out[:, t], h_hi[:, k, tok], wl, start=False, stop=k == KD - 1)
                last.then_inc(pe_done.sem, pe_done.mark(("used", q), key))

            def modk(l, r, k):
                if k == 0:
                    pe.wait_ge(act_done.sem, act_done.after("silu_c",))
                    if (l, r) != rounds[0]:
                        pe.wait_ge(act_done.sem, act_done.after("mrow", *rounds[rounds.index((l, r)) - 1]))
                if (l, r) == (0, 0):
                    pe.wait_ge(mod0_loaded[k], 16)
                    src = mod0[:, k, :]
                else:
                    pe.wait_ge(mod_loaded, 16 * (mods.index((l, r, k)) + 1))
                    src = modraw
                for j in range(4):
                    last = pe.matmul(oo[32 * j:32 * (j + 1), :], cs[:, k, :], src[:, j * 512:(j + 1) * 512], start=k == 0,
                                     stop=k == KD - 1, tile_position=(0, 32 * j))
                last.then_inc(pe_done.sem, pe_done.mark(("modk", l, r, k)))

            def modend(l, r):
                out = take(("modT", l, r))
                pe.wait_ge(act_done.sem, act_done.after("mrow", l, r))
                for c in range(4):
                    last = pe.transpose(out[:, c * P:(c + 1) * P], mrow[:, c * P:(c + 1) * P], ident[:])
                last.then_inc(pe_done.sem, pe_done.mark(("modT", l, r)))

            def square(l, which, k):
                if k == 0:
                    pe.wait_ge(pool_done.sem, pool_done.after("ones",))
                pe.wait_ge(act_done.sem, act_done.after("square", l, which, k))
                tiles = range(4) if which == 0 else qtiles(l)
                for t in tiles:
                    last = pe.matmul(stat[:, t:t + 1], sq[:, k % 2, t * P:(t + 1) * P], ones[:, 0:1],
                                     start=k == 0 and t == tiles[0], stop=k == KD - 1, skip_group_check=True)
                last.then_inc(pe_done.sem, pe_done.mark(("squared", l, which, k)))

            def norm(l, which):
                key = ("spread", l, which)
                out = take(key)
                for t in range(4) if which == 0 else qtiles(l):
                    pe.wait_ge(dve_done.sem, dve_done.after("diag", l, which, t))
                    last = pe.matmul(out[:, t * P:(t + 1) * P], ones[:], diag[:, t, :], start=True, stop=True)
                last.then_inc(pe_done.sem, pe_done.mark(key))

            def none(*args):
                pass

            def proj(l, kind, t):
                if kind in ("av", "bv"):
                    gemm_tokens(("proj", l, kind, t))
                else:
                    whole = kind in ("cu", "ak", "bk")
                    ready = (lambda i: ("h_lo", l, 0, i)) if (kind, t) == ("cg", 0) else None
                    gemm(("proj", l, kind, t), hh, hl, slice(0 if whole else c0(l), T), ready)

            def lru(l, t):
                pe.wait_ge(lru_loaded, 16 * (l + 1))
                pe.wait_ge(dve_done.sem, dve_done.after("conv", l, t))
                for d in range(2):
                    for g in range(2):
                        key = ("gate", l, t, d, g)
                        pe.matmul(take(key), lruw[:, (d * 2 + g) * KC + t, :], uu[:, t, :], start=True, stop=True)\
                            .then_inc(pe_done.sem, pe_done.mark(key))

            def keys_of(t):
                return T if t >= 2 else CTX

            def scores(key, n, q, kk, t, local):
                if n >= 3:
                    pe.wait_ge(act_done.sem, act_done.after("exp", key[1], n - 3))
                qt = q[:, t * P:(t + 1) * P]
                if local and t >= 2:
                    pe.matmul(sc[:, n % 3, 0:CTX], qt, kk[:, 0:CTX], start=True, stop=True)
                    pe.matmul(sc[:, n % 3, CTX:T], qt, kk[:, CTX:T], start=True, stop=False)
                    last = pe.matmul(sc[:, n % 3, CTX:T], identb[:], mask[:, t - 2, :], start=False, stop=True)
                else:
                    last = pe.matmul(sc[:, n % 3, 0:keys_of(t)], qt, kk[:, 0:keys_of(t)], start=True, stop=True)
                last.then_inc(pe_done.sem, pe_done.mark(key))

            def turn_keys(key, src, t):
                out = take(key)
                nk = keys_of(t) // P
                for j in range(nk):
                    last = pe.transpose(out[:, j * P:(j + 1) * P], src[:, j * P:(j + 1) * P], ident[:])
                last.then_inc(pe_done.sem, pe_done.mark(key))

            def weigh(key, slot, v, t):
                o = take(key)[:, 0:v.stop - v.start]
                nk = keys_of(t) // P
                for j in range(nk):
                    last = pe.matmul(o, pt[:, slot, j, :], vv[:, j, v], start=j == 0, stop=j == nk - 1)
                last.then_inc(pe_done.sem, pe_done.mark(key))

            def score_b(l, i):
                t, h = unit_b(l, i)
                if t == qtiles(l)[0]:
                    for kind in ("bk", "bq"):
                        pe.wait_ge(dve_done.sem, dve_done.after("qk", l, kind, h))
                for m in range(2):
                    half = slice(HEAD * m, HEAD * (m + 1))
                    scores(("s_b", l, 2 * i + m), 2 * i + m, q_b[half, h, :], k_b[half, h, :], t, False)

            def turn_b(l, i):
                pe.wait_ge(dve_done.sem, dve_done.after("w_b", l, i))
                turn_keys(("pt_b", l, i), ww[:, i % 2, :], unit_b(l, i)[0])

            def value_b(l, i):
                t, h = unit_b(l, i)
                if t == qtiles(l)[0]:
                    pe.wait_ge(act_done.sem, act_done.after("v", l, "bv", h))
                pe.wait_ge(act_done.sem, act_done.after("read", ("pt_b", l, i)))
                weigh(("pv_b", l, i), i % 2, slice(P * (h + 1), P * (h + 2)), t)

            def b_start(l):
                score_b(l, 0)

            def b(l, i):
                if i:
                    value_b(l, i - 1)
                if i + 1 < n_b(l):
                    score_b(l, i + 1)
                turn_b(l, i)

            def b_end(l):
                value_b(l, n_b(l) - 1)

            def turn_rows(key, src):
                out = take(key)
                for j in range(4):
                    last = pe.transpose(out[:, j * P:(j + 1) * P], src[:, j * P:(j + 1) * P], ident[:])
                last.then_inc(pe_done.sem, pe_done.mark(key))

            def b_rows(l):
                for j, t in enumerate(qtiles(l)):
                    pe.wait_ge(dve_done.sem, dve_done.after("yrow_b", l, t))
                    turn_rows(("yt_b", l, t), yrow[:, j, :])

            def score_a(l, i):
                t, h = unit_a(l, i)
                if i < A_HEADS and h % 2 == 0:
                    pe.wait_ge(dve_done.sem, dve_done.after("qk", l, "aq", h // 2))
                half = slice(HEAD * (h % 2), HEAD * (h % 2 + 1))
                kk = k_a if h // 4 == h % 2 else k_sw
                scores(("s_a", l, i), 2 * n_b(l) + i, q_a[half, h // 2, :], kk[half, 0, :], t, True)

            def turn_a(l, i):
                pe.wait_ge(act_done.sem, act_done.after("exp", l, 2 * n_b(l) + i))
                turn_keys(("pt_a", l, i), pp[:, i % 4, :], unit_a(l, i)[0])

            def value_a(l, i):
                t, h = unit_a(l, i)
                pe.wait_ge(act_done.sem, act_done.after("read", ("pt_a", l, i)))
                weigh(("pv_a", l, i), i % 2, slice(HEAD * (h // 4), HEAD * (h // 4 + 1)), t)

            def a_start(l):
                pe.wait_ge(act_done.sem, act_done.after("k_sw", l))
                pe.wait_ge(act_done.sem, act_done.after("v", l, "av", 0))
                score_a(l, 0)
                score_a(l, 1)

            def a(l, i):
                if i + 2 < n_a(l):
                    score_a(l, i + 2)
                turn_a(l, i)
                if i:
                    value_a(l, i - 1)

            def a_end(l):
                value_a(l, n_a(l) - 1)

            def a_rows(l, t):
                pe.wait_ge(dve_done.sem, dve_done.after("o_a", l, t, A_HEADS - 1))
                turn_rows(("yt_a", l, t), yrow_a[:, t % 2, :])

            def gate_store(l, m, n):
                gemm(("mgate", l, m, n), hh, hl, slice(c0(l), T))

            def merge(l, m):
                cols = slice(c0(l), T)
                for n in range(N_BRANCH):
                    if m * N_BRANCH + n >= N_STORED[l]:
                        gemm(("mgate", l, m, n), hh, hl, cols)
                    ready = (lambda i: ("y_lo", l, n, i)) if m == 0 else None
                    gemm(("mbranch", l, m, n), [yh[n][:, k] for k in range(KC)], [yl[n][:, k] for k in range(KC)],
                         cols, ready)

            def wout(l, m):
                gemm(("wout", l, m), mx_hi, mx_lo, slice(c0(l), T), (lambda i: ("mx_lo", l, i)) if m == 0 else None)

            def ffn_in(l, j):
                gemm(("fgate", l, j), hh, hl, slice(c0(l), T), (lambda i: ("h_lo", l, 2, i)) if j == 0 else None)
                gemm(("fup", l, j), hh, hl, slice(c0(l), T))

            def ffn_out(l, m):
                gemm(("ffn_out", l, m), f_hi, f_lo, slice(c0(l), T), (lambda i: ("f_lo", l, i)) if m == 0 else None)

            pe.wait_ge(consts_loaded, 16 * len(consts))
            pe.wait_ge(dve_done.sem, dve_done.after("mask",))
            steps = dict(square=square, norm=norm, modk=modk, modend=modend, modulate=none, proj=proj, lru=lru,
                         b_start=b_start, b=b, b_end=b_end, b_rows=b_rows, a_start=a_start, a=a, a_end=a_end,
                         a_rows=a_rows, gate_store=gate_store, ysplit=none, merge=merge, wout=wout, ffn_in=ffn_in,
                         ffn_out=ffn_out, residual=none)
            for step, *args in plan:
                steps[step](*args)

        @block.scalar
        def _(act):
            def finish(ins, *names):
                ins.then_inc(act_done.sem, act_done.mark(*names))

            def own():
                act.wait_ge(act_done.sem, act_done.count)

            def modk(l, r, k):
                u = (l, r, k)
                if u in mods and mods.index(u) + 1 < len(mods):
                    nl, nr, nk = mods[mods.index(u) + 1]
                    act.wait_ge(pe_done.sem, pe_done.after("modk", l, r, k))
                    act.dma_start(modraw[:], io["w_mod"][nl, nk, :, nr * MOD_COLS:(nr + 1) * MOD_COLS])\
                       .then_inc(mod_loaded, 16)

            def modend(l, r):
                act.wait_ge(pe_done.sem, pe_done.after("modk", l, r, KD - 1))
                if (l, r) != rounds[0]:
                    before = rounds[rounds.index((l, r)) - 1]
                    act.wait_ge(pe_done.sem, pe_done.after("modT", *before))
                    if l:
                        act.wait_ge(dve_done.sem, dve_done.after("mixt", l - 1, KD - 1))
                finish(act.activation(mrow[:], oo[:], ACT.Copy), ("mrow", l, r))

            def start():
                finish(act.activation(cs[:, :, 0:2], cT[:], ACT.Silu), ("silu_c",))
                act.wait_ge(dve_done.sem, dve_done.after("dots",))
                finish(act.activation(small[:, 56:60], small[:, 16:20], ACT.Exp), ("exp_dots",))

            def exp_lambda(l):
                if l:
                    act.wait_ge(dve_done.sem, dve_done.after("kdec", l - 1))
                finish(act.activation(small[:, 0:8], vec[:, l, V_LAM:V_LAM + 8], ACT.Abs))
                own()
                finish(act.activation(small[:, 8:16], small[:, 0:8], ACT.Exp, scale=-1.0), ("exp_lam", l))

            def square(l, which, k):
                cols = slice(0 if which == 0 else c0(l), T)
                n = k if k >= 2 else None
                if n is not None:
                    act.wait_ge(pe_done.sem, pe_done.after("squared", l, which, k - 2))
                if which in (0, 2):
                    if which == 0 and l == 0:
                        act.wait_ge(x_loaded, 16)
                    else:
                        act.wait_ge(dve_done.sem, dve_done.after("x", l if which else l - 1, 1 if which else 3, k))
                    src = xT[:, k, cols]
                else:
                    act.wait_ge(act_done.sem, act_done.after("read", ({1: "wout", 3: "ffn_out"}[which], l, k)))
                    src = fout[:, k, cols]
                finish(act.activation(sq[:, k % 2, cols], src, ACT.Square), ("square", l, which, k))

            def norm(l, which):
                tiles = slice(0, 4) if which == 0 or l == 0 else slice(2, 4)
                cols = slice(0 if which == 0 else c0(l), T)
                act.wait_ge(pe_done.sem, pe_done.after("squared", l, which, KD - 1))
                finish(act.activation(rt[:, 0, tiles], stat[:, tiles], ACT.Sqrt, bias=EPS,
                                      scale=1.0 / D), ("read", ("stat", l, which)))
                act.wait_ge(pe_done.sem, pe_done.after("spread", l, which))
                finish(act.activation(rstd[:, cols], bank(("spread", l, which))[:, cols], ACT.Copy),
                       ("read", ("spread", l, which)))

            def modulate(l, which):
                if which == 0:
                    exp_lambda(l)
                for k in range(KD):
                    for s, a in ([(0, 0), (1, CTX)] if which == 0 else streams(l)):
                        act.wait_ge(dve_done.sem, dve_done.after("ht", l, which, k, s))
                        finish(act.activation(h_hi[:, k, a:a + CTX], ht[:, k % 2, a:a + CTX], ACT.Identity,
                                              bias=modv[:, l, (0 if which == 0 else 3 * KD) + k, s:s + 1]),
                               ("h_hi", l, which, k, s))

            def proj(l, kind, t):
                key = ("proj", l, kind, t)
                b = bank(key)
                act.wait_ge(pe_done.sem, pe_done.after(*key))
                if kind == "cu":
                    act.wait_ge(dve_done.sem, dve_done.after("pad", l))
                    finish(act.activation(cu[:, t, :, 2:2 + CTX], b.rearrange("p (s n) -> p s n", s=2), ACT.Copy),
                           ("read", key))
                elif kind in ("av", "bv"):
                    col = 0 if kind == "av" else P * (t + 1)
                    finish(act.activation(vv[:, :, col:col + P], b.rearrange("p (t n) -> p t n", n=P), ACT.Copy),
                           ("read", key), ("v", l, kind, t))
                elif kind == "cg":
                    finish(act.activation(y_c[:, t, c0(l):T], b[:, c0(l):T], ACT.Gelu_apprx_tanh), ("read", key))
                else:
                    dst = {"aq": q_a, "ak": k_a, "bq": q_b, "bk": k_b}[kind]
                    cols = slice(0 if kind in ("ak", "bk") else c0(l), T)
                    finish(act.activation(dst[:, t, cols], b[:, cols], ACT.Copy), ("read", key))
                    if kind == "ak":
                        act.wait_ge(dve_done.sem, dve_done.after("qk", l, kind, t))
                        own()
                        finish(act.activation(k_sw[0:HEAD, 0, :], k_a[HEAD:P, 0, :], ACT.Copy))
                        finish(act.activation(k_sw[HEAD:P, 0, :], k_a[0:HEAD, 0, :], ACT.Copy), ("k_sw", l))

            def lru(l, t):
                for d in range(2):
                    kd = kdec[:, 0, d * 4 + t:d * 4 + t + 1]
                    kn = kdec[:, 1, d * 4 + t:d * 4 + t + 1]
                    if d == 0:
                        act.wait_ge(dve_done.sem, dve_done.after("kdec", l))
                        if t:
                            act.wait_ge(dve_done.sem, dve_done.after("hsum", l, t - 1))
                    for g, dst in ((0, l_r), (1, l_i)):
                        key = ("gate", l, t, d, g)
                        act.wait_ge(pe_done.sem, pe_done.after(*key))
                        j = (d * 2 + g) * KC + t
                        finish(act.activation(dst[:, d], bank(key), ACT.Tanh, bias=hb[:, j:j + 1], scale=0.5),
                               ("read", key), ("l_gate", l, t, d, g))
                    act.wait_ge(act_done.sem, act_done.after("l_gate", l, t, d, 0))
                    finish(act.activation(l_a[:, d], l_r[:, d], ACT.Exp, bias=kd, scale=kd), ("l_a", l, t, d))
                    own()
                    finish(act.activation(l_r[:, d], l_r[:, d], ACT.Tanh, bias=kn, scale=kn), ("l_th", l, t, d))
                for d in range(2):
                    act.wait_ge(dve_done.sem, dve_done.after("l_q", l, t, d))
                    finish(act.activation(l_q[:, d], l_q[:, d], ACT.Sqrt, scale=0.25), ("l_sqrt", l, t, d))

            def nk(t):
                return T if t >= 2 else CTX

            def exp(l, n, ring, t, key):
                act.wait_ge(pe_done.sem, pe_done.after(*key))
                act.wait_ge(dve_done.sem, dve_done.after("nmax", l, n))
                finish(act.activation(pp[:, ring, 0:nk(t)], sc[:, n % 3, 0:nk(t)], ACT.Exp, bias=sm[:, n % 8, 1:2],
                                      scale=SCALE, accum_out=sm[:, n % 8, 2:3]), ("exp", l, n))

            def copy_pt(key, slot, t):
                act.wait_ge(pe_done.sem, pe_done.after(*key))
                finish(act.activation(pt[:, slot, 0:nk(t) // P, :].rearrange("p j n -> p (j n)"), bank(key)[:, 0:nk(t)], ACT.Copy),
                       ("read", key))

            def score_b(l, i):
                t = unit_b(l, i)[0]
                for m in range(2):
                    n = 2 * i + m
                    if i >= 2:
                        act.wait_ge(dve_done.sem, dve_done.after("w_b", l, i - 2))
                    exp(l, n, n % 4, t, ("s_b", l, n))

            def value_b(l, i):
                t, h = unit_b(l, i)
                j = qtiles(l).index(t)
                act.wait_ge(pe_done.sem, pe_done.after("pv_b", l, i))
                o = bank(("pv_b", l, i))[:, 0:P]
                finish(act.activation(yrow[:, j, h * P:(h + 1) * P], o, ACT.Copy))
                own()
                finish(act.activation(osq[:], o, ACT.Square, accum_out=bss[:, j, h:h + 1]), ("read", ("pv_b", l, i)))

            def turn_b(l, i):
                if i >= 2:
                    act.wait_ge(pe_done.sem, pe_done.after("pv_b", l, i - 2))
                copy_pt(("pt_b", l, i), i % 2, unit_b(l, i)[0])

            def b_start(l):
                score_b(l, 0)

            def b(l, i):
                if i:
                    value_b(l, i - 1)
                turn_b(l, i)
                if i + 1 < n_b(l):
                    score_b(l, i + 1)

            def b_end(l):
                value_b(l, n_b(l) - 1)
                own()
                n = len(qtiles(l)) * B_HEADS
                finish(act.activation(bst[:, 0, 0:n], bss[:].rearrange("p a b -> p (a b)")[:, 0:n], ACT.Sqrt, bias=EPS,
                                      scale=1.0 / B_VDIM), ("bst", l))

            def rows(name, dst, l, t, scale):
                key = (name, l, t)
                act.wait_ge(pe_done.sem, pe_done.after(*key))
                finish(act.activation(dst[:, :, t * P:(t + 1) * P], bank(key).rearrange("p (j n) -> p j n", n=P),
                                      ACT.Copy, scale=scale), ("read", key))

            def b_rows(l):
                for t in qtiles(l):
                    rows("yt_b", q_b, l, t, gsub[:, 0:1])

            def score_a(l, i):
                t, h = unit_a(l, i)
                n = 2 * n_b(l) + i
                if i >= 4:
                    act.wait_ge(pe_done.sem, pe_done.after("pt_a", l, i - 4))
                else:
                    act.wait_ge(dve_done.sem, dve_done.after("w_b", l, n_b(l) - 1))
                exp(l, n, i % 4, t, ("s_a", l, i))
                finish(act.activation(sm[:, n % 8, 3:4], vec[:, l, V_SINK + h:V_SINK + h + 1], ACT.Exp,
                                      bias=sm[:, n % 8, 1:2]), ("exp_sink", l, n))

            def turn_a(l, i):
                if i >= 2:
                    act.wait_ge(pe_done.sem, pe_done.after("pv_a", l, i - 2))
                else:
                    act.wait_ge(pe_done.sem, pe_done.after("pv_b", l, n_b(l) - 1))
                copy_pt(("pt_a", l, i), i % 2, unit_a(l, i)[0])

            def a_start(l):
                score_a(l, 0)
                score_a(l, 1)

            def a(l, i):
                turn_a(l, i)
                if i + 2 < n_a(l):
                    score_a(l, i + 2)

            def a_rows(l, t):
                rows("yt_a", q_a, l, t, 1.0)

            def gate_store(l, m, n):
                key = ("mgate", l, m, n)
                u, per = m * N_BRANCH + n, (T - c0(l)) // CTX
                act.wait_ge(pe_done.sem, pe_done.after(*key))
                if (m, n) == (0, 0):
                    act.wait_ge(dve_done.sem, dve_done.after("y_c", l, KC - 1))
                finish(act.activation(gst[:, u * per:(u + 1) * per].rearrange("p a n -> p (a n)"), bank(key)[:, c0(l):T],
                                      ACT.Tanh, scale=0.5), ("read", key), ("tg", l, m, n))

            def ysplit(l):
                cols = slice(c0(l), T)
                act.wait_ge(pe_done.sem, pe_done.after("yt_a", l, qtiles(l)[-1]))
                own()
                for n in range(N_BRANCH):
                    for k in range(KC):
                        if n == 2:
                            act.wait_ge(dve_done.sem, dve_done.after("y_c", l, k))
                        finish(act.activation(yh[n][:, k, cols], (q_a, q_b, y_c)[n][:, k, cols], ACT.Copy), ("y_hi", l, n, k))

            def merge(l, m):
                cols = slice(c0(l), T)
                for n in range(N_BRANCH):
                    u = m * N_BRANCH + n
                    if u < N_STORED[l]:
                        continue
                    key = ("mgate", l, m, n)
                    act.wait_ge(pe_done.sem, pe_done.after(*key))
                    act.wait_ge(dve_done.sem, dve_done.after("read", ("mbranch", l, *divmod(u - 2, N_BRANCH))))
                    finish(act.activation(tg[:, u % 2, cols], bank(key)[:, cols], ACT.Tanh, scale=0.5),
                           ("read", key), ("tg", l, m, n))
                act.wait_ge(dve_done.sem, dve_done.after("mixt", l, m))
                finish(act.activation(mx_hi[m][:, cols], mixt[:, cols], ACT.Copy, scale=0.5), ("mx_hi", l, m))

            def wout(l, m):
                key = ("wout", l, m)
                act.wait_ge(pe_done.sem, pe_done.after(*key))
                finish(act.activation(fout[:, m, c0(l):T], bank(key)[:, c0(l):T], ACT.Copy), ("read", key))

            def ffn_in(l, j):
                key, cols = ("fgate", l, j), slice(c0(l), T)
                act.wait_ge(pe_done.sem, pe_done.after(*key))
                if j >= 2:
                    act.wait_ge(dve_done.sem, dve_done.after("read", ("fup", l, j - 2)))
                finish(act.activation(sg[:, j % 2, cols], bank(key)[:, cols], ACT.Silu), ("read", key))
                act.wait_ge(dve_done.sem, dve_done.after("read", ("fup", l, j)))
                finish(act.activation(f_hi[j][:, cols], hid[:, cols], ACT.Copy), ("f_hi", l, j))

            def ffn_out(l, m):
                key = ("ffn_out", l, m)
                act.wait_ge(pe_done.sem, pe_done.after(*key))
                finish(act.activation(fout[:, m, c0(l):T], bank(key)[:, c0(l):T], ACT.Copy), ("read", key))

            def none(*args):
                pass

            act.wait_ge(consts_loaded, 16 * len(consts))
            act.wait_ge(dve_done.sem, dve_done.after("cs_zero",))
            start()
            steps = dict(square=square, norm=norm, modk=modk, modend=modend, modulate=modulate, proj=proj, lru=lru,
                         b_start=b_start, b=b, b_end=b_end, b_rows=b_rows, a_start=a_start, a=a, a_end=none,
                         a_rows=a_rows, gate_store=gate_store, ysplit=ysplit, merge=merge, wout=wout, ffn_in=ffn_in,
                         ffn_out=ffn_out, residual=none)
            for step, *args in plan:
                steps[step](*args)

        @block.vector
        def _(dve):
            split = [0]

            def finish(ins, *names):
                ins.then_inc(dve_done.sem, dve_done.mark(*names))

            def own():
                dve.wait_ge(dve_done.sem, dve_done.count)

            def splits(key):
                n = blocks_end[key]
                before = n - info[key][0]
                limit = min(max(before // 8 + SPLIT, -(-n // 8)), DEPTH * N_GRAN)
                while split[0] < limit:
                    q = split[0]
                    dve.wait_ge(pool_done.sem, pool_done.after("w_hi", q))
                    finish(dve.tensor_tensor(w_lo[:, q % SPLIT].rearrange("p k n -> p (k n)"), raw[:, q % RAW, :],
                                             w_hi[:, q % SPLIT].bitcast(F32).rearrange("p k n -> p (k n)"),
                                             ALU.subtract), ("w_lo", q))
                    split[0] += 1

            def start():
                finish(dve.tensor_tensor(dots[:], dl[:].rearrange("p l (a b) n -> p (l a) b n", b=2)[:, :, 0, :],
                                         dl[:].rearrange("p l (a b) n -> p (l a) b n", b=2)[:, :, 1, :], ALU.mult))
                own()
                finish(dve.tensor_reduce(small[:, 16:20], dots[:], AX, ALU.add), ("dots",))
                dve.wait_ge(act_done.sem, act_done.after("exp_dots",))
                for l in range(DEPTH):
                    e = small[:, 56 + 2 * l:58 + 2 * l]
                    finish(dve.tensor_tensor(nlam[:, l, 0:1], e[:, 1:2], e[:, 0:1], ALU.subtract))
                own()
                for l in range(DEPTH):
                    finish(dve.tensor_scalar(nlam[:, l, 1:2], nlam[:, l, 0:1], -lam_init(l), None, ALU.add), ("nlam", l))

            def modend(l, r):
                v, key = vec[:, l], ("modT", l, r)
                dve.wait_ge(pe_done.sem, pe_done.after(*key))
                turned = bank(key).rearrange("p (c j s) -> p j c s", c=4, j=4)[:, :, :, 0:2]
                finish(dve.tensor_tensor(modv[:, l, 16 * r:16 * (r + 1), :].rearrange("p (j c) s -> p j c s", j=4), turned,
                                         v[:, V_BMOD + 32 * r:V_BMOD + 32 * (r + 1)].rearrange(
                                             "p (j c s) -> p j c s", j=4, c=4), ALU.add), ("read", key))
                own()
                for i, (chunk, add) in enumerate(((1, 1.0), (2, 0.0), (4, 1.0), (5, 0.0))):
                    if chunk // 2 == r:
                        finish(dve.scalar_tensor_tensor(gain[:, l, i].rearrange("p k s -> p (k s)"),
                                                        modv[:, l, chunk * KD:(chunk + 1) * KD, :].rearrange("p k s -> p (k s)"),
                                                        add, v[:, V_G + 16 * i:V_G + 16 * (i + 1)], ALU.add, ALU.mult),
                               ("gain", l, i))
                own()

            def decay(l):
                v = vec[:, l]
                finish(dve.tensor_scalar(gsub[:], v[:, V_SUB:V_SUB + 1], 1.0 - lam_init(l), None, ALU.mult), ("gsub", l))
                finish(dve.tensor_scalar(nsink[:], v[:, V_SINK:V_SINK + 8], -1.0, None, ALU.mult))
                finish(dve.tensor_scalar(hb[:], v[:, V_LB:V_LB + 16], 0.5, None, ALU.mult))
                dve.wait_ge(act_done.sem, act_done.after("exp_lam", l))
                y, z, z2, p = small[:, 8:16], small[:, 24:32], small[:, 32:40], small[:, 40:48]
                w = small[:, 48:56]
                finish(dve.tensor_scalar(w, y, 2.0, None, ALU.add))
                own()
                finish(dve.reciprocal(p, w))
                own()
                finish(dve.tensor_tensor(z, y, p, ALU.mult))
                own()
                finish(dve.tensor_tensor(z2, z, z, ALU.mult))
                own()
                finish(dve.tensor_scalar(p, z2, 1.0 / 17, None, ALU.mult))
                for c in (15, 13, 11, 9, 7, 5, 3):
                    own()
                    finish(dve.scalar_tensor_tensor(p, p, 1.0 / c, z2, ALU.add, ALU.mult))
                own()
                finish(dve.scalar_tensor_tensor(p, p, 1.0, z, ALU.add, ALU.mult))
                finish(dve.tensor_scalar(w, v[:, V_LAM:V_LAM + 8], -1.0, 0.0, ALU.mult, ALU.max))
                own()
                finish(dve.scalar_tensor_tensor(z, p, 2.0, w, ALU.mult, ALU.add))
                own()
                finish(dve.tensor_scalar(kdec[:, 0, :], z, -4.0, None, ALU.mult))
                finish(dve.tensor_scalar(kdec[:, 1, :], z, 4.0, None, ALU.mult), ("kdec", l))

            def norm(l, which):
                tiles = range(4) if which == 0 else qtiles(l)
                dve.wait_ge(act_done.sem, act_done.after("read", ("stat", l, which)))
                finish(dve.reciprocal(rt[:, 1, tiles[0]:4], rt[:, 0, tiles[0]:4]))
                own()
                for t in tiles:
                    finish(dve.tensor_scalar(diag[:, t, :], ident[:], rt[:, 1, t:t + 1], None, ALU.mult),
                           ("diag", l, which, t))

            def modulate(l, which):
                def low(k):
                    for s, a in sts:
                        dve.wait_ge(act_done.sem, act_done.after("h_hi", l, which, k, s))
                        finish(dve.scalar_tensor_tensor(h_lo[:, k, a:a + CTX], ht[:, k % 2, a:a + CTX],
                                                        modv[:, l, (0 if which == 0 else 3 * KD) + k, s:s + 1],
                                                        h_hi[:, k, a:a + CTX].bitcast(F32), ALU.add, ALU.subtract),
                               ("h_lo", l, which, k))

                sts = [(0, 0), (1, CTX)] if which == 0 else streams(l)
                dve.wait_ge(act_done.sem, act_done.after("read", ("spread", l, which)))
                for k in range(KD):
                    if k >= 2:
                        dve.wait_ge(dve_done.sem, dve_done.after("h_lo", l, which, k - 2))
                    for s, a in sts:
                        finish(dve.scalar_tensor_tensor(ht[:, k % 2, a:a + CTX], xT[:, k, a:a + CTX],
                                                        gain[:, l, which, k, s:s + 1], rstd[:, a:a + CTX], ALU.mult, ALU.mult),
                               ("ht", l, which, k, s))
                    if k:
                        low(k - 1)
                low(KD - 1)
                if which == 0:
                    decay(l)

            def proj(l, kind, t):
                key = ("proj", l, kind, t)
                if (kind, t) == ("cu", 0):
                    finish(dve.memset(cu[:, :, :, 0:2], 0.0))
                    finish(dve.memset(cu[:, :, :, 2 + CTX:4 + CTX], 0.0), ("pad", l))
                splits(key)
                b = bank(key)
                if kind == "cu":
                    dve.wait_ge(act_done.sem, act_done.after("read", key))
                    u = uu[:, t].rearrange("p (s n) -> p s n", s=2)
                    tap = lambda i: vec[:, l, V_CW + i * KC + t:V_CW + i * KC + t + 1]
                    own()
                    finish(dve.tensor_scalar(u, cu[:, t, :, 0:CTX], tap(0), vec[:, l, V_CB + t:V_CB + t + 1], ALU.mult, ALU.add))
                    for i in range(1, CONV_W):
                        own()
                        finish(dve.scalar_tensor_tensor(u, cu[:, t, :, i:i + CTX], tap(i), u, ALU.mult, ALU.add),
                               ("conv", l, t))
                elif kind in ("aq", "ak", "bq", "bk"):
                    dst = {"aq": q_a, "ak": k_a, "bq": q_b, "bk": k_b}[kind][:, t, CTX:T]
                    dve.wait_ge(act_done.sem, act_done.after("read", key))
                    own()
                    finish(dve.stream_shuffle(rope[:, 0, :], dst, [i ^ 16 for i in range(32)]))
                    own()
                    finish(dve.tensor_tensor(dst, dst, cos[:], ALU.mult))
                    finish(dve.tensor_tensor(rope[:, 1, :], rope[:, 0, :], sin[:], ALU.mult))
                    own()
                    finish(dve.tensor_tensor(dst, dst, rope[:, 1, :], ALU.add), ("qk", l, kind, t))

            def lru(l, t):
                for d in range(2):
                    dve.wait_ge(act_done.sem, act_done.after("l_a", l, t, d))
                    finish(dve.tensor_tensor(l_q[:, d], l_a[:, d], l_a[:, d], ALU.mult))
                    dve.wait_ge(act_done.sem, act_done.after("l_gate", l, t, d, 1))
                    finish(dve.scalar_tensor_tensor(l_i[:, d], l_i[:, d], 1.0, uu[:, t], ALU.add, ALU.mult))
                    dve.wait_ge(act_done.sem, act_done.after("l_th", l, t, d))
                    own()
                    finish(dve.scalar_tensor_tensor(l_q[:, d], l_q[:, d], 1.0, l_r[:, d], ALU.add, ALU.mult),
                           ("l_q", l, t, d))
                for d in range(2):
                    dve.wait_ge(act_done.sem, act_done.after("l_sqrt", l, t, d))
                    finish(dve.tensor_tensor(l_i[:, d], l_i[:, d], l_q[:, d], ALU.mult))
                    own()
                    if d == 0:
                        finish(dve.tensor_tensor_scan(l_r[:, 0], l_a[:, 0], l_i[:, 0], 0.0, ALU.mult, ALU.add))
                    else:
                        finish(dve.tensor_tensor_scan(l_r[:, 1, CTX - 1::-1], l_a[:, 1, CTX - 1::-1],
                                                      l_i[:, 1, CTX - 1::-1], 0.0, ALU.mult, ALU.add))
                        own()
                        finish(dve.tensor_tensor_scan(l_r[:, 1, T - 1:CTX - 1:-1], l_a[:, 1, T - 1:CTX - 1:-1],
                                                      l_i[:, 1, T - 1:CTX - 1:-1], l_r[:, 1, 0:1], ALU.mult, ALU.add))
                own()
                cols = slice(c0(l), T)
                finish(dve.tensor_tensor(uu[:, t, cols], l_r[:, 0, cols], l_r[:, 1, cols], ALU.add), ("hsum", l, t))
                own()
                dve.wait_ge(act_done.sem, act_done.after("read", ("proj", l, "cg", t)))
                finish(dve.tensor_tensor(y_c[:, t, cols], y_c[:, t, cols], uu[:, t, cols], ALU.mult), ("y_c", l, t))

            def nk(t):
                return T if t >= 2 else CTX

            def row_max(l, n, key, t, sink):
                dve.wait_ge(pe_done.sem, pe_done.after(*key))
                finish(dve.tensor_reduce(sm[:, n % 8, 0:1], sc[:, n % 3, 0:nk(t)], AX, ALU.max, negate=True))
                own()
                if sink is None:
                    ins = dve.tensor_scalar(sm[:, n % 8, 1:2], sm[:, n % 8, 0:1], SCALE, None, ALU.mult)
                else:
                    ins = dve.tensor_scalar(sm[:, n % 8, 1:2], sm[:, n % 8, 0:1], SCALE, sink, ALU.mult, ALU.min)
                finish(ins, ("nmax", l, n))

            def max_b(l, i):
                for m in range(2):
                    n = 2 * i + m
                    row_max(l, n, ("s_b", l, n), unit_b(l, i)[0], None)

            def combine(l, i):
                a, b = 2 * i, 2 * i + 1
                cols = slice(0, nk(unit_b(l, i)[0]))
                dve.wait_ge(act_done.sem, act_done.after("exp", l, b))
                finish(dve.reciprocal(sm[:, a % 8, 4:5], sm[:, a % 8, 2:3]))
                finish(dve.reciprocal(sm[:, b % 8, 4:5], sm[:, b % 8, 2:3]))
                own()
                finish(dve.tensor_scalar(sm[:, b % 8, 5:6], sm[:, b % 8, 4:5], nlam[:, l, 1:2], None, ALU.mult))
                if i >= 2:
                    dve.wait_ge(pe_done.sem, pe_done.after("pt_b", l, i - 2))
                finish(dve.tensor_scalar(ww[:, i % 2, cols], pp[:, a % 4, cols], sm[:, a % 8, 4:5], None, ALU.mult))
                own()
                finish(dve.scalar_tensor_tensor(ww[:, i % 2, cols], pp[:, b % 4, cols], sm[:, b % 8, 5:6],
                                                ww[:, i % 2, cols], ALU.mult, ALU.add), ("w_b", l, i))

            def b_start(l):
                max_b(l, 0)

            def b(l, i):
                combine(l, i)
                if i + 1 < n_b(l):
                    max_b(l, i + 1)

            def max_a(l, i):
                t, h = unit_a(l, i)
                row_max(l, 2 * n_b(l) + i, ("s_a", l, i), t, nsink[:, h:h + 1])

            def out_a(l, i):
                t, h = unit_a(l, i)
                r = (2 * n_b(l) + i) % 8
                dve.wait_ge(act_done.sem, act_done.after("exp_sink", l, 2 * n_b(l) + i))
                finish(dve.tensor_tensor(sm[:, r, 4:5], sm[:, r, 2:3], sm[:, r, 3:4], ALU.add))
                own()
                finish(dve.reciprocal(sm[:, r, 5:6], sm[:, r, 4:5]))
                own()
                dve.wait_ge(pe_done.sem, pe_done.after("pv_a", l, i))
                if i >= 2 * A_HEADS:
                    dve.wait_ge(pe_done.sem, pe_done.after("yt_a", l, t - 2))
                finish(dve.tensor_scalar(yrow_a[:, t % 2, h * HEAD:(h + 1) * HEAD], bank(("pv_a", l, i))[:, 0:HEAD],
                                         sm[:, r, 5:6], None, ALU.mult), ("o_a", l, t, h), ("read", ("pv_a", l, i)))

            def b_rows(l):
                n = len(qtiles(l)) * B_HEADS
                dve.wait_ge(act_done.sem, act_done.after("bst", l))
                finish(dve.reciprocal(bst[:, 1, 0:n], bst[:, 0, 0:n]))
                own()
                for j, t in enumerate(qtiles(l)):
                    for h in range(B_HEADS):
                        c = slice(h * P, (h + 1) * P)
                        finish(dve.tensor_scalar(yrow[:, j, c], yrow[:, j, c], bst[:, 1, j * 4 + h:j * 4 + h + 1],
                                                 None, ALU.mult), ("yrow_b", l, t))

            def a_start(l):
                max_a(l, 0)
                max_a(l, 1)

            def a(l, i):
                if i + 2 < n_a(l):
                    max_a(l, i + 2)
                if i >= 2:
                    out_a(l, i - 2)

            def a_end(l):
                out_a(l, n_a(l) - 2)
                out_a(l, n_a(l) - 1)

            def gate_store(l, m, n):
                splits(("mgate", l, m, n))

            def ysplit(l):
                cols = slice(c0(l), T)
                for n in range(N_BRANCH):
                    for k in range(KC):
                        dve.wait_ge(act_done.sem, act_done.after("y_hi", l, n, k))
                        finish(dve.tensor_tensor(yl[n][:, k, cols], (q_a, q_b, y_c)[n][:, k, cols],
                                                 yh[n][:, k, cols].bitcast(F32), ALU.subtract), ("y_lo", l, n, k))

            def merge(l, m):
                cols = slice(c0(l), T)
                for n in range(N_BRANCH):
                    key = ("mbranch", l, m, n)
                    u = m * N_BRANCH + n
                    if u < N_STORED[l]:
                        per = (T - c0(l)) // CTX
                        g = gst[:, u * per:(u + 1) * per].rearrange("p a n -> p (a n)")
                    else:
                        splits(("mgate", l, m, n))
                        g = tg[:, u % 2, cols]
                    splits(key)
                    dve.wait_ge(act_done.sem, act_done.after("tg", l, m, n))
                    dve.wait_ge(pe_done.sem, pe_done.after(*key))
                    own()
                    if n == 0:
                        if m:
                            dve.wait_ge(act_done.sem, act_done.after("mx_hi", l, m - 1))
                        finish(dve.scalar_tensor_tensor(mixt[:, cols], g, 1.0, bank(key)[:, cols], ALU.add, ALU.mult),
                               ("read", key))
                    else:
                        finish(dve.scalar_tensor_tensor(mixu[:, cols], g, 1.0, bank(key)[:, cols], ALU.add, ALU.mult),
                               ("read", key))
                        own()
                        finish(dve.tensor_tensor(mixt[:, cols], mixt[:, cols], mixu[:, cols], ALU.add), ("mixt", l, m))
                dve.wait_ge(act_done.sem, act_done.after("mx_hi", l, m))
                finish(dve.scalar_tensor_tensor(mx_lo[m][:, cols], mixt[:, cols], 0.5, mx_hi[m][:, cols].bitcast(F32),
                                                ALU.mult, ALU.subtract), ("mx_lo", l, m))

            def wout(l, m):
                splits(("wout", l, m))

            def residual(l, which):
                cols = slice(c0(l), T)
                dve.wait_ge(act_done.sem, act_done.after("read", ("spread", l, which)))
                for k in range(KD):
                    for s, a in streams(l):
                        finish(dve.scalar_tensor_tensor(ht[:, k % 2, a:a + CTX], fout[:, k, a:a + CTX],
                                                        gain[:, l, which, k, s:s + 1], rstd[:, a:a + CTX], ALU.mult, ALU.mult))
                    own()
                    finish(dve.tensor_tensor(xT[:, k, cols], xT[:, k, cols], ht[:, k % 2, cols], ALU.add),
                           ("x", l, which, k))

            def ffn_in(l, j):
                cols = slice(c0(l), T)
                splits(("fgate", l, j))
                key = ("fup", l, j)
                splits(key)
                dve.wait_ge(act_done.sem, act_done.after("read", ("fgate", l, j)))
                dve.wait_ge(pe_done.sem, pe_done.after(*key))
                if j:
                    own()
                finish(dve.tensor_tensor(hid[:, cols], sg[:, j % 2, cols], bank(key)[:, cols], ALU.mult), ("read", key))
                dve.wait_ge(act_done.sem, act_done.after("f_hi", l, j))
                own()
                finish(dve.tensor_tensor(f_lo[j][:, cols], hid[:, cols], f_hi[j][:, cols].bitcast(F32), ALU.subtract),
                       ("f_lo", l, j))

            def ffn_out(l, m):
                splits(("ffn_out", l, m))

            def none(*args):
                pass

            finish(dve.memset(cs[:], 0.0), ("cs_zero",))
            dve.wait_ge(consts_loaded, 16 * len(consts))
            finish(dve.tensor_copy(identb[:], ident[:]))
            finish(dve.tensor_copy(mask[:], maskf[:]), ("mask",))
            start()
            steps = dict(square=none, norm=norm, modk=none, modend=modend, modulate=modulate, proj=proj, lru=lru,
                         b_start=b_start, b=b, b_end=none, b_rows=b_rows, a_start=a_start, a=a, a_end=a_end,
                         a_rows=none, gate_store=gate_store, ysplit=ysplit, merge=merge, wout=wout, ffn_in=ffn_in,
                         ffn_out=ffn_out, residual=residual)
            for step, *args in plan:
                steps[step](*args)

    return {"pe_done": pe_done.marks, "act_done": act_done.marks, "dve_done": dve_done.marks, "pool_done": pool_done.marks}


def build(make, shapes, launch_args):
    known = {n: {} for n in ("pe_done", "act_done", "dve_done", "pool_done")}
    nc = None
    for _ in range(2):
        nc = make()
        io = {n: nc.dram_tensor(f"{n}_dram", s, F32, kind=k).ap() for n, (s, k) in shapes.items()}
        known = program(nc, io, known)
    return nc


def rotary_tables():
    rd = HEAD // 4
    t = np.arange(SEQ)
    pos = np.stack([t // GRID_W, t % GRID_W]).astype(np.float32)
    inv = (1.0 / (10000.0 ** (np.arange(rd, dtype=np.float32) * 2.0 / (HEAD // 2)))).astype(np.float32)
    cos, sin = np.zeros((HEAD, SEQ), np.float32), np.zeros((HEAD, SEQ), np.float32)
    for axis in range(2):
        ang = (pos[axis][None, :] * inv[:, None]).astype(np.float32)
        for half in range(2):
            rows = slice((axis * 2 + half) * rd, (axis * 2 + half + 1) * rd)
            cos[rows] = np.cos(ang)
            sin[rows] = np.sin(ang) * (1 if half else -1)
    return np.tile(cos, (2, 1)), np.tile(sin, (2, 1))


def window_mask():
    q = np.arange(SEQ)[:, None]
    k = np.arange(SEQ)[None, :]
    m = np.where(np.abs(k - q) <= WINDOW, 0.0, MASKED).astype(np.float32)
    return np.ascontiguousarray(m.reshape(2, P, SEQ).transpose(1, 0, 2))


def columns(a):
    a = np.asarray(a)
    return a.reshape(-1, P).T


def kernel(x, c, ctx, c_ctx, w_mod, b_mod, norm_g, w_in, attn_sink, diff_lambda, diff_subln, conv_w, conv_b, lru_w,
           lru_b, lru_lambda, w_branch, w_out, w_ffn_in, w_ffn_out):
    import concourse.bacc as bacc
    from concourse.bass_utils import run_bass_kernel_spmd

    def blocks(w):
        w = np.asarray(w)
        k, n = w.shape
        return w.reshape(k // P, P, n // P, P).transpose(0, 2, 1, 3)

    stream = np.empty((DEPTH * N_GRAN, P, 8, P), np.float32)
    for l in range(DEPTH):
        cut = {"w_in": blocks(w_in[l]), "w_branch": blocks(np.asarray(w_branch[l]).reshape(N_BRANCH * C_W, D)),
               "w_out": blocks(w_out[l]), "w_ffn_in": blocks(w_ffn_in[l]), "w_ffn_out": blocks(w_ffn_out[l])}
        for i, (name, k, n) in enumerate(block_order(l)):
            stream[l * N_GRAN + i // 8, :, i % 8, :] = cut[name][k, n]

    vec = np.empty((P, DEPTH, V_N), np.float32)
    lruw = np.zeros((DEPTH, P, 16, P), np.float32)
    for l in range(DEPTH):
        v = vec[:, l]
        v[:, V_BMOD:V_BMOD + 96] = np.repeat(columns(b_mod[l]), 2, axis=1)
        v[:, V_G:V_G + 64] = np.repeat(columns(norm_g[l]), 2, axis=1)
        v[:, V_CW:V_CW + 16] = columns(conv_w[l])
        v[:, V_CB:V_CB + 4] = columns(conv_b[l])
        v[:, V_LB:V_LB + 16] = columns(lru_b[l])
        v[:, V_LAM:V_LAM + 8] = columns(lru_lambda[l])
        v[:, V_SINK:V_SINK + 8] = np.asarray(attn_sink[l])[None, :]
        v[:, V_SUB] = np.asarray(diff_subln[l])
        w = np.asarray(lru_w[l]).reshape(4, C_BLOCKS, HEAD, HEAD)
        for dg in range(4):
            for n in range(C_BLOCKS):
                half = slice(HEAD * (n % 2), HEAD * (n % 2 + 1))
                lruw[l, half, dg * KC + n // 2, half] = w[dg, n]

    cos, sin = rotary_tables()
    both = np.concatenate([np.asarray(ctx)[0], np.asarray(x)[0]], axis=0)
    arrays = {
        "xT": both.T.reshape(KD, P, T).transpose(1, 0, 2),
        "cT": np.stack([columns(c_ctx), columns(np.asarray(c)[0])], axis=2),
        "vec": vec, "lruw": lruw, "w_mod": np.asarray(w_mod).reshape(DEPTH, KD, P, 6 * D),
        "dl": np.broadcast_to(np.asarray(diff_lambda)[None], (P, DEPTH, 4, HEAD)), "stream": stream.reshape(-1, P, 8 * P),
        "ident": np.eye(P, dtype=np.float32), "cos": cos, "sin": sin, "maskf": window_mask(),
    }
    arrays = {n: np.ascontiguousarray(a) for n, a in arrays.items()}
    shapes = {n: (a.shape, "ExternalInput") for n, a in arrays.items()}
    shapes["out"] = ((P, KD, SEQ), "ExternalOutput")
    nc = build(lambda: bacc.Bacc("TRN2", target_bir_lowering=False, num_devices=1), shapes, None)
    result = run_bass_kernel_spmd(nc, [{f"{n}_dram": a for n, a in arrays.items()}], core_ids=[0])
    out = result.results[0]["out_dram"]
    return np.ascontiguousarray(out.transpose(1, 0, 2).reshape(D, SEQ).T)[None]
```

```python
import math
from contextlib import ExitStack

import numpy as np
import concourse.bass as bass
from concourse import mybir

P = 128
F32, F32R, BF16 = mybir.dt.float32, mybir.dt.float32r, mybir.dt.bfloat16
ACT = mybir.ActivationFunctionType
ALU = mybir.AluOpType
AX = mybir.AxisListType.X

DEPTH, D, SEQ, CTX = 2, 1024, 256, 256
T = CTX + SEQ
KD = D // P
HEAD = 64
A_HEADS, A_KV, B_HEADS, B_VDIM = 8, 2, 4, 128
C_W, CONV_W, C_BLOCKS = 512, 4, 8
KC = C_W // P
N_BRANCH = 3
BRANCHES = (2, 1, 0)
FFN = 2816
KF = FFN // P
EPS = 1e-6
SCALE = HEAD ** -0.5
GRID_W, WINDOW = 64, 128
MASKED = -1e30

IN_TILE = {"aq": 0, "ak": 4, "av": 5, "bq": 6, "bk": 10, "bv": 14, "cu": 18, "cg": 22, "gt": 26}
N_STORED = (9, 18)
LATE = 2
MOD_ROUNDS, MOD_COLS = 3, 2048
ACC = 4
POOL_TILES = (1, 3, 5)
SQ = 4
RAW = 3
SPLIT = 3

V_BMOD, V_G, V_CW, V_CB, V_LB, V_LAM, V_SINK, V_SUB = 0, 96, 160, 176, 180, 196, 204, 212
V_N = 213


def plan_layer(l):
    tiles = [0, 1, 2, 3] if l == 0 else [2, 3]
    gates = [("gate_store", l, *divmod(i, N_BRANCH)) for i in range(N_STORED[l])]
    heads = (("cu", 0), ("cu", 1), ("cg", 0))
    if l == 0:
        steps = [("square", 0, 0, k) for k in range(KD)] + [("norm", 0, 0)]
        steps += [("modk0", 0, 0, k) for k in range(KD)] + [("modend0", 0, 0), ("modulate", 0, 0, 0, 4)]
        steps += [("modk0", 0, 1, k) for k in range(2)] + [("group", 0, 0, 2) + heads]
        steps += [("modk0", 0, 1, k) for k in range(2, KD)]
        steps += [("modend0", 0, 1), ("group", 0, 2, 4) + heads, ("modulate", 0, 0, 4, KD), ("group", 0, 4, KD) + heads]
    else:
        late = [[("modk", l, MOD_ROUNDS - 1, k)] for k in range(KD - LATE, KD)]
        steps = late[0] + [("square", l, 0, k) for k in range(KD)]
        steps += [("norm", l, 0)] + late[1] + [("modrow", l, MOD_ROUNDS - 1), ("modulate", l, 0, 0, KD)]
        steps += [("group", l, 0, KD) + heads, ("modend", l, MOD_ROUNDS - 1)]

    def proj(kind, t):
        return ("proj", l, kind, t)

    def rotate(kind, t):
        return ("rotate", l, kind, t)

    first = [proj("cg", 1), ("lru_a", l, 0), proj("cu", 2), proj("cu", 3),
             ("lru_a", l, 1), proj("cg", 2), proj("cg", 3), ("lru_b", l, 0), ("lru_b", l, 1), proj("bk", 0),
             ("lru_a", l, 2), proj("bq", 0), ("lru_a", l, 3), rotate("bk", 0), proj("bk", 1), ("lru_b", l, 2),
             rotate("bq", 0), proj("bq", 1), ("lru_b", l, 3), proj("bv", 0), rotate("bk", 1), proj("bv", 1),
             ("b_start", l), proj("bk", 2)]
    k = 0
    for step in first:
        steps.append(step)
        if l == 0 and step[0] == "proj" and k < KD:
            steps.append(("modk", 0, 1, k))
            k += 1
            if k == KD:
                steps.append(("modrow", 0, 1))
    if l == 0:
        steps.append(("modend", 0, 1))

    products = [proj(kind, t) for kind, t in (
        ("bq", 2), ("bv", 2), ("ak", 0), ("bk", 3), ("bq", 3), ("bv", 3), ("av", 0), ("aq", 0), ("aq", 1),
        ("aq", 2), ("aq", 3))] + gates[:5]
    after = {("bq", 1): [rotate("bq", 1)], ("bv", 1): [("turn_v", l, "bv", 1)]}
    for step in products:
        if step[0] == "proj":
            after[step[2:]] = [("turn_v",) + step[1:] if step[2][1] == "v" else rotate(*step[2:])]
    n = len(tiles) * B_HEADS
    each = len(products) // n
    pending = [[("turn_v", l, "bv", 0)], after["bq", 1], after["bv", 1], [rotate("bk", 2)]]
    for i in range(n):
        steps += [("b", l, i)] + sum(pending, [])
        some = products[i * each:(i + 1) * each]
        steps += some
        pending = [after.get(step[2:], []) for step in some]
    steps += [("b_end", l)] + sum(pending, [])

    fill = gates[5:]
    n = len(tiles) * A_HEADS
    steps += [("a_start", l), fill[0], ("b_rows", l)]
    fill = fill[1:]
    done = k = 0
    for i in range(n):
        steps.append(("a", l, i))
        if i % A_HEADS == 1 and i > A_HEADS:
            steps.append(("a_rows", l, tiles[i // A_HEADS - 1]))
        if l == 0 and i % 4 == 2:
            steps.append(("modk", 0, 2, k))
            k += 1
            if k == KD:
                steps.append(("modrow", 0, 2))
        while done < (i + 1) * len(fill) // n:
            steps.append(fill[done])
            done += 1
    steps += [("a_end", l)] + ([("modend", 0, 2)] if l == 0 else [])
    steps += [("ysplit", l, 0), ("a_rows", l, tiles[-1]), ("ysplit", l, 1), ("ysplit", l, 2)]

    summed = {m: [] for m in range(KD)}
    summed.update({3: [0, 1, 2], 6: [3, 4, 5], 7: [6, 7]})

    steps += [("merge", l, m) for m in range(KD)]
    for m in range(KD):
        steps += [("wout", l, m)] + [("square", l, 1, k) for k in summed[m]]
    mods = []
    if l + 1 < DEPTH:
        for r in range(MOD_ROUNDS):
            mods += [[("modk", l + 1, r, k)] for k in range(KD)]
            mods[-1].append(("modrow", l + 1, r))
            if r:
                mods[-KD].append(("modend", l + 1, r - 1))
        mods.append([("modend", l + 1, MOD_ROUNDS - 1)])

    def mod():
        return mods.pop(0) if mods else []

    steps += [("norm", l, 1), ("residual", l, 1)] + mod()
    steps += [("square", l, 2, k) for k in range(KD)]
    steps += [("norm", l, 2)] + mod() + [("modulate", l, 2, 0, KD)]

    steps.append(("ffn_group", l))
    for j in range(KF):
        steps += [("ffn_in", l, j)] + (mod() if len(mods) > LATE + 1 else [])
    for m in range(KD):
        steps += [("ffn_out", l, m)] + [("square", l, 3, k) for k in summed[m]]
    return steps + [("norm", l, 3), ("residual", l, 3)]


def blocks_of(step):
    s, l, a = step[0], step[1], step[2:]

    def gate(m, n):
        return [("w_in", k, IN_TILE["gt"] + BRANCHES[n] * KD + m) for k in range(KD)]

    if s == "proj":
        return [("w_in", k, IN_TILE[a[0]] + a[1]) for k in range(KD)]
    if s == "group":
        return [("w_in", k, IN_TILE[kind] + t) for k in range(a[0], a[1]) for kind, t in a[2:]]
    if s == "gate_store":
        return gate(*a)
    if s == "merge":
        out = []
        for n in range(N_BRANCH):
            if a[0] * N_BRANCH + n >= N_STORED[l]:
                out += gate(a[0], n)
            out += [("w_branch", BRANCHES[n] * KC + k, a[0]) for k in range(KC)]
        return out
    if s == "wout":
        return [("w_out", k, a[0]) for k in range(KD)]
    if s == "ffn_group":
        return [("w_ffn_in", k, n) for k in range(KD) for n in (0, KF, 1)]
    if s == "ffn_in":
        halves = {0: (), 1: (1,)}.get(a[0], (0, 1))
        return [("w_ffn_in", k, a[0] + half * KF) for half in halves for k in range(KD)]
    if s == "ffn_out":
        return [("w_ffn_out", k, a[0]) for k in range(KF)]
    return []


def block_order(l):
    return [b for step in plan_layer(l) for b in blocks_of(step)]


N_GRAN = len(block_order(0)) // 8


class Done:

    def __init__(self, sem, known):
        self.sem, self.known, self.marks, self.count = sem, known, {}, 0

    def mark(self, *keys):
        self.count += 1
        for key in keys:
            self.marks[key] = self.count
        return 1

    def after(self, *key):
        return self.known[key] if self.known else 1


def lam_init(l):
    return 0.8 - 0.6 * math.exp(-0.3 * l)


def program(nc, io, known):
    with ExitStack() as ctx:
        def sem(name):
            return ctx.enter_context(nc.semaphore(name))

        def sb(name, shape, dt=F32):
            return ctx.enter_context(nc.sbuf_tensor(name, shape, dt))

        xT = sb("xT", [P, KD, T])
        h_base = -(-nc.sbuf_base // 32) * 32
        h_hi = sb("h_hi", [P, KD, T], F32R)
        h_lo = sb("h_lo", [P, KD, T], F32R)
        raw = sb("raw", [P, RAW, 8 * P])
        w_hi = sb("w_hi", [P, SPLIT, 8, P], F32R)
        w_lo = sb("w_lo", [P, SPLIT, 8, P], F32R)
        modraw = sb("modraw", [P, MOD_COLS])
        mrow = sb("mrow", [P, T])
        vec = sb("vec", [P, DEPTH, V_N])
        cos, sin = sb("cos", [P, SEQ]), sb("sin", [P, SEQ])
        ident, identb = sb("ident", [P, P]), sb("identb", [P, P], BF16)
        ones = sb("ones", [P, P])
        mask = sb("mask", [P, 2, SEQ], BF16)
        cT, cs = sb("cT", [P, KD, 2]), sb("cs", [P, KD, 32])
        modv = sb("modv", [P, DEPTH, 6 * KD, 2])
        gain = sb("gain", [P, DEPTH, 4, KD, 2])
        small = sb("small", [P, 8, DEPTH, 8])
        kdec = sb("kdec", [P, 2, DEPTH, 8])
        hb = sb("hb", [P, DEPTH, 16])
        nlam, gsub = sb("nlam", [P, DEPTH, 2]), sb("gsub", [P, DEPTH])
        nsink = sb("nsink", [P, DEPTH, 8])
        sm = sb("sm", [P, 8, 8])
        bss, bst = sb("bss", [P, 4, 4]), sb("bst", [P, 2, 16])
        rt = sb("rt", [P, 2, 4])

        base = -(-nc.sbuf_base // 32) * 32
        sb("arena", [P, 104 * 256])

        def at(name, kib, shape, dt=F32):
            return nc.alloc_sbuf_tensor_at(name, shape, dt, offset=base + int(kib * 1024))

        q_a, q_b = at("q_a", 0, [P, 4, T]), at("q_b", 8, [P, 4, T])
        k_a, k_b = at("k_a", 16, [P, 1, T]), at("k_b", 20, [P, 4, T])
        k_sw = at("k_sw", 18, [P, 1, T])
        vv = at("vv", 28, [P, 4, 5 * P])
        y_c = at("y_c", 38, [P, 4, T])
        cu = at("cu", 46, [P, 4, 2, CTX + 4])
        uu = at("uu", 54.25, [P, 4, T])
        l_r, l_i, l_a, l_q = (
            [at(f"{name}{i}", a, [P, 2, T]) for i, a in enumerate(places)]
            for name, places in (("l_r", (62.25, 0)), ("l_i", (66.25, 4)), ("l_a", (70.25, 80)), ("l_q", (74.25, 84))))
        gst = at("gst", 46, [P, 18, CTX])
        vt = at("vt", 72, [P, 2, T])
        yrow, yrow_a = at("yrow", 64, [P, 4, C_W]), at("yrow_a", 72, [P, 2, C_W])
        pt = at("pt", 76, [P, 2, 4, P])
        pp, ww = at("pp", 80, [P, 4, T]), at("ww", 88, [P, 2, T])
        rope, osq = at("rope", 92, [P, 2, SEQ]), at("osq", 94, [P, P])
        lruw = at("lruw", 96, [P, 16, P])
        yh = [at(f"yh{n}", a, [P, KC, T], F32R) for n, a in enumerate((80, 64, 16))]
        yl = [at(f"yl{n}", a, [P, KC, T], F32R) for n, a in enumerate((88, 72, 24))]
        tg, mixt = at("tg", 32, [P, 2, T]), at("mixt", 36, [P, T])
        mixu = mrow
        mx_hi = [at(f"mx_hi{m}", 2 * m, [P, T], F32R) for m in range(KD)]
        mx_lo = [at(f"mx_lo{m}", a, [P, T], F32R) for m, a in enumerate((38, 40, 42, 44, 96, 98, 100, 102))]
        f_hi = [at(f"f_hi{j}", 2 * j, [P, T], F32R) for j in range(KF)]
        f_lo = [at(f"f_lo{j}", 44 + 2 * j, [P, T], F32R) for j in range(KF)]
        sg, hid = at("sg", 88, [P, 2, T]), at("hid", 92, [P, T])
        sq = at("sq", 88, [P, SQ, T])
        ht = at("ht", 0, [P, KD, T])
        rstd, diag = at("rstd", 80, [P, T]), at("diag", 82, [P, 4, P])
        rows = at("rows", 84, [P, T])
        mod0 = [at(f"mod0_{h}", 32 * h, [P, KD, 2, MOD_COLS // 4]) for h in range(2)]
        maskf, dl, dots = at("maskf", 64, [P, 2, SEQ]), at("dl", 68, [P, DEPTH, 4, HEAD]), at("dots", 70, [P, DEPTH, 2, HEAD])
        fout = nc.alloc_sbuf_tensor_at("fout", [P, KD, T], F32, offset=h_base)
        hh, hl = [h_hi[:, k] for k in range(KD)], [h_lo[:, k] for k in range(KD)]

        acc = ctx.enter_context(nc.psum_tensor("acc", [P, ACC, 512], F32))
        sc = ctx.enter_context(nc.psum_tensor("sc", [P, 3, 512], F32))
        oo = ctx.enter_context(nc.psum_tensor("oo", [P, 512], F32))
        half_bank = oo[:], sc[:, 2, :]
        stat, sums = sc[:, 0, :], sc[:, 1, :]

        pe_done, act_done, dve_done, pool_done = (
            Done(sem(n), known[n]) for n in ("pe_done", "act_done", "dve_done", "pool_done"))
        raw_loaded = [sem(f"raw_loaded{i}") for i in range(RAW)]
        x_loaded = [sem(f"x_loaded{i}") for i in range(KD // 2)]
        mod0_loaded = [sem(f"mod0_loaded{k}") for k in range(2 * KD)]
        consts_loaded, tables_loaded, lru_loaded, mod_loaded, stored = (
            sem("consts_loaded"), sem("tables_loaded"), sem("lru_loaded"), sem("mod_loaded"), sem("stored"))

        def c0(l):
            return 0 if l == 0 else CTX

        def streams(l):
            return [(0, 0), (1, CTX)] if l == 0 else [(1, CTX)]

        def qtiles(l):
            return [0, 1, 2, 3] if l == 0 else [2, 3]

        plan = [step for l in range(DEPTH) for step in plan_layer(l)]
        mods = [step[1:] for step in plan if step[0] == "modk"]
        rounds = [(0, 0)] + [step[1:] for step in plan if step[0] == "modend"]

        def keys_of_step(s, l, *a):
            if s == "proj":
                return [(("proj", l) + a, KD, "A")]
            if s == "group":
                return [] if a[0] else [(("proj", l) + what, KD, "A") for what in a[2:]]
            if s == "turn_v":
                return [(("vT", l) + a, 0, "A")]
            if s == "gate_store":
                return [(("mgate", l) + a, KD, "A")]
            if s == "lru_a":
                return [(("gate", l, a[0], d, g), 0, "A") for d in range(2) for g in range(2)]
            if s == "norm":
                return [(("spread", l, a[0]), 0, "A" if (l, a[0]) == (0, 0) else "D")]
            if s == "modend0":
                return [(("modT0", l, a[0]), 0, "D")]
            if s == "modend":
                return [(("modT", l, a[0]), 0, "D")]
            if s == "b":
                return ([(("pv_b", l, a[0] - 1), 0, "A")] if a[0] else []) + [(("pt_b", l, a[0]), 0, "A")]
            if s == "b_end":
                return [(("pv_b", l, len(qtiles(l)) * B_HEADS - 1), 0, "A")]
            if s == "b_rows":
                return [(("yt_b", l, t), 0, "A") for t in qtiles(l)]
            if s == "a":
                return [(("pt_a", l, a[0]), 0, "A")] + ([(("pv_a", l, a[0] - 1), 0, "D")] if a[0] else [])
            if s == "a_end":
                return [(("pv_a", l, len(qtiles(l)) * A_HEADS - 1), 0, "D")]
            if s == "a_rows":
                return [(("yt_a", l, a[0]), 0, "A")]
            if s == "merge":
                out = []
                for n in range(N_BRANCH):
                    if a[0] * N_BRANCH + n >= N_STORED[l]:
                        out.append((("mgate", l, a[0], n), KD, "A"))
                    out.append((("mbranch", l, a[0], n), KC, "D"))
                return out
            if s in ("wout", "ffn_out"):
                return [((s, l, a[0]), KD if s == "wout" else KF, "A")]
            if s == "ffn_in":
                return [(("fgate", l, a[0]), KD, "A"), (("fup", l, a[0]), KD, "D")]
            return []

        def keys_in(*step):
            return [key for key, n, by in keys_of_step(*step) if n]

        items = [item for step in plan for item in keys_of_step(*step)]
        order = [key for key, n, by in items]
        info = {key: (n, by) for key, n, by in items}
        slot_of = {key: i for i, key in enumerate(order)}
        blocks_end, total = {}, 0
        for key in order:
            total += info[key][0]
            blocks_end[key] = total
        assert total == DEPTH * N_GRAN * 8

        def granules_at(key):
            n = blocks_end[key]
            return min(max((n - info[key][0]) // 8 + SPLIT, -(-n // 8)), DEPTH * N_GRAN)

        def after_norm(l, which):
            if which == 1:
                return ("fgate", l, 0)
            if which == 3 and l + 1 < DEPTH:
                return ("proj", l + 1, "cu", 0)
            return None

        def bank(key):
            return acc[:, slot_of[key] % ACC, :]

        def wait_x(eng, l, which, k):
            done = pool_done if k in POOL_TILES else dve_done
            eng.wait_ge(done.sem, done.after("x", l, which, k))

        def wait_raw(eng, g):
            eng.wait_ge(raw_loaded[g % RAW], 16 * (g // RAW + 1))

        def unit_b(l, i):
            h, t = divmod(i, len(qtiles(l)))
            return qtiles(l)[t], h

        def unit_a(l, i):
            return qtiles(l)[i // A_HEADS], i % A_HEADS

        def n_b(l):
            return len(qtiles(l)) * B_HEADS

        def n_a(l):
            return len(qtiles(l)) * A_HEADS

        def mix(buf, l, m):
            return buf[:, 0:T] if l == 0 else buf[:, m % 2 * CTX:(m % 2 + 1) * CTX]

        block = ctx.enter_context(nc.Block())

        consts = (("cT", cT), ("vec", vec), ("ident", ident), ("dl", dl))
        tables = (("cos", cos), ("sin", sin), ("maskf", maskf))

        @block.sync
        def _(sp):
            for name, t in consts:
                sp.dma_start(t[:], io[name]).then_inc(consts_loaded, 16)
            for i in range(KD // 2):
                sp.dma_start(xT[:, 2 * i:2 * i + 2], io["xT"][:, 2 * i:2 * i + 2]).then_inc(x_loaded[i], 16)
            for h in range(2):
                for k in range(KD):
                    sp.dma_start(mod0[h][:, k], io["w_mod"][0, k, :, 0:MOD_COLS].rearrange(
                        "p (j h n) -> p j h n", j=2, h=2)[:, :, h, :]).then_inc(mod0_loaded[h * KD + k], 16)
                    if h == 0 and k in (4, KD - 1):
                        g = 0 if k == 4 else 1
                        sp.dma_start(raw[:, g, :], io["stream"][g]).then_inc(raw_loaded[g], 16)
            for g in range(2, DEPTH * N_GRAN):
                if g >= RAW:
                    sp.wait_ge(dve_done.sem, dve_done.after("w_lo", g - RAW))
                sp.dma_start(raw[:, g % RAW, :], io["stream"][g]).then_inc(raw_loaded[g % RAW], 16)
                if g == RAW - 1:
                    for name, t in tables:
                        sp.dma_start(t[:], io[name]).then_inc(tables_loaded, 16)
                    sp.dma_start(lruw[:], io["lruw"][0]).then_inc(lru_loaded, 16)
                    l, r, k = mods[0]
                    sp.dma_start(modraw[:], io["w_mod"][l, k, :, r * MOD_COLS:(r + 1) * MOD_COLS]).then_inc(mod_loaded, 16)
                if g == N_GRAN - 10:
                    sp.wait_ge(pe_done.sem, pe_done.after("wout", 0, KD - 1))
                    sp.dma_start(lruw[:], io["lruw"][1]).then_inc(lru_loaded, 16)
            for k in range(KD):
                wait_x(sp, DEPTH - 1, 3, k)
                sp.dma_start(io["out"][:, k, :], xT[:, k, CTX:T]).then_inc(stored, 16)
            sp.wait_ge(stored, 16 * KD)

        @block.gpsimd
        def _(pool):
            pool.memset(ones[:], 1.0).then_inc(pool_done.sem, pool_done.mark(("ones",)))
            high = [0]

            def highs(key):
                limit = granules_at(key)
                while high[0] < limit:
                    q = high[0]
                    wait_raw(pool, q)
                    if q >= SPLIT:
                        pool.wait_ge(pe_done.sem, pe_done.after("used", q - SPLIT))
                    pool.tensor_scalar(w_hi[:, q % SPLIT].rearrange("p k n -> p (k n)"), raw[:, q % RAW, :], 1.0, 0.0,
                                       ALU.mult, ALU.add).then_inc(pool_done.sem, pool_done.mark(("w_hi", q)))
                    high[0] += 1

            def residual(l, which):
                cols = slice(c0(l), T)
                for k in POOL_TILES:
                    pool.wait_ge(dve_done.sem, dve_done.after("scaled", l, which, k))
                    pool.tensor_tensor(xT[:, k, cols], xT[:, k, cols], ht[:, k, cols], ALU.add)\
                        .then_inc(pool_done.sem, pool_done.mark(("x", l, which, k)))

            for step, l, *args in plan:
                if step == "norm" and after_norm(l, *args):
                    highs(after_norm(l, *args))
                elif step == "residual":
                    residual(l, *args)
                for key in keys_in(step, l, *args):
                    highs(key)

        @block.tensor
        def _(pe):
            blocks = [0]

            def take(key):
                n = slot_of[key]
                if n >= ACC:
                    last = order[n - ACC]
                    if info[last][1] == "A":
                        pe.wait_ge(act_done.sem, act_done.after("read", last))
                    else:
                        pe.wait_ge(dve_done.sem, dve_done.after("read", last))
                return bank(key)

            def next_block():
                q, k = divmod(blocks[0], 8)
                blocks[0] += 1
                if k == 0:
                    pe.wait_ge(dve_done.sem, dve_done.after("w_lo", q))
                return q, k

            def gemm_group(keys, cols, ready, first=0, end=KD):
                outs = [(bank(key) if first else take(key))[:, c] for key, c in zip(keys, cols)]
                for i in range(first, end):
                    pe.wait_ge(dve_done.sem, dve_done.after(*ready(i)))
                    for key, o, c in zip(keys, outs, cols):
                        q, k = next_block()
                        wh, wl = w_hi[:, q % SPLIT, k, :], w_lo[:, q % SPLIT, k, :]
                        pe.matmul(o, wh, hh[i][:, c], start=i == 0, stop=False)
                        pe.matmul(o, wh, hl[i][:, c], start=False, stop=False)
                        last = pe.matmul(o, wl, hh[i][:, c], start=False, stop=i == KD - 1)
                        names = ([("used", q)] if k == 7 else []) + ([key] if i == KD - 1 else [])
                        if names:
                            last.then_inc(pe_done.sem, pe_done.mark(*names))

            def gemm(key, src_hi, src_lo, cols, ready=None):
                out = take(key)
                n = info[key][0]
                for i in range(n):
                    q, k = next_block()
                    wh, wl = w_hi[:, q % SPLIT, k, :], w_lo[:, q % SPLIT, k, :]
                    if ready:
                        pe.wait_ge(dve_done.sem, dve_done.after(*ready(i)))
                    o = out[:, cols]
                    pe.matmul(o, wh, src_hi[i][:, cols], start=i == 0, stop=False)
                    pe.matmul(o, wh, src_lo[i][:, cols], start=False, stop=False)
                    last = pe.matmul(o, wl, src_hi[i][:, cols], start=False, stop=i == n - 1)
                    names = ([("used", q)] if k == 7 else []) + ([key] if i == n - 1 else [])
                    if names:
                        last.then_inc(pe_done.sem, pe_done.mark(*names))

            def modk(l, r, k):
                if k == 0:
                    pe.wait_ge(act_done.sem, act_done.after("mrow", *rounds[rounds.index((l, r)) - 1]))
                pe.wait_ge(mod_loaded, 16 * (mods.index((l, r, k)) + 1))
                for j in range(4):
                    last = pe.matmul(oo[32 * j:32 * (j + 1), :], cs[:, k, :], modraw[:, j * 512:(j + 1) * 512], start=k == 0,
                                     stop=k == KD - 1, tile_position=(0, 32 * j))
                last.then_inc(pe_done.sem, pe_done.mark(("modk", l, r, k)))

            def modk0(l, h, k):
                if k == 0:
                    pe.wait_ge(act_done.sem, act_done.after("silu_c",))
                pe.wait_ge(mod0_loaded[h * KD + k], 16)
                for j in range(2):
                    quarter = 32 * (k % 2 * 2 + j)
                    last = pe.matmul(half_bank[h][quarter:quarter + 32, :], cs[:, k, :], mod0[h][:, k, j], start=k < 2,
                                     stop=k >= KD - 2, tile_position=(0, quarter))
                last.then_inc(pe_done.sem, pe_done.mark(("modk0", l, h, k)))

            def modend0(l, h):
                out = take(("modT0", l, h))
                pe.wait_ge(act_done.sem, act_done.after("mrow0", l, h))
                for c in range(4):
                    last = pe.transpose(out[:, c * P:(c + 1) * P], mrow[:, c * P:(c + 1) * P], ident[:])
                last.then_inc(pe_done.sem, pe_done.mark(("modT0", l, h), *([("modT", l, 0)] if h else [])))

            def modend(l, r):
                out = take(("modT", l, r))
                pe.wait_ge(act_done.sem, act_done.after("mrow", l, r))
                for c in range(4):
                    last = pe.transpose(out[:, c * P:(c + 1) * P], mrow[:, c * P:(c + 1) * P], ident[:])
                last.then_inc(pe_done.sem, pe_done.mark(("modT", l, r)))

            def square(l, which, k):
                if k == 0:
                    pe.wait_ge(pool_done.sem, pool_done.after("ones",))
                pe.wait_ge(act_done.sem, act_done.after("square", l, which, k))
                cols, j = slice(0 if which == 0 else c0(l), T), k % 4
                pe.matmul(stat[32 * j:32 * (j + 1), cols], ones[:, 0:32], sq[:, k % SQ, cols], start=k < 4, stop=k >= 4,
                          tile_position=(0, 32 * j)).then_inc(pe_done.sem, pe_done.mark(("squared", l, which, k)))

            def norm(l, which):
                tiles = range(4) if which == 0 else qtiles(l)
                pe.wait_ge(act_done.sem, act_done.after("rows", l, which))
                for t in tiles:
                    last = pe.matmul(sums[:, t:t + 1], rows[:, t * P:(t + 1) * P], ones[:, 0:1], start=t == tiles[0],
                                     stop=t == tiles[-1], skip_group_check=True)
                last.then_inc(pe_done.sem, pe_done.mark(("total", l, which)))
                key = ("spread", l, which)
                out = take(key)
                for t in range(4) if which == 0 else qtiles(l):
                    pe.wait_ge(dve_done.sem, dve_done.after("diag", l, which, t))
                    last = pe.matmul(out[:, t * P:(t + 1) * P], ones[:], diag[:, t, :], start=True, stop=True)
                last.then_inc(pe_done.sem, pe_done.mark(key))

            def none(*args):
                pass

            def cols_of(l, kind):
                return slice(c0(l) if kind in ("aq", "bq", "cg") else 0, T)

            def proj(l, kind, t):
                gemm(("proj", l, kind, t), hh, hl, cols_of(l, kind))

            def group(l, first, end, *what):
                gemm_group([("proj", l) + w for w in what], [cols_of(l, w[0]) for w in what],
                           lambda i: ("h_lo", l, 0, i), first, end)

            def turn_v(l, kind, t):
                key = ("vT", l, kind, t)
                out = take(key)
                pe.wait_ge(act_done.sem, act_done.after("read", ("proj", l, kind, t)))
                for j in range(T // P):
                    last = pe.transpose(out[:, j * P:(j + 1) * P], vt[:, t % 2, j * P:(j + 1) * P], ident[:])
                last.then_inc(pe_done.sem, pe_done.mark(key))

            def lru_a(l, t):
                pe.wait_ge(lru_loaded, 16 * (l + 1))
                pe.wait_ge(dve_done.sem, dve_done.after("conv", l, t))
                for d in range(2):
                    for g in range(2):
                        key = ("gate", l, t, d, g)
                        pe.matmul(take(key), lruw[:, (d * 2 + g) * KC + t, :], uu[:, t, :], start=True, stop=True)\
                            .then_inc(pe_done.sem, pe_done.mark(key))

            def keys_of(t):
                return T if t >= 2 else CTX

            def scores(key, n, q, kk, t, local):
                if n >= 3:
                    pe.wait_ge(act_done.sem, act_done.after("exp", key[1], n - 3))
                qt = q[:, t * P:(t + 1) * P]
                if local and t >= 2:
                    pe.wait_ge(dve_done.sem, dve_done.after("mask",))
                    pe.matmul(sc[:, n % 3, 0:CTX], qt, kk[:, 0:CTX], start=True, stop=True)
                    pe.matmul(sc[:, n % 3, CTX:T], qt, kk[:, CTX:T], start=True, stop=False)
                    last = pe.matmul(sc[:, n % 3, CTX:T], identb[:], mask[:, t - 2, :], start=False, stop=True)
                else:
                    last = pe.matmul(sc[:, n % 3, 0:keys_of(t)], qt, kk[:, 0:keys_of(t)], start=True, stop=True)
                last.then_inc(pe_done.sem, pe_done.mark(key))

            def turn_keys(key, src, t):
                out = take(key)
                nk = keys_of(t) // P
                for j in range(nk):
                    last = pe.transpose(out[:, j * P:(j + 1) * P], src[:, j * P:(j + 1) * P], ident[:])
                last.then_inc(pe_done.sem, pe_done.mark(key))

            def weigh(key, slot, v, t):
                o = take(key)[:, 0:v.stop - v.start]
                nk = keys_of(t) // P
                for j in range(nk):
                    last = pe.matmul(o, pt[:, slot, j, :], vv[:, j, v], start=j == 0, stop=j == nk - 1)
                last.then_inc(pe_done.sem, pe_done.mark(key))

            def score_b(l, i):
                t, h = unit_b(l, i)
                if t == qtiles(l)[0]:
                    for kind in ("bk", "bq"):
                        pe.wait_ge(dve_done.sem, dve_done.after("qk", l, kind, h))
                for m in range(2):
                    half = slice(HEAD * m, HEAD * (m + 1))
                    scores(("s_b", l, 2 * i + m), 2 * i + m, q_b[half, h, :], k_b[half, h, :], t, False)

            def turn_b(l, i):
                pe.wait_ge(dve_done.sem, dve_done.after("w_b", l, i))
                turn_keys(("pt_b", l, i), ww[:, i % 2, :], unit_b(l, i)[0])

            def value_b(l, i):
                t, h = unit_b(l, i)
                if t == qtiles(l)[0]:
                    pe.wait_ge(act_done.sem, act_done.after("v", l, "bv", h))
                pe.wait_ge(act_done.sem, act_done.after("read", ("pt_b", l, i)))
                weigh(("pv_b", l, i), i % 2, slice(P * (h + 1), P * (h + 2)), t)

            def b_start(l):
                score_b(l, 0)

            def b(l, i):
                if i:
                    value_b(l, i - 1)
                if i + 1 < n_b(l):
                    score_b(l, i + 1)
                turn_b(l, i)

            def b_end(l):
                value_b(l, n_b(l) - 1)

            def turn_rows(key, src):
                out = take(key)
                for j in range(4):
                    last = pe.transpose(out[:, j * P:(j + 1) * P], src[:, j * P:(j + 1) * P], ident[:])
                last.then_inc(pe_done.sem, pe_done.mark(key))

            def b_rows(l):
                for j, t in enumerate(qtiles(l)):
                    pe.wait_ge(dve_done.sem, dve_done.after("yrow_b", l, t))
                    turn_rows(("yt_b", l, t), yrow[:, j, :])

            def score_a(l, i):
                t, h = unit_a(l, i)
                if i < A_HEADS and h % 2 == 0:
                    pe.wait_ge(dve_done.sem, dve_done.after("qk", l, "aq", h // 2))
                half = slice(HEAD * (h % 2), HEAD * (h % 2 + 1))
                kk = k_a if h // 4 == h % 2 else k_sw
                scores(("s_a", l, i), 2 * n_b(l) + i, q_a[half, h // 2, :], kk[half, 0, :], t, True)

            def turn_a(l, i):
                pe.wait_ge(act_done.sem, act_done.after("exp", l, 2 * n_b(l) + i))
                turn_keys(("pt_a", l, i), pp[:, i % 4, :], unit_a(l, i)[0])

            def value_a(l, i):
                t, h = unit_a(l, i)
                pe.wait_ge(act_done.sem, act_done.after("read", ("pt_a", l, i)))
                weigh(("pv_a", l, i), i % 2, slice(HEAD * (h // 4), HEAD * (h // 4 + 1)), t)

            def a_start(l):
                pe.wait_ge(act_done.sem, act_done.after("k_sw", l))
                pe.wait_ge(act_done.sem, act_done.after("v", l, "av", 0))
                score_a(l, 0)
                score_a(l, 1)

            def a(l, i):
                if i + 2 < n_a(l):
                    score_a(l, i + 2)
                turn_a(l, i)
                if i:
                    value_a(l, i - 1)

            def a_end(l):
                value_a(l, n_a(l) - 1)

            def a_rows(l, t):
                pe.wait_ge(dve_done.sem, dve_done.after("o_a", l, t, A_HEADS - 1))
                turn_rows(("yt_a", l, t), yrow_a[:, t % 2, :])

            def gate_store(l, m, n):
                gemm(("mgate", l, m, n), hh, hl, slice(c0(l), T))

            def merge(l, m):
                cols = slice(c0(l), T)
                for n in range(N_BRANCH):
                    if m * N_BRANCH + n >= N_STORED[l]:
                        gemm(("mgate", l, m, n), hh, hl, cols)
                    ready = (lambda i, n=n: ("y_lo", l, n, i)) if m == 0 else None
                    gemm(("mbranch", l, m, n), [yh[n][:, k] for k in range(KC)], [yl[n][:, k] for k in range(KC)],
                         cols, ready)

            def wout(l, m):
                gemm(("wout", l, m), mx_hi, mx_lo, slice(c0(l), T), (lambda i: ("mx_lo", l, i)) if m == 0 else None)

            def ffn_group(l):
                gemm_group([("fgate", l, 0), ("fup", l, 0), ("fgate", l, 1)], [slice(c0(l), T)] * 3,
                           lambda i: ("h_lo", l, 2, i))

            def ffn_in(l, j):
                if j > 1:
                    gemm(("fgate", l, j), hh, hl, slice(c0(l), T))
                if j:
                    gemm(("fup", l, j), hh, hl, slice(c0(l), T))

            def ffn_out(l, m):
                gemm(("ffn_out", l, m), f_hi, f_lo, slice(c0(l), T), (lambda i: ("f_lo", l, i)) if m == 0 else None)

            pe.wait_ge(consts_loaded, 16 * len(consts))
            steps = dict(square=square, norm=norm, modk=modk, modk0=modk0, modrow=none, modend=modend, modend0=modend0,
                         modulate=none, proj=proj, group=group, rotate=none,
                         turn_v=turn_v, ffn_group=ffn_group, lru_a=lru_a, lru_b=none,
                         b_start=b_start, b=b, b_end=b_end, b_rows=b_rows, a_start=a_start, a=a, a_end=a_end,
                         a_rows=a_rows, gate_store=gate_store, ysplit=none, merge=merge, wout=wout, ffn_in=ffn_in,
                         ffn_out=ffn_out, residual=none)
            for step, *args in plan:
                steps[step](*args)

        @block.scalar
        def _(act):
            def finish(ins, *names):
                ins.then_inc(act_done.sem, act_done.mark(*names))

            def own():
                act.wait_ge(act_done.sem, act_done.count)

            def modk(l, r, k):
                u = (l, r, k)
                if mods.index(u) + 1 < len(mods):
                    nl, nr, nk = mods[mods.index(u) + 1]
                    act.wait_ge(pe_done.sem, pe_done.after("modk", l, r, k))
                    act.dma_start(modraw[:], io["w_mod"][nl, nk, :, nr * MOD_COLS:(nr + 1) * MOD_COLS])\
                       .then_inc(mod_loaded, 16)

            def modrow(l, r):
                act.wait_ge(pe_done.sem, pe_done.after("modk", l, r, KD - 1))
                before = rounds[rounds.index((l, r)) - 1]
                act.wait_ge(pe_done.sem, pe_done.after("modT", *before))
                if l:
                    act.wait_ge(dve_done.sem, dve_done.after("mixt", l - 1, KD - 1))
                finish(act.activation(mrow[:], oo[:], ACT.Copy), ("mrow", l, r))

            def modend0(l, h):
                act.wait_ge(pe_done.sem, pe_done.after("modk0", l, h, KD - 1))
                if h:
                    act.wait_ge(pe_done.sem, pe_done.after("modT0", l, 0))
                finish(act.activation(mrow[:], half_bank[h], ACT.Copy), ("mrow0", l, h),
                       *([("mrow", l, 0)] if h else []))

            def start():
                finish(act.activation(cs[:, :, 0:2], cT[:], ACT.Silu), ("silu_c",))
                lam = vec[:, :, V_LAM:V_LAM + 8]
                finish(act.activation(small[:, 0], lam, ACT.Abs))
                own()
                finish(act.activation(small[:, 1], small[:, 0], ACT.Exp, scale=-1.0), ("exp_lam",))
                act.wait_ge(dve_done.sem, dve_done.after("dots",))
                finish(act.activation(small[:, 2, :, 2:4], small[:, 2, :, 0:2], ACT.Exp), ("exp_dots",))

            def square(l, which, k):
                cols = slice(0 if which == 0 else c0(l), T)
                if which in (1, 3):
                    return
                if k >= SQ:
                    act.wait_ge(pe_done.sem, pe_done.after("squared", l, which, k - SQ))
                if which == 0 and l == 0:
                    act.wait_ge(x_loaded[k // 2], 16)
                else:
                    wait_x(act, l if which else l - 1, 1 if which else 3, k)
                finish(act.activation(sq[:, k % SQ, cols], xT[:, k, cols], ACT.Square), ("square", l, which, k))

            def product_out(l, which, key, m):
                cols = slice(c0(l), T)
                act.wait_ge(pe_done.sem, pe_done.after(*key))
                if m >= SQ:
                    act.wait_ge(pe_done.sem, pe_done.after("squared", l, which, m - SQ))
                finish(act.activation(sq[:, m % SQ, cols], bank(key)[:, cols], ACT.Square), ("square", l, which, m))
                act.wait_ge(dve_done.sem, dve_done.after("gain", l, which))
                for s, a in streams(l):
                    finish(act.activation(fout[:, m, a:a + CTX], bank(key)[:, a:a + CTX], ACT.Copy,
                                          scale=gain[:, l, which, m, s:s + 1]), ("read", key))

            def norm(l, which):
                tiles = slice(0, 4) if which == 0 or l == 0 else slice(2, 4)
                cols = slice(0 if which == 0 else c0(l), T)
                act.wait_ge(pe_done.sem, pe_done.after("squared", l, which, KD - 1))
                finish(act.activation(rows[:, cols], stat[:, cols], ACT.Copy), ("rows", l, which))
                finish(act.activation(small[:, 7, 0, 0:1], ones[:, 0:1], ACT.Sqrt))
                act.wait_ge(pe_done.sem, pe_done.after("total", l, which))
                finish(act.activation(rt[:, 0, tiles], sums[:, tiles], ACT.Sqrt, bias=EPS,
                                      scale=1.0 / (32 * D)), ("read", ("stat", l, which)))
                if (l, which) == (0, 0):
                    act.wait_ge(pe_done.sem, pe_done.after("spread", l, which))
                    finish(act.activation(rstd[:, cols], bank(("spread", l, which))[:, cols], ACT.Copy),
                           ("read", ("spread", l, which)))

            def modulate(l, which, first, end):
                for k in range(first, end):
                    for s, a in ([(0, 0), (1, CTX)] if which == 0 else streams(l)):
                        act.wait_ge(dve_done.sem, dve_done.after("ht", l, which, k, s))
                        finish(act.activation(h_hi[:, k, a:a + CTX], ht[:, k, a:a + CTX], ACT.Identity,
                                              bias=modv[:, l, (0 if which == 0 else 3 * KD) + k, s:s + 1]),
                               ("h_hi", l, which, k, s))

            def proj(l, kind, t):
                key = ("proj", l, kind, t)
                b = bank(key)
                act.wait_ge(pe_done.sem, pe_done.after(*key))
                if kind == "cu":
                    act.wait_ge(dve_done.sem, dve_done.after("pad", l))
                    finish(act.activation(cu[:, t, :, 2:2 + CTX], b.rearrange("p (s n) -> p s n", s=2), ACT.Copy),
                           ("read", key))
                elif kind in ("av", "bv"):
                    if (kind, t) == ("bv", 0):
                        act.wait_ge(dve_done.sem, dve_done.after("y_c", l, KC - 1))
                    own()
                    finish(act.activation(vt[:, t % 2, :], b, ACT.Copy), ("read", key))
                elif kind == "cg":
                    finish(act.activation(y_c[:, t, c0(l):T], b[:, c0(l):T], ACT.Gelu_apprx_tanh), ("read", key))
                else:
                    dst = {"aq": q_a, "ak": k_a, "bq": q_b, "bk": k_b}[kind]
                    cols = slice(0 if kind in ("ak", "bk") else c0(l), T)
                    finish(act.activation(dst[:, t, cols], b[:, cols], ACT.Copy), ("read", key))

            def rotate(l, kind, t):
                if kind == "ak":
                    act.wait_ge(dve_done.sem, dve_done.after("qk", l, kind, t))
                    own()
                    finish(act.activation(k_sw[0:HEAD, 0, :], k_a[HEAD:P, 0, :], ACT.Copy))
                    finish(act.activation(k_sw[HEAD:P, 0, :], k_a[0:HEAD, 0, :], ACT.Copy), ("k_sw", l))

            def group(l, first, end, *what):
                if end == KD:
                    for w in what:
                        proj(l, *w)

            def turn_v(l, kind, t):
                key = ("vT", l, kind, t)
                col = 0 if kind == "av" else P * (t + 1)
                act.wait_ge(pe_done.sem, pe_done.after(*key))
                finish(act.activation(vv[:, :, col:col + P], bank(key).rearrange("p (t n) -> p t n", n=P), ACT.Copy),
                       ("read", key), ("v", l, kind, t))

            def lru_a(l, t):
                r, i, a, q = l_r[t % 2], l_i[t % 2], l_a[t % 2], l_q[t % 2]
                act.wait_ge(dve_done.sem, dve_done.after("kdec",))
                if t >= 2:
                    act.wait_ge(dve_done.sem, dve_done.after("hsum", l, t - 2))
                for d in range(2):
                    for g, dst in ((0, r), (1, i)):
                        key = ("gate", l, t, d, g)
                        act.wait_ge(pe_done.sem, pe_done.after(*key))
                        j = (d * 2 + g) * KC + t
                        finish(act.activation(dst[:, d], bank(key), ACT.Tanh, bias=hb[:, l, j:j + 1], scale=0.5),
                               ("read", key), ("l_gate", l, t, d, g))
                for d in range(2):
                    kd = kdec[:, 0, l, d * 4 + t:d * 4 + t + 1]
                    act.wait_ge(act_done.sem, act_done.after("l_gate", l, t, d, 0))
                    finish(act.activation(a[:, d], r[:, d], ACT.Exp, bias=kd, scale=kd), ("l_a", l, t, d))
                for d in range(2):
                    kn = kdec[:, 1, l, d * 4 + t:d * 4 + t + 1]
                    act.wait_ge(act_done.sem, act_done.after("l_a", l, t, d))
                    finish(act.activation(r[:, d], r[:, d], ACT.Tanh, bias=kn, scale=kn))
                finish(act.activation(q[:], a[:], ACT.Square), ("l_sq", l, t))

            def lru_b(l, t):
                act.wait_ge(dve_done.sem, dve_done.after("l_q", l, t))
                finish(act.activation(l_q[t % 2][:], l_q[t % 2][:], ACT.Sqrt, scale=0.25), ("l_sqrt", l, t))

            def nk(t):
                return T if t >= 2 else CTX

            def exp(l, n, ring, t, key):
                act.wait_ge(pe_done.sem, pe_done.after(*key))
                act.wait_ge(dve_done.sem, dve_done.after("nmax", l, n))
                finish(act.activation(pp[:, ring, 0:nk(t)], sc[:, n % 3, 0:nk(t)], ACT.Exp, bias=sm[:, n % 8, 1:2],
                                      scale=SCALE, accum_out=sm[:, n % 8, 2:3]), ("exp", l, n))

            def copy_pt(key, slot, t):
                act.wait_ge(pe_done.sem, pe_done.after(*key))
                finish(act.activation(pt[:, slot, 0:nk(t) // P, :].rearrange("p j n -> p (j n)"), bank(key)[:, 0:nk(t)], ACT.Copy),
                       ("read", key))

            def score_b(l, i):
                t = unit_b(l, i)[0]
                for m in range(2):
                    n = 2 * i + m
                    if i >= 2:
                        act.wait_ge(dve_done.sem, dve_done.after("w_b", l, i - 2))
                    exp(l, n, n % 4, t, ("s_b", l, n))

            def value_b(l, i):
                t, h = unit_b(l, i)
                j = qtiles(l).index(t)
                act.wait_ge(pe_done.sem, pe_done.after("pv_b", l, i))
                o = bank(("pv_b", l, i))[:, 0:P]
                finish(act.activation(yrow[:, j, h * P:(h + 1) * P], o, ACT.Copy))
                own()
                finish(act.activation(osq[:], o, ACT.Square, accum_out=bss[:, j, h:h + 1]), ("read", ("pv_b", l, i)))

            def turn_b(l, i):
                if i >= 2:
                    act.wait_ge(pe_done.sem, pe_done.after("pv_b", l, i - 2))
                copy_pt(("pt_b", l, i), i % 2, unit_b(l, i)[0])

            def b_start(l):
                score_b(l, 0)

            def b(l, i):
                if i:
                    value_b(l, i - 1)
                turn_b(l, i)
                if i + 1 < n_b(l):
                    score_b(l, i + 1)

            def b_end(l):
                value_b(l, n_b(l) - 1)
                own()
                n = len(qtiles(l)) * B_HEADS
                finish(act.activation(bst[:, 0, 0:n], bss[:].rearrange("p a b -> p (a b)")[:, 0:n], ACT.Sqrt, bias=EPS,
                                      scale=1.0 / B_VDIM), ("bst", l))

            def rows_out(name, dst, l, t, scale):
                key = (name, l, t)
                act.wait_ge(pe_done.sem, pe_done.after(*key))
                finish(act.activation(dst[:, :, t * P:(t + 1) * P], bank(key).rearrange("p (j n) -> p j n", n=P),
                                      ACT.Copy, scale=scale), ("read", key))

            def b_rows(l):
                for t in qtiles(l):
                    rows_out("yt_b", q_b, l, t, gsub[:, l:l + 1])

            def score_a(l, i):
                t, h = unit_a(l, i)
                n = 2 * n_b(l) + i
                if i >= 4:
                    act.wait_ge(pe_done.sem, pe_done.after("pt_a", l, i - 4))
                else:
                    act.wait_ge(dve_done.sem, dve_done.after("w_b", l, n_b(l) - 1))
                exp(l, n, i % 4, t, ("s_a", l, i))
                finish(act.activation(sm[:, n % 8, 3:4], vec[:, l, V_SINK + h:V_SINK + h + 1], ACT.Exp,
                                      bias=sm[:, n % 8, 1:2]), ("exp_sink", l, n))

            def turn_a(l, i):
                if i >= 2:
                    act.wait_ge(pe_done.sem, pe_done.after("pv_a", l, i - 2))
                else:
                    act.wait_ge(pe_done.sem, pe_done.after("pv_b", l, n_b(l) - 1))
                copy_pt(("pt_a", l, i), i % 2, unit_a(l, i)[0])

            def a_start(l):
                score_a(l, 0)
                score_a(l, 1)

            def a(l, i):
                turn_a(l, i)
                if i + 2 < n_a(l):
                    score_a(l, i + 2)

            def a_rows(l, t):
                rows_out("yt_a", q_a, l, t, 1.0)

            def gate_store(l, m, n):
                key = ("mgate", l, m, n)
                u, per = m * N_BRANCH + n, (T - c0(l)) // CTX
                act.wait_ge(pe_done.sem, pe_done.after(*key))
                if (m, n) == (0, 0):
                    act.wait_ge(dve_done.sem, dve_done.after("y_c", l, KC - 1))
                finish(act.activation(gst[:, u * per:(u + 1) * per].rearrange("p a n -> p (a n)"), bank(key)[:, c0(l):T],
                                      ACT.Tanh, scale=0.5), ("read", key), ("tg", l, m, n))

            def ysplit(l, n):
                cols = slice(c0(l), T)
                if n == 0:
                    act.wait_ge(pe_done.sem, pe_done.after("pt_a", l, n_a(l) - 1))
                if n == 2:
                    act.wait_ge(pe_done.sem, pe_done.after("yt_a", l, qtiles(l)[-1]))
                own()
                for k in range(KC):
                    if n == 0:
                        act.wait_ge(dve_done.sem, dve_done.after("y_c", l, k))
                    finish(act.activation(yh[n][:, k, cols], (y_c, q_b, q_a)[n][:, k, cols], ACT.Copy), ("y_hi", l, n, k))

            def merge(l, m):
                cols = slice(c0(l), T)
                for n in range(N_BRANCH):
                    u = m * N_BRANCH + n
                    if u < N_STORED[l]:
                        continue
                    key = ("mgate", l, m, n)
                    act.wait_ge(pe_done.sem, pe_done.after(*key))
                    act.wait_ge(dve_done.sem, dve_done.after("read", ("mbranch", l, *divmod(u - 2, N_BRANCH))))
                    finish(act.activation(tg[:, u % 2, cols], bank(key)[:, cols], ACT.Tanh, scale=0.5),
                           ("read", key), ("tg", l, m, n))
                act.wait_ge(dve_done.sem, dve_done.after("mixt", l, m))
                finish(act.activation(mx_hi[m][:, cols], mix(mixt, l, m), ACT.Copy, scale=0.5), ("mx_hi", l, m))

            def wout(l, m):
                product_out(l, 1, ("wout", l, m), m)

            def ffn_in(l, j):
                key, cols = ("fgate", l, j), slice(c0(l), T)
                act.wait_ge(pe_done.sem, pe_done.after(*key))
                if j >= 2:
                    act.wait_ge(dve_done.sem, dve_done.after("read", ("fup", l, j - 2)))
                finish(act.activation(sg[:, j % 2, cols], bank(key)[:, cols], ACT.Silu), ("read", key))
                act.wait_ge(dve_done.sem, dve_done.after("read", ("fup", l, j)))
                finish(act.activation(f_hi[j][:, cols], hid[:, cols], ACT.Copy), ("f_hi", l, j))

            def ffn_out(l, m):
                product_out(l, 3, ("ffn_out", l, m), m)

            def none(*args):
                pass

            act.wait_ge(consts_loaded, 16 * len(consts))
            act.wait_ge(dve_done.sem, dve_done.after("cs_zero",))
            start()
            steps = dict(square=square, norm=norm, modk=modk, modk0=none, modrow=modrow, modend=none, modend0=modend0,
                         modulate=modulate, proj=proj, group=group, rotate=rotate,
                         turn_v=turn_v, ffn_group=none, lru_a=lru_a, lru_b=lru_b,
                         b_start=b_start, b=b, b_end=b_end, b_rows=b_rows, a_start=a_start, a=a, a_end=none,
                         a_rows=a_rows, gate_store=gate_store, ysplit=ysplit, merge=merge, wout=wout, ffn_in=ffn_in,
                         ffn_out=ffn_out, residual=none)
            for step, *args in plan:
                steps[step](*args)

        @block.vector
        def _(dve):
            split = [0]

            def finish(ins, *names):
                ins.then_inc(dve_done.sem, dve_done.mark(*names))

            def own():
                dve.wait_ge(dve_done.sem, dve_done.count)

            def splits(key):
                split_to(granules_at(key))

            def split_to(limit):
                while split[0] < limit:
                    q = split[0]
                    dve.wait_ge(pool_done.sem, pool_done.after("w_hi", q))
                    finish(dve.tensor_tensor(w_lo[:, q % SPLIT].rearrange("p k n -> p (k n)"), raw[:, q % RAW, :],
                                             w_hi[:, q % SPLIT].bitcast(F32).rearrange("p k n -> p (k n)"),
                                             ALU.subtract), ("w_lo", q))
                    split[0] += 1

            def start():
                pairs = dl[:].rearrange("p l (a b) n -> p l a b n", b=2)
                finish(dve.tensor_tensor(dots[:], pairs[:, :, :, 0, :], pairs[:, :, :, 1, :], ALU.mult))
                own()
                finish(dve.tensor_reduce(small[:, 2, :, 0:2], dots[:], AX, ALU.add), ("dots",))
                finish(dve.tensor_scalar(nsink[:], vec[:, :, V_SINK:V_SINK + 8], -1.0, None, ALU.mult))
                finish(dve.tensor_scalar(hb[:], vec[:, :, V_LB:V_LB + 16], 0.5, None, ALU.mult))
                for l in range(DEPTH):
                    finish(dve.tensor_scalar(gsub[:, l:l + 1], vec[:, l, V_SUB:V_SUB + 1], 1.0 - lam_init(l), None, ALU.mult),
                           ("gsub", l))
                dve.wait_ge(act_done.sem, act_done.after("exp_lam",))
                y, z, z2, p, w = (small[:, i] for i in (1, 3, 4, 5, 6))
                finish(dve.tensor_scalar(w, y, 2.0, None, ALU.add))
                own()
                finish(dve.reciprocal(p, w))
                own()
                finish(dve.tensor_tensor(z, y, p, ALU.mult))
                own()
                finish(dve.tensor_tensor(z2, z, z, ALU.mult))
                own()
                finish(dve.tensor_scalar(p, z2, 1.0 / 17, None, ALU.mult))
                for c in (15, 13, 11, 9, 7, 5, 3):
                    own()
                    finish(dve.scalar_tensor_tensor(p, p, 1.0 / c, z2, ALU.add, ALU.mult))
                own()
                finish(dve.scalar_tensor_tensor(p, p, 1.0, z, ALU.add, ALU.mult))
                finish(dve.tensor_scalar(w, vec[:, :, V_LAM:V_LAM + 8], -1.0, 0.0, ALU.mult, ALU.max))
                own()
                finish(dve.scalar_tensor_tensor(z, p, 2.0, w, ALU.mult, ALU.add))
                own()
                finish(dve.tensor_scalar(kdec[:, 0], z, -4.0, None, ALU.mult))
                finish(dve.tensor_scalar(kdec[:, 1], z, 4.0, None, ALU.mult), ("kdec",))
                dve.wait_ge(act_done.sem, act_done.after("exp_dots",))
                finish(dve.tensor_tensor(nlam[:, :, 0:1], small[:, 2, :, 3:4], small[:, 2, :, 2:3], ALU.subtract))
                own()
                for l in range(DEPTH):
                    finish(dve.tensor_scalar(nlam[:, l, 1:2], nlam[:, l, 0:1], -lam_init(l), None, ALU.add), ("nlam", l))

            def modend0(l, h):
                v, key, tiles = vec[:, l], ("modT0", l, h), slice(4 * h, 4 * (h + 1))
                if h == 0:
                    split_to(1)
                dve.wait_ge(pe_done.sem, pe_done.after(*key))
                turned = bank(key).rearrange("p (c r j s) -> p r j c s", c=4, r=2, j=2)[:, :, :, :, 0:2]
                dst = modv[:, l, 0:16, :].rearrange("p (j c) s -> p j c s", j=2)[:, :, tiles]
                bias = v[:, V_BMOD:V_BMOD + 32].rearrange("p (j c s) -> p j c s", j=2, s=2)[:, :, tiles]
                finish(dve.tensor_tensor(dst, turned[:, 0], bias, ALU.add))
                own()
                finish(dve.tensor_tensor(dst, turned[:, 1], dst, ALU.add), ("read", key))
                own()
                finish(dve.scalar_tensor_tensor(gain[:, l, 0, tiles], modv[:, l, 8 + 4 * h:12 + 4 * h, :], 1.0,
                                                v[:, V_G + 8 * h:V_G + 8 * (h + 1)].rearrange("p (c s) -> p c s", s=2),
                                                ALU.add, ALU.mult))
                own()

            def modend(l, r):
                v, key = vec[:, l], ("modT", l, r)
                dve.wait_ge(pe_done.sem, pe_done.after(*key))
                turned = bank(key).rearrange("p (c j s) -> p j c s", c=4, j=4)[:, :, :, 0:2]
                finish(dve.tensor_tensor(modv[:, l, 16 * r:16 * (r + 1), :].rearrange("p (j c) s -> p j c s", j=4), turned,
                                         v[:, V_BMOD + 32 * r:V_BMOD + 32 * (r + 1)].rearrange(
                                             "p (j c s) -> p j c s", j=4, c=4), ALU.add), ("read", key))
                own()
                for i, (chunk, add) in enumerate(((1, 1.0), (2, 0.0), (4, 1.0), (5, 0.0))):
                    if chunk // 2 == r:
                        finish(dve.scalar_tensor_tensor(gain[:, l, i].rearrange("p k s -> p (k s)"),
                                                        modv[:, l, chunk * KD:(chunk + 1) * KD, :].rearrange("p k s -> p (k s)"),
                                                        add, v[:, V_G + 16 * i:V_G + 16 * (i + 1)], ALU.add, ALU.mult),
                               ("gain", l, i))
                own()

            def norm(l, which):
                tiles = range(4) if which == 0 else qtiles(l)
                if after_norm(l, which):
                    splits(after_norm(l, which))
                dve.wait_ge(act_done.sem, act_done.after("read", ("stat", l, which)))
                finish(dve.reciprocal(rt[:, 1, tiles[0]:4], rt[:, 0, tiles[0]:4]))
                own()
                for t in tiles:
                    finish(dve.tensor_scalar(diag[:, t, :], ident[:], rt[:, 1, t:t + 1], None, ALU.mult),
                           ("diag", l, which, t))

            def spread(l, which):
                if (l, which) == (0, 0):
                    dve.wait_ge(act_done.sem, act_done.after("read", ("spread", l, which)))
                    return rstd
                dve.wait_ge(pe_done.sem, pe_done.after("spread", l, which))
                return bank(("spread", l, which))

            def modulate(l, which, first, end):
                def low(k):
                    for s, a in sts:
                        dve.wait_ge(act_done.sem, act_done.after("h_hi", l, which, k, s))
                        finish(dve.scalar_tensor_tensor(h_lo[:, k, a:a + CTX], ht[:, k, a:a + CTX],
                                                        modv[:, l, (0 if which == 0 else 3 * KD) + k, s:s + 1],
                                                        h_hi[:, k, a:a + CTX].bitcast(F32), ALU.add, ALU.subtract),
                               ("h_lo", l, which, k))

                sts = [(0, 0), (1, CTX)] if which == 0 else streams(l)
                r = spread(l, which)
                for k in range(first, end):
                    if k in POOL_TILES and (l or which):
                        wait_x(dve, l if which else l - 1, 1 if which else 3, k)
                    for s, a in sts:
                        finish(dve.scalar_tensor_tensor(ht[:, k, a:a + CTX], xT[:, k, a:a + CTX],
                                                        gain[:, l, which, k, s:s + 1], r[:, a:a + CTX], ALU.mult, ALU.mult),
                               ("ht", l, which, k, s), ("read", ("spread", l, which)))
                    if k > first:
                        low(k - 1)
                    if (l, which) == (0, 0) and k in (2, 5):
                        split_to(2 if k == 2 else 3)
                low(end - 1)

            def proj(l, kind, t):
                key = ("proj", l, kind, t)
                if (kind, t) == ("cu", 0):
                    finish(dve.memset(cu[:, :, :, 0:2], 0.0))
                    finish(dve.memset(cu[:, :, :, 2 + CTX:4 + CTX], 0.0), ("pad", l))
                splits(key)
                b = bank(key)
                if kind == "cu":
                    dve.wait_ge(act_done.sem, act_done.after("read", key))
                    u = uu[:, t].rearrange("p (s n) -> p s n", s=2)
                    tap = [vec[:, l, V_CW + i * KC + t:V_CW + i * KC + t + 1] for i in range(CONV_W)]
                    own()
                    finish(dve.tensor_scalar(u, cu[:, t, :, 0:CTX], tap[0], vec[:, l, V_CB + t:V_CB + t + 1], ALU.mult, ALU.add))
                    for i in range(1, CONV_W):
                        own()
                        finish(dve.scalar_tensor_tensor(u, cu[:, t, :, i:i + CTX], tap[i], u, ALU.mult, ALU.add),
                               ("conv", l, t))

            def rotate(l, kind, t):
                dst = {"aq": q_a, "ak": k_a, "bq": q_b, "bk": k_b}[kind][:, t, CTX:T]
                dve.wait_ge(act_done.sem, act_done.after("read", ("proj", l, kind, t)))
                own()
                finish(dve.stream_shuffle(rope[:, 0, :], dst, [i ^ 16 for i in range(32)]))
                own()
                finish(dve.tensor_tensor(dst, dst, cos[:], ALU.mult))
                finish(dve.tensor_tensor(rope[:, 1, :], rope[:, 0, :], sin[:], ALU.mult))
                own()
                finish(dve.tensor_tensor(dst, dst, rope[:, 1, :], ALU.add), ("qk", l, kind, t))

            def group(l, first, end, *what):
                if end < KD:
                    return
                if l == 0:
                    dve.wait_ge(tables_loaded, 16 * len(tables))
                    finish(dve.tensor_copy(mask[:], maskf[:]), ("mask",))
                for w in what:
                    splits(("proj", l) + w)
                for w in what:
                    proj(l, *w)

            def lru_a(l, t):
                r, i, q = l_r[t % 2], l_i[t % 2], l_q[t % 2]
                for d in range(2):
                    dve.wait_ge(act_done.sem, act_done.after("l_gate", l, t, d, 1))
                    finish(dve.scalar_tensor_tensor(i[:, d], i[:, d], 1.0, uu[:, t], ALU.add, ALU.mult))
                dve.wait_ge(act_done.sem, act_done.after("l_sq", l, t))
                finish(dve.scalar_tensor_tensor(q[:], q[:], 1.0, r[:], ALU.add, ALU.mult), ("l_q", l, t))

            def lru_b(l, t):
                h, i, a, q = l_r[t % 2], l_i[t % 2], l_a[t % 2], l_q[t % 2]
                dve.wait_ge(act_done.sem, act_done.after("l_sqrt", l, t))
                own()
                finish(dve.tensor_tensor(i[:], i[:], q[:], ALU.mult))
                own()
                finish(dve.tensor_tensor_scan(h[:, 1, CTX - 1::-1], a[:, 1, CTX - 1::-1], i[:, 1, CTX - 1::-1], 0.0,
                                              ALU.mult, ALU.add))
                finish(dve.tensor_tensor_scan(h[:, 0], a[:, 0], i[:, 0], 0.0, ALU.mult, ALU.add))
                dve.wait_ge(dve_done.sem, dve_done.count - 1)
                finish(dve.tensor_tensor_scan(h[:, 1, T - 1:CTX - 1:-1], a[:, 1, T - 1:CTX - 1:-1],
                                              i[:, 1, T - 1:CTX - 1:-1], h[:, 1, 0:1], ALU.mult, ALU.add))
                own()
                cols = slice(c0(l), T)
                finish(dve.tensor_tensor(uu[:, t, cols], h[:, 0, cols], h[:, 1, cols], ALU.add), ("hsum", l, t))
                own()
                dve.wait_ge(act_done.sem, act_done.after("read", ("proj", l, "cg", t)))
                finish(dve.tensor_tensor(y_c[:, t, cols], y_c[:, t, cols], uu[:, t, cols], ALU.mult), ("y_c", l, t))

            def nk(t):
                return T if t >= 2 else CTX

            def row_max(l, n, key, t, sink):
                dve.wait_ge(pe_done.sem, pe_done.after(*key))
                finish(dve.tensor_reduce(sm[:, n % 8, 0:1], sc[:, n % 3, 0:nk(t)], AX, ALU.max, negate=True))
                own()
                if sink is None:
                    ins = dve.tensor_scalar(sm[:, n % 8, 1:2], sm[:, n % 8, 0:1], SCALE, None, ALU.mult)
                else:
                    ins = dve.tensor_scalar(sm[:, n % 8, 1:2], sm[:, n % 8, 0:1], SCALE, sink, ALU.mult, ALU.min)
                finish(ins, ("nmax", l, n))

            def max_b(l, i):
                for m in range(2):
                    n = 2 * i + m
                    row_max(l, n, ("s_b", l, n), unit_b(l, i)[0], None)

            def combine(l, i):
                a, b = 2 * i, 2 * i + 1
                cols = slice(0, nk(unit_b(l, i)[0]))
                dve.wait_ge(act_done.sem, act_done.after("exp", l, b))
                finish(dve.reciprocal(sm[:, a % 8:a % 8 + 2, 4:5], sm[:, a % 8:a % 8 + 2, 2:3]))
                own()
                finish(dve.tensor_scalar(sm[:, b % 8, 5:6], sm[:, b % 8, 4:5], nlam[:, l, 1:2], None, ALU.mult))
                if i >= 2:
                    dve.wait_ge(pe_done.sem, pe_done.after("pt_b", l, i - 2))
                finish(dve.tensor_scalar(ww[:, i % 2, cols], pp[:, a % 4, cols], sm[:, a % 8, 4:5], None, ALU.mult))
                own()
                finish(dve.scalar_tensor_tensor(ww[:, i % 2, cols], pp[:, b % 4, cols], sm[:, b % 8, 5:6],
                                                ww[:, i % 2, cols], ALU.mult, ALU.add), ("w_b", l, i))

            def b_start(l):
                max_b(l, 0)

            def b(l, i):
                combine(l, i)
                if i + 1 < n_b(l):
                    max_b(l, i + 1)

            def max_a(l, i):
                t, h = unit_a(l, i)
                row_max(l, 2 * n_b(l) + i, ("s_a", l, i), t, nsink[:, l, h:h + 1])

            def out_a(l, i):
                r = (2 * n_b(l) + i) % 8
                rows = slice(r, r + 2)
                dve.wait_ge(act_done.sem, act_done.after("exp_sink", l, 2 * n_b(l) + i + 1))
                finish(dve.tensor_tensor(sm[:, rows, 4:5], sm[:, rows, 2:3], sm[:, rows, 3:4], ALU.add))
                own()
                finish(dve.reciprocal(sm[:, rows, 5:6], sm[:, rows, 4:5]))
                own()
                for j in (i, i + 1):
                    t, h = unit_a(l, j)
                    dve.wait_ge(pe_done.sem, pe_done.after("pv_a", l, j))
                    if j >= 2 * A_HEADS:
                        dve.wait_ge(pe_done.sem, pe_done.after("yt_a", l, t - 2))
                    finish(dve.tensor_scalar(yrow_a[:, t % 2, h * HEAD:(h + 1) * HEAD], bank(("pv_a", l, j))[:, 0:HEAD],
                                             sm[:, r + j - i, 5:6], None, ALU.mult),
                           ("o_a", l, t, h), ("read", ("pv_a", l, j)))

            def b_rows(l):
                n = len(qtiles(l)) * B_HEADS
                dve.wait_ge(act_done.sem, act_done.after("bst", l))
                finish(dve.reciprocal(bst[:, 1, 0:n], bst[:, 0, 0:n]))
                own()
                for j, t in enumerate(qtiles(l)):
                    for h in range(B_HEADS):
                        c = slice(h * P, (h + 1) * P)
                        finish(dve.tensor_scalar(yrow[:, j, c], yrow[:, j, c], bst[:, 1, j * 4 + h:j * 4 + h + 1],
                                                 None, ALU.mult), ("yrow_b", l, t))

            def a_start(l):
                max_a(l, 0)
                max_a(l, 1)

            def a(l, i):
                if i + 2 < n_a(l):
                    max_a(l, i + 2)
                if i and i % 2 == 0:
                    out_a(l, i - 2)

            def a_end(l):
                out_a(l, n_a(l) - 2)

            def gate_store(l, m, n):
                splits(("mgate", l, m, n))

            def ysplit(l, n):
                cols = slice(c0(l), T)
                if n == 1:
                    dve.wait_ge(pe_done.sem, pe_done.after("yt_a", l, qtiles(l)[-1]))
                for k in range(KC):
                    dve.wait_ge(act_done.sem, act_done.after("y_hi", l, n, k))
                    finish(dve.tensor_tensor(yl[n][:, k, cols], (y_c, q_b, q_a)[n][:, k, cols],
                                             yh[n][:, k, cols].bitcast(F32), ALU.subtract), ("y_lo", l, n, k))

            def merge(l, m):
                cols = slice(c0(l), T)

                def low(m):
                    dve.wait_ge(act_done.sem, act_done.after("mx_hi", l, m))
                    finish(dve.scalar_tensor_tensor(mx_lo[m][:, cols], mix(mixt, l, m), 0.5, mx_hi[m][:, cols].bitcast(F32),
                                                    ALU.mult, ALU.subtract), ("mx_lo", l, m))

                for n in range(N_BRANCH):
                    key = ("mbranch", l, m, n)
                    u = m * N_BRANCH + n
                    if u < N_STORED[l]:
                        per = (T - c0(l)) // CTX
                        g = gst[:, u * per:(u + 1) * per].rearrange("p a n -> p (a n)")
                    else:
                        splits(("mgate", l, m, n))
                        g = tg[:, u % 2, cols]
                    splits(key)
                    dve.wait_ge(act_done.sem, act_done.after("tg", l, m, n))
                    dve.wait_ge(pe_done.sem, pe_done.after(*key))
                    if n == 0:
                        if m and l == 0:
                            low(m - 1)
                        if m >= 2 or (m and l == 0):
                            dve.wait_ge(dve_done.sem, dve_done.after("mx_lo", l, m - 1 if l == 0 else m - 2))
                        finish(dve.scalar_tensor_tensor(mix(mixt, l, m), g, 1.0, bank(key)[:, cols], ALU.add, ALU.mult),
                               ("read", key), ("added", l, m, n))
                        if m and l:
                            low(m - 1)
                        continue
                    if n == 2 or m:
                        dve.wait_ge(dve_done.sem, dve_done.after("added", l, m if n == 2 else m - 1, 1 if n == 2 else 2))
                    finish(dve.scalar_tensor_tensor(mix(mixu, l, n), g, 1.0, bank(key)[:, cols], ALU.add, ALU.mult),
                           ("read", key))
                    splits(("mbranch", l, m, n + 1) if n == 1 and m * N_BRANCH + 2 < N_STORED[l] else key)
                    own()
                    finish(dve.tensor_tensor(mix(mixt, l, m), mix(mixt, l, m), mix(mixu, l, n), ALU.add),
                           ("mixt", l, m), ("added", l, m, n))
                if m == KD - 1:
                    low(m)

            def wout(l, m):
                splits(("wout", l, m))

            def residual(l, which):
                cols = slice(c0(l), T)
                r = spread(l, which)
                for k in range(KD + 1):
                    if k < KD:
                        finish(dve.tensor_tensor(ht[:, k, cols], fout[:, k, cols], r[:, cols], ALU.mult),
                               ("scaled", l, which, k), ("read", ("spread", l, which)))
                    if k and k - 1 not in POOL_TILES:
                        dve.wait_ge(dve_done.sem, dve_done.after("scaled", l, which, k - 1))
                        finish(dve.tensor_tensor(xT[:, k - 1, cols], xT[:, k - 1, cols], ht[:, k - 1, cols], ALU.add),
                               ("x", l, which, k - 1))

            def ffn_in(l, j):
                cols = slice(c0(l), T)
                splits(("fgate", l, j))
                key = ("fup", l, j)
                splits(key)
                dve.wait_ge(act_done.sem, act_done.after("read", ("fgate", l, j)))
                dve.wait_ge(pe_done.sem, pe_done.after(*key))
                if j:
                    own()
                finish(dve.tensor_tensor(hid[:, cols], sg[:, j % 2, cols], bank(key)[:, cols], ALU.mult), ("read", key))
                dve.wait_ge(act_done.sem, act_done.after("f_hi", l, j))
                own()
                finish(dve.tensor_tensor(f_lo[j][:, cols], hid[:, cols], f_hi[j][:, cols].bitcast(F32), ALU.subtract),
                       ("f_lo", l, j))

            def ffn_out(l, m):
                splits(("ffn_out", l, m))

            def none(*args):
                pass

            finish(dve.memset(cs[:], 0.0), ("cs_zero",))
            dve.wait_ge(consts_loaded, 16 * len(consts))
            finish(dve.tensor_copy(identb[:], ident[:]))
            start()
            steps = dict(square=none, norm=norm, modk=none, modk0=none, modrow=none, modend=modend, modend0=modend0,
                         modulate=modulate, proj=proj, group=group, rotate=rotate,
                         turn_v=none, ffn_group=none, lru_a=lru_a, lru_b=lru_b,
                         b_start=b_start, b=b, b_end=none, b_rows=b_rows, a_start=a_start, a=a, a_end=a_end,
                         a_rows=none, gate_store=gate_store, ysplit=ysplit, merge=merge, wout=wout, ffn_in=ffn_in,
                         ffn_out=ffn_out, residual=residual)
            for step, *args in plan:
                steps[step](*args)

    return {"pe_done": pe_done.marks, "act_done": act_done.marks, "dve_done": dve_done.marks, "pool_done": pool_done.marks}


def build(make, shapes):
    known = {n: {} for n in ("pe_done", "act_done", "dve_done", "pool_done")}
    for _ in range(2):
        nc = make()
        io = {n: nc.dram_tensor(f"{n}_dram", s, F32, kind=k).ap() for n, (s, k) in shapes.items()}
        known = program(nc, io, known)
    return nc


def rotary_tables():
    rd = HEAD // 4
    t = np.arange(SEQ)
    pos = np.stack([t // GRID_W, t % GRID_W]).astype(np.float32)
    inv = (1.0 / (10000.0 ** (np.arange(rd, dtype=np.float32) * 2.0 / (HEAD // 2)))).astype(np.float32)
    cos, sin = np.zeros((HEAD, SEQ), np.float32), np.zeros((HEAD, SEQ), np.float32)
    for axis in range(2):
        ang = (pos[axis][None, :] * inv[:, None]).astype(np.float32)
        for half in range(2):
            rows = slice((axis * 2 + half) * rd, (axis * 2 + half + 1) * rd)
            cos[rows] = np.cos(ang)
            sin[rows] = np.sin(ang) * (1 if half else -1)
    return np.tile(cos, (2, 1)), np.tile(sin, (2, 1))


def window_mask():
    q = np.arange(SEQ)[:, None]
    k = np.arange(SEQ)[None, :]
    m = np.where(np.abs(k - q) <= WINDOW, 0.0, MASKED).astype(np.float32)
    return np.ascontiguousarray(m.reshape(2, P, SEQ).transpose(1, 0, 2))


def columns(a):
    a = np.asarray(a)
    return a.reshape(-1, P).T


def kernel(x, c, ctx, c_ctx, w_mod, b_mod, norm_g, w_in, attn_sink, diff_lambda, diff_subln, conv_w, conv_b, lru_w,
           lru_b, lru_lambda, w_branch, w_out, w_ffn_in, w_ffn_out):
    import concourse.bacc as bacc
    from concourse.bass_utils import run_bass_kernel_spmd

    def blocks(w):
        w = np.asarray(w)
        k, n = w.shape
        return w.reshape(k // P, P, n // P, P).transpose(0, 2, 1, 3)

    stream = np.empty((DEPTH * N_GRAN, P, 8, P), np.float32)
    for l in range(DEPTH):
        cut = {"w_in": blocks(w_in[l]), "w_branch": blocks(np.asarray(w_branch[l]).reshape(N_BRANCH * C_W, D)),
               "w_out": blocks(w_out[l]), "w_ffn_in": blocks(w_ffn_in[l]), "w_ffn_out": blocks(w_ffn_out[l])}
        for i, (name, k, n) in enumerate(block_order(l)):
            stream[l * N_GRAN + i // 8, :, i % 8, :] = cut[name][k, n]

    vec = np.empty((P, DEPTH, V_N), np.float32)
    lruw = np.zeros((DEPTH, P, 16, P), np.float32)
    for l in range(DEPTH):
        v = vec[:, l]
        v[:, V_BMOD:V_BMOD + 96] = np.repeat(columns(b_mod[l]), 2, axis=1)
        v[:, V_G:V_G + 64] = np.repeat(columns(norm_g[l]), 2, axis=1)
        v[:, V_CW:V_CW + 16] = columns(conv_w[l])
        v[:, V_CB:V_CB + 4] = columns(conv_b[l])
        v[:, V_LB:V_LB + 16] = columns(lru_b[l])
        v[:, V_LAM:V_LAM + 8] = columns(lru_lambda[l])
        v[:, V_SINK:V_SINK + 8] = np.asarray(attn_sink[l])[None, :]
        v[:, V_SUB] = np.asarray(diff_subln[l])
        w = np.asarray(lru_w[l]).reshape(4, C_BLOCKS, HEAD, HEAD)
        for dg in range(4):
            for n in range(C_BLOCKS):
                half = slice(HEAD * (n % 2), HEAD * (n % 2 + 1))
                lruw[l, half, dg * KC + n // 2, half] = w[dg, n]

    cos, sin = rotary_tables()
    both = np.concatenate([np.asarray(ctx)[0], np.asarray(x)[0]], axis=0)
    arrays = {
        "xT": both.T.reshape(KD, P, T).transpose(1, 0, 2),
        "cT": np.stack([columns(c_ctx), columns(np.asarray(c)[0])], axis=2),
        "vec": vec, "lruw": lruw, "w_mod": np.asarray(w_mod).reshape(DEPTH, KD, P, 6 * D),
        "dl": np.broadcast_to(np.asarray(diff_lambda)[None], (P, DEPTH, 4, HEAD)), "stream": stream.reshape(-1, P, 8 * P),
        "ident": np.eye(P, dtype=np.float32), "cos": cos, "sin": sin, "maskf": window_mask(),
    }
    arrays = {n: np.ascontiguousarray(a) for n, a in arrays.items()}
    shapes = {n: (a.shape, "ExternalInput") for n, a in arrays.items()}
    shapes["out"] = ((P, KD, SEQ), "ExternalOutput")
    nc = build(lambda: bacc.Bacc("TRN2", target_bir_lowering=False, num_devices=1), shapes)
    result = run_bass_kernel_spmd(nc, [{f"{n}_dram": a for n, a in arrays.items()}], core_ids=[0])
    out = result.results[0]["out_dram"]
    return np.ascontiguousarray(out.transpose(1, 0, 2).reshape(D, SEQ).T)[None]
```
